# Optimizing a Trainium2 kernel written in Bass

```python
import math
import jax, jax.numpy as jnp
from jax import lax
import numpy as np
import jax
import jax.numpy as jnp

D_MODEL = 1024
BATCH = 1
SEQ = 256
DEPTH = 1

HEAD_DIM = 128
N_HEADS_MOBA = 8
N_HEADS_GDN = 8
MOBA_WIDTH = N_HEADS_MOBA * HEAD_DIM
GDN_WIDTH = N_HEADS_GDN * HEAD_DIM
MOBA_BLOCK = 256
MOBA_TOPK = 3
MOBA_Q_CHUNK = 32
GDN_CHUNK = 64
CONV_WIDTH = 4
ROPE_THETA = 10000.0
D_FF = -(-8 * D_MODEL // (3 * 256)) * 256
PLE_DIM = 256
EPS = 1e-6

IN_SIZES = (MOBA_WIDTH, MOBA_WIDTH, MOBA_WIDTH, 3 * GDN_WIDTH, GDN_WIDTH,
            N_HEADS_GDN, N_HEADS_GDN, D_MODEL, D_MODEL)
IN_SPLITS = tuple(int(s) for s in np.cumsum(IN_SIZES)[:-1])
IN_WIDTH = int(sum(IN_SIZES))


def rms_norm(x, w):
    xf = x.astype(jnp.float32)
    y = xf * lax.rsqrt(jnp.mean(xf * xf, axis=-1, keepdims=True) + EPS)
    return (y * w.astype(jnp.float32)).astype(x.dtype)

def l2_norm(x):
    xf = x.astype(jnp.float32)
    return xf * lax.rsqrt(jnp.sum(xf * xf, axis=-1, keepdims=True) + EPS)

def rope_tables(seq):
    inv = 1.0 / (ROPE_THETA ** (jnp.arange(0, HEAD_DIM, 2, dtype=jnp.float32) / HEAD_DIM))
    ang = jnp.arange(seq, dtype=jnp.float32)[:, None] * inv[None, :]
    return jnp.cos(ang), jnp.sin(ang)

def apply_rope(x, cos, sin):
    x1, x2 = jnp.split(x.astype(jnp.float32), 2, axis=-1)
    out = jnp.concatenate([x1 * cos - x2 * sin, x2 * cos + x1 * sin], axis=-1)
    return out.astype(x.dtype)

def causal_depthwise_conv(x, w):
    c = x.shape[-1]
    return lax.conv_general_dilated(
        x, w[:, None, :].astype(x.dtype), window_strides=(1,),
        padding=[(CONV_WIDTH - 1, 0)], dimension_numbers=("NWC", "WIO", "NWC"),
        feature_group_count=c)

def moba_attention(q, k, v):
    b, h, s, hd = q.shape
    nb = -(-s // MOBA_BLOCK)
    pad = nb * MOBA_BLOCK - s
    n_sel = min(MOBA_TOPK, nb)
    scale = hd ** -0.5
    k_blocks = jnp.pad(k, ((0, 0), (0, 0), (0, pad), (0, 0))).reshape(b, h, nb, MOBA_BLOCK, hd)
    v_blocks = jnp.pad(v, ((0, 0), (0, 0), (0, pad), (0, 0))).reshape(b, h, nb, MOBA_BLOCK, hd)
    k_mean = jnp.mean(k_blocks.astype(jnp.float32), axis=3)
    blk_ids = jnp.arange(nb)
    n_chunks = s // MOBA_Q_CHUNK

    def one_chunk(c):
        start = c * MOBA_Q_CHUNK
        q_c = lax.dynamic_slice_in_dim(q, start, MOBA_Q_CHUNK, axis=2)
        q_blk = start // MOBA_BLOCK
        gate = jnp.einsum("bhcd,bhnd->bhcn", q_c.astype(jnp.float32), k_mean)
        gate = jnp.where(blk_ids < q_blk, gate, -jnp.inf)
        _, sel = lax.top_k(gate, n_sel)
        sel_valid = sel < q_blk
        idx = sel.reshape(b, h, MOBA_Q_CHUNK * n_sel, 1, 1)
        k_sel = jnp.take_along_axis(k_blocks, idx, axis=2).reshape(
            b, h, MOBA_Q_CHUNK, n_sel, MOBA_BLOCK, hd)
        v_sel = jnp.take_along_axis(v_blocks, idx, axis=2).reshape(
            b, h, MOBA_Q_CHUNK, n_sel, MOBA_BLOCK, hd)
        s_past = jnp.einsum("bhcd,bhcknd->bhckn", q_c, k_sel).astype(jnp.float32) * scale
        s_past = jnp.where(sel_valid[..., None], s_past, -jnp.inf)
        s_past = s_past.reshape(b, h, MOBA_Q_CHUNK, n_sel * MOBA_BLOCK)
        k_own = lax.dynamic_index_in_dim(k_blocks, q_blk, axis=2, keepdims=False)
        v_own = lax.dynamic_index_in_dim(v_blocks, q_blk, axis=2, keepdims=False)
        s_own = jnp.einsum("bhcd,bhnd->bhcn", q_c, k_own).astype(jnp.float32) * scale
        q_pos = start + jnp.arange(MOBA_Q_CHUNK)
        k_pos = q_blk * MOBA_BLOCK + jnp.arange(MOBA_BLOCK)
        s_own = jnp.where(k_pos[None, :] <= q_pos[:, None], s_own, -jnp.inf)
        probs = jax.nn.softmax(jnp.concatenate([s_past, s_own], axis=-1), axis=-1)
        p_past = probs[..., : n_sel * MOBA_BLOCK].reshape(
            b, h, MOBA_Q_CHUNK, n_sel, MOBA_BLOCK).astype(v.dtype)
        p_own = probs[..., n_sel * MOBA_BLOCK:].astype(v.dtype)
        return (jnp.einsum("bhckn,bhcknd->bhcd", p_past, v_sel)
                + jnp.einsum("bhcn,bhnd->bhcd", p_own, v_own))

    out = lax.map(one_chunk, jnp.arange(n_chunks))
    return out.transpose(1, 2, 0, 3, 4).reshape(b, h, s, hd)

def gated_delta_rule(q, k, v, g, beta):
    b, h, s, dk = q.shape
    dv = v.shape[-1]
    L = GDN_CHUNK
    nc = s // L
    f32 = jnp.float32
    q = q.astype(f32) * (dk ** -0.5)
    k = k.astype(f32)
    v = v.astype(f32)
    q = q.reshape(b, h, nc, L, dk)
    k = k.reshape(b, h, nc, L, dk)
    v = v.reshape(b, h, nc, L, dv)
    g = g.astype(f32).reshape(b, h, nc, L)
    beta = beta.astype(f32).reshape(b, h, nc, L)
    gc = jnp.cumsum(g, axis=-1)
    causal = jnp.tril(jnp.ones((L, L), dtype=bool))
    strict = jnp.tril(jnp.ones((L, L), dtype=bool), k=-1)
    decay = jnp.exp(jnp.where(causal, gc[..., :, None] - gc[..., None, :], -jnp.inf))
    k_beta = k * beta[..., None]
    a_low = jnp.where(strict, jnp.einsum("bhnid,bhnjd->bhnij", k_beta, k) * decay, 0.0)
    t_mat = a_low + jnp.eye(L, dtype=f32)
    rhs = jnp.concatenate([v * beta[..., None], k_beta * jnp.exp(gc)[..., None]], axis=-1)
    sol = lax.linalg.triangular_solve(t_mat, rhs, left_side=True, lower=True, unit_diagonal=True)
    u = sol[..., :dv]
    w = sol[..., dv:]
    attn = jnp.where(causal, jnp.einsum("bhnid,bhnjd->bhnij", q, k) * decay, 0.0)

    def step(state, inp):
        q_i, k_i, u_i, w_i, g_i, a_i = inp
        v_new = u_i - jnp.einsum("bhld,bhde->bhle", w_i, state)
        o = (jnp.einsum("bhld,bhde->bhle", q_i * jnp.exp(g_i)[..., None], state)
             + jnp.einsum("bhlm,bhme->bhle", a_i, v_new))
        g_last = g_i[..., -1]
        state = (state * jnp.exp(g_last)[..., None, None]
                 + jnp.einsum("bhld,bhle->bhde", k_i * jnp.exp(g_last[..., None] - g_i)[..., None], v_new))
        return state, o

    xs = tuple(jnp.moveaxis(t, 2, 0) for t in (q, k, u, w, gc, attn))
    state0 = jnp.zeros((b, h, dk, dv), dtype=f32)
    _, o = lax.scan(step, state0, xs)
    return jnp.moveaxis(o, 0, 2).reshape(b, h, s, dv)

def first_inputs(seed: int = 0) -> dict:
    key = jax.random.key(seed)
    ks = jax.random.split(key, 24)
    f32 = jnp.float32

    def nrm(k, shape, scale):
        return jax.random.normal(k, shape, f32) * scale

    def gain(k, n):
        return 1.0 + 0.1 * jax.random.normal(k, (DEPTH, n), f32)

    dt = jnp.exp(jax.random.uniform(ks[7], (DEPTH, N_HEADS_GDN), f32,
                                    math.log(1e-3), math.log(1e-1)))
    return {
        "x": nrm(ks[0], (BATCH, SEQ, D_MODEL), 1.0),
        "p": nrm(ks[1], (DEPTH, BATCH, SEQ, PLE_DIM), 1.0),
        "ln_pre_mix": gain(ks[2], D_MODEL),
        "w_in": nrm(ks[3], (DEPTH, D_MODEL, IN_WIDTH), D_MODEL ** -0.5),
        "conv_w": nrm(ks[4], (DEPTH, CONV_WIDTH, 3 * GDN_WIDTH), CONV_WIDTH ** -0.5),
        "a_log": jnp.log(jax.random.uniform(ks[5], (DEPTH, N_HEADS_GDN), f32, 1.0, 16.0)),
        "dt_bias": jnp.log(jnp.expm1(dt)),
        "gdn_norm": gain(ks[6], HEAD_DIM),
        "w_proj_a": nrm(ks[8], (DEPTH, MOBA_WIDTH, D_MODEL), MOBA_WIDTH ** -0.5),
        "w_proj_b": nrm(ks[9], (DEPTH, GDN_WIDTH, D_MODEL), GDN_WIDTH ** -0.5),
        "w_out": nrm(ks[10], (DEPTH, D_MODEL, D_MODEL), D_MODEL ** -0.5),
        "ln_post_mix": gain(ks[11], D_MODEL),
        "ln_pre_ffn": gain(ks[12], D_MODEL),
        "w_ffn_gate": nrm(ks[13], (DEPTH, D_MODEL, D_FF), D_MODEL ** -0.5),
        "w_ffn_up": nrm(ks[14], (DEPTH, D_MODEL, D_FF), D_MODEL ** -0.5),
        "w_ffn_down": nrm(ks[15], (DEPTH, D_FF, D_MODEL), D_FF ** -0.5),
        "ln_post_ffn": gain(ks[16], D_MODEL),
        "w_ple": nrm(ks[17], (DEPTH, PLE_DIM, D_MODEL), PLE_DIM ** -0.5),
        "ln_ple": gain(ks[18], D_MODEL),
        "w_ple_gate": nrm(ks[19], (DEPTH, D_MODEL, D_MODEL), D_MODEL ** -0.5),
    }

def first_block(x, p, ln_pre_mix, w_in, conv_w, a_log, dt_bias, gdn_norm, w_proj_a, w_proj_b,
              w_out, ln_post_mix, ln_pre_ffn, w_ffn_gate, w_ffn_up, w_ffn_down, ln_post_ffn,
              w_ple, ln_ple, w_ple_gate):
    b, s, _ = x.shape
    cos, sin = rope_tables(s)

    def to_heads(t, n):
        return t.reshape(b, s, n, HEAD_DIM).transpose(0, 2, 1, 3)

    def from_heads(t):
        return t.transpose(0, 2, 1, 3).reshape(b, s, -1)

    h = x
    for i in range(DEPTH):
        u = rms_norm(h, ln_pre_mix[i])
        proj = u @ w_in[i]
        q_a, k_a, v_a, qkv_b, z_b, b_b, a_b, gate_a, gate_b = jnp.split(proj, IN_SPLITS, axis=-1)

        qa = apply_rope(to_heads(q_a, N_HEADS_MOBA), cos, sin)
        ka = apply_rope(to_heads(k_a, N_HEADS_MOBA), cos, sin)
        va = to_heads(v_a, N_HEADS_MOBA)
        y_a = from_heads(moba_attention(qa, ka, va))

        qkv_b = jax.nn.silu(causal_depthwise_conv(qkv_b, conv_w[i]))
        q_b, k_b, v_b = jnp.split(qkv_b, 3, axis=-1)
        qb = l2_norm(to_heads(q_b, N_HEADS_GDN))
        kb = l2_norm(to_heads(k_b, N_HEADS_GDN))
        vb = to_heads(v_b, N_HEADS_GDN)
        g_log = -jnp.exp(a_log[i].astype(jnp.float32)) * jax.nn.softplus(
            a_b.astype(jnp.float32) + dt_bias[i].astype(jnp.float32))
        beta = jax.nn.sigmoid(b_b.astype(jnp.float32))
        o_b = gated_delta_rule(qb, kb, vb, g_log.transpose(0, 2, 1), beta.transpose(0, 2, 1))
        o_b = o_b.transpose(0, 2, 1, 3).astype(h.dtype)
        z = z_b.reshape(b, s, N_HEADS_GDN, HEAD_DIM)
        y_b = (rms_norm(o_b, gdn_norm[i]) * jax.nn.silu(z)).reshape(b, s, GDN_WIDTH)

        merged = (jax.nn.sigmoid(gate_a) * (y_a @ w_proj_a[i])
                  + jax.nn.sigmoid(gate_b) * (y_b @ w_proj_b[i]))
        h = h + rms_norm(merged @ w_out[i], ln_post_mix[i])

        f = rms_norm(h, ln_pre_ffn[i])
        f = (jax.nn.silu(f @ w_ffn_gate[i]) * (f @ w_ffn_up[i])) @ w_ffn_down[i]
        h = h + rms_norm(f, ln_post_ffn[i])

        e = rms_norm(p[i].astype(h.dtype) @ w_ple[i], ln_ple[i])
        h = h + jax.nn.sigmoid(h @ w_ple_gate[i]) * e
    return h


DEPTH_2 = 2

GRID_W = 64
CTX_LEN = 256
N_MOD = 6

SSD_HEADS = 16
SSD_HEAD_DIM = 64
SSD_INNER = SSD_HEADS * SSD_HEAD_DIM
SSD_GROUPS = 4
SSD_STATE = 128
SSD_CONV = 5
SSD_CHUNK = 128
SSD_BC = SSD_GROUPS * SSD_STATE
SSD_CONV_DIM = SSD_INNER + 2 * SSD_BC
SSD_STATE_COLS = SSD_CONV_DIM + 2 * SSD_HEADS

CF_CH = 1024
CF_KERNEL = 31

AB_IN = SSD_INNER + SSD_STATE_COLS + 2 * CF_CH
AB_OUT = SSD_INNER + CF_CH

HG_HEADS = 8
HG_DK = 128
HG_DV = D_MODEL // HG_HEADS
HG_KEY = HG_HEADS * HG_DK
HG_VAL = HG_HEADS * HG_DV
HG_CHUNK = 64
HG_IN = HG_KEY + 2 * HG_VAL + 2 * HG_KEY

N_EXPERTS = 16
N_EXPERT_GROUPS = 4
EXPERTS_PER_GROUP = N_EXPERTS // N_EXPERT_GROUPS
TOP_K = 2
D_EXPERT = 512

N_EVEN = (DEPTH_2 + 1) // 2
N_ODD = DEPTH_2 // 2


def rmsnorm(x, g):
    xf = x.astype(jnp.float32)
    y = xf * lax.rsqrt(jnp.mean(xf * xf, axis=-1, keepdims=True) + EPS)
    return (y * g.astype(jnp.float32)).astype(x.dtype)

def layernorm(x, g, b):
    xf = x.astype(jnp.float32)
    mu = jnp.mean(xf, axis=-1, keepdims=True)
    xc = xf - mu
    var = jnp.mean(xc * xc, axis=-1, keepdims=True)
    return (xc * lax.rsqrt(var + EPS) * g.astype(jnp.float32) + b.astype(jnp.float32)).astype(x.dtype)

def modulation(cond, w, b):
    m = jax.nn.silu(cond) @ w + b
    return m.reshape(cond.shape[:-1] + (N_MOD, D_MODEL))

def dwconv(x, w, b):
    k = w.shape[0]
    y = lax.conv_general_dilated(x, w[:, None, :].astype(x.dtype), window_strides=(1,),
                                 padding=[(k // 2, k // 2)], dimension_numbers=("NWC", "WIO", "NWC"),
                                 feature_group_count=x.shape[-1])
    return y + b.astype(y.dtype)

def _flip(t):
    return jnp.flip(t, axis=1)

def _same(t):
    return t

def to_col_major(t, rows):
    b, _, ch = t.shape
    return t.reshape(b, rows, GRID_W, ch).transpose(0, 2, 1, 3).reshape(b, rows * GRID_W, ch)

def from_col_major(t, rows):
    b, _, ch = t.shape
    return t.reshape(b, GRID_W, rows, ch).transpose(0, 2, 1, 3).reshape(b, rows * GRID_W, ch)

def _carry_step(s, inp):
    dec, st = inp
    return dec * s + st, s

def ssd_scan(xs, dt, a_neg, bm, cm, s0, with_output):
    bsz, seqlen, nh, hp = xs.shape
    ng, ns = bm.shape[2], bm.shape[3]
    rep = nh // ng
    nc = seqlen // SSD_CHUNK
    la = (dt * a_neg).reshape(bsz, nc, SSD_CHUNK, ng, rep)
    acum = jnp.cumsum(la, axis=2)
    xdt = (xs.astype(jnp.float32) * dt[..., None]).reshape(bsz, nc, SSD_CHUNK, ng, rep, hp)
    bc = bm.astype(jnp.float32).reshape(bsz, nc, SSD_CHUNK, ng, ns)
    to_end = jnp.exp(acum[:, :, -1:] - acum)
    chunk_states = jnp.einsum("bcsgn,bcsgr,bcsgrp->bcgrpn", bc, to_end, xdt).reshape(bsz, nc, nh, hp, ns)
    chunk_decay = jnp.exp(acum[:, :, -1]).reshape(bsz, nc, nh)[..., None, None]
    s_final, s_in = lax.scan(_carry_step, s0, (jnp.moveaxis(chunk_decay, 1, 0), jnp.moveaxis(chunk_states, 1, 0)))
    if not with_output:
        return None, s_final
    s_in = jnp.moveaxis(s_in, 0, 1).reshape(bsz, nc, ng, rep, hp, ns)
    cc = cm.astype(jnp.float32).reshape(bsz, nc, SSD_CHUNK, ng, ns)
    causal = jnp.tril(jnp.ones((SSD_CHUNK, SSD_CHUNK), dtype=bool))[:, :, None, None]
    seg = acum[:, :, :, None] - acum[:, :, None, :]
    decay = jnp.exp(jnp.where(causal, seg, -jnp.inf))
    cb = jnp.einsum("bclgn,bcsgn->bclsg", cc, bc)
    y_diag = jnp.einsum("bclsg,bclsgr,bcsgrp->bclgrp", cb, decay, xdt)
    y_off = jnp.einsum("bclgn,bcgrpn,bclgr->bclgrp", cc, s_in, jnp.exp(acum))
    return (y_diag + y_off).reshape(bsz, seqlen, nh, hp), s_final

def ssd_inputs(p_state, conv_w, conv_b, dt_bias):
    b, n, _ = p_state.shape
    xbc = jax.nn.silu(dwconv(p_state[..., :SSD_CONV_DIM], conv_w, conv_b))
    xs = xbc[..., :SSD_INNER].reshape(b, n, SSD_HEADS, SSD_HEAD_DIM)
    bm = xbc[..., SSD_INNER:SSD_INNER + SSD_BC].reshape(b, n, SSD_GROUPS, SSD_STATE)
    cm = xbc[..., SSD_INNER + SSD_BC:].reshape(b, n, SSD_GROUPS, SSD_STATE)
    dt_raw = p_state[..., SSD_CONV_DIM:].astype(jnp.float32).reshape(b, n, 2, SSD_HEADS)
    dt = jax.nn.softplus(dt_raw + dt_bias.astype(jnp.float32))
    return xs, bm, cm, dt

def ssd_readout(y, xs, z, d_skip, norm_g):
    b, n = y.shape[0], y.shape[1]
    y = y + d_skip.astype(jnp.float32)[:, None] * xs.astype(jnp.float32)
    y = y.reshape(b, n, SSD_INNER) * jax.nn.silu(z.astype(jnp.float32))
    return rmsnorm(y, norm_g)

def conformer_conv(v, gate, dw_w, dw_b, ln_g, ln_b, rows):
    u = v * jax.nn.sigmoid(gate)
    b, n, ch = u.shape
    if rows is not None:
        u = u.reshape(b * rows, GRID_W, ch)
    u = dwconv(u, dw_w, dw_b).reshape(b, n, ch)
    return jax.nn.silu(layernorm(u, ln_g, ln_b))

def even_mixer(hc, hl, w_in, conv_w, conv_b, dt_bias, a_log, d_skip, ssd_g,
               cf_w, cf_b, cf_lng, cf_lnb, w_out, rows, need_ctx):
    a_neg = -jnp.exp(a_log.astype(jnp.float32))
    s_lo, s_hi = SSD_INNER, SSD_INNER + SSD_STATE_COLS
    pl = hl @ w_in
    if need_ctx:
        pc = hc @ w_in
        pc_state = pc[..., s_lo:s_hi]
    else:
        pc_state = hc @ w_in[:, s_lo:s_hi]
    xs_l, b_l, c_l, dt_l = ssd_inputs(pl[..., s_lo:s_hi], conv_w, conv_b, dt_bias)
    xs_c, b_c, c_c, dt_c = ssd_inputs(pc_state, conv_w, conv_b, dt_bias)
    bsz = hl.shape[0]
    ys_c, ys_l = [], []
    for d in range(2):
        flip = _flip if d else _same
        s0 = jnp.zeros((bsz, SSD_HEADS, SSD_HEAD_DIM, SSD_STATE), jnp.float32)
        y_c, s_ctx = ssd_scan(flip(xs_c), flip(dt_c[:, :, d]), a_neg[d], flip(b_c), flip(c_c), s0, need_ctx)
        y_l, _ = ssd_scan(flip(xs_l), flip(dt_l[:, :, d]), a_neg[d], flip(b_l), flip(c_l), s_ctx, True)
        ys_l.append(flip(y_l))
        if need_ctx:
            ys_c.append(flip(y_c))
    cf0 = SSD_INNER + SSD_STATE_COLS
    o_ssd = ssd_readout(ys_l[0] + ys_l[1], xs_l, pl[..., :SSD_INNER], d_skip, ssd_g)
    o_cf = conformer_conv(pl[..., cf0:cf0 + CF_CH], pl[..., cf0 + CF_CH:], cf_w, cf_b, cf_lng, cf_lnb, rows)
    y_lat = (jnp.concatenate([o_ssd, o_cf.astype(o_ssd.dtype)], axis=-1) @ w_out).astype(hl.dtype)
    y_ctx = None
    if need_ctx:
        oc_ssd = ssd_readout(ys_c[0] + ys_c[1], xs_c, pc[..., :SSD_INNER], d_skip, ssd_g)
        oc_cf = conformer_conv(pc[..., cf0:cf0 + CF_CH], pc[..., cf0 + CF_CH:], cf_w, cf_b, cf_lng, cf_lnb, None)
        y_ctx = (jnp.concatenate([oc_ssd, oc_cf.astype(oc_ssd.dtype)], axis=-1) @ w_out).astype(hc.dtype)
    return y_ctx, y_lat

def hgrn2_scan(q, k, v, logf, s0, with_output):
    bsz, seqlen, nh, dk = k.shape
    dv = v.shape[-1]
    nc = seqlen // HG_CHUNK

    def chunks(t):
        return t.astype(jnp.float32).reshape(bsz, nc, HG_CHUNK, nh, t.shape[-1])

    kc, vc = chunks(k), chunks(v)
    gcum = jnp.cumsum(chunks(logf), axis=2)
    g_end = gcum[:, :, -1]
    k_end = kc * jnp.exp(g_end[:, :, None] - gcum)
    chunk_states = jnp.einsum("bcshk,bcshv->bchkv", k_end, vc)
    s_final, s_in = lax.scan(_carry_step, s0, (jnp.moveaxis(jnp.exp(g_end)[..., None], 1, 0),
                                               jnp.moveaxis(chunk_states, 1, 0)))
    if not with_output:
        return None, s_final
    s_in = jnp.moveaxis(s_in, 0, 1)
    qc = chunks(q)
    g_mid = gcum[:, :, HG_CHUNK // 2 - 1:HG_CHUNK // 2]
    q_rel = qc * jnp.exp(gcum - g_mid)
    k_rel = kc * jnp.exp(g_mid - gcum)
    causal = jnp.tril(jnp.ones((HG_CHUNK, HG_CHUNK), dtype=bool))
    att = jnp.where(causal, jnp.einsum("bclhk,bcshk->bchls", q_rel, k_rel), 0.0)
    o_intra = jnp.einsum("bchls,bcshv->bclhv", att, vc)
    o_inter = jnp.einsum("bclhk,bchkv->bclhv", qc * jnp.exp(gcum), s_in)
    return (o_intra + o_inter).reshape(bsz, seqlen, nh, dv), s_final

def hgrn2_gates(p_state, lb):
    b, n, _ = p_state.shape
    v = p_state[..., :HG_VAL].reshape(b, n, HG_HEADS, HG_DV)
    f_raw = p_state[..., HG_VAL:].astype(jnp.float32).reshape(b, n, 2, HG_HEADS, HG_DK)
    lbh = lb.reshape(HG_HEADS, HG_DK)
    f = lbh + (1.0 - lbh) * jax.nn.sigmoid(f_raw)
    return v, 1.0 - f, jnp.log(f)

def hgrn2_readout(o, g, norm_g):
    b, n = o.shape[0], o.shape[1]
    return rmsnorm(o, norm_g).reshape(b, n, HG_VAL) * jax.nn.silu(g.astype(jnp.float32))

def odd_mixer(hc, hl, w_in, lb, norm_g, w_out, rows, need_ctx):
    st0 = HG_KEY + HG_VAL
    bsz, n_lat = hl.shape[0], hl.shape[1]
    pl = to_col_major(hl, rows) @ w_in
    q_l = jax.nn.silu(pl[..., :HG_KEY]).reshape(bsz, n_lat, HG_HEADS, HG_DK)
    v_l, k_l, lf_l = hgrn2_gates(pl[..., st0:], lb)
    if need_ctx:
        pc = hc @ w_in
        q_c = jax.nn.silu(pc[..., :HG_KEY]).reshape(bsz, hc.shape[1], HG_HEADS, HG_DK)
        pc_state = pc[..., st0:]
    else:
        pc_state = hc @ w_in[:, st0:]
    v_c, k_c, lf_c = hgrn2_gates(pc_state, lb)
    os_c, os_l = [], []
    for d in range(2):
        flip = _flip if d else _same
        s0 = jnp.zeros((bsz, HG_HEADS, HG_DK, HG_DV), jnp.float32)
        qc_d = flip(q_c) if need_ctx else None
        o_c, s_ctx = hgrn2_scan(qc_d, flip(k_c[:, :, d]), flip(v_c), flip(lf_c[:, :, d]), s0, need_ctx)
        o_l, _ = hgrn2_scan(flip(q_l), flip(k_l[:, :, d]), flip(v_l), flip(lf_l[:, :, d]), s_ctx, True)
        os_l.append(flip(o_l))
        if need_ctx:
            os_c.append(flip(o_c))
    y_lat = from_col_major(hgrn2_readout(os_l[0] + os_l[1], pl[..., HG_KEY:st0], norm_g) @ w_out, rows).astype(hl.dtype)
    y_ctx = None
    if need_ctx:
        y_ctx = (hgrn2_readout(os_c[0] + os_c[1], pc[..., HG_KEY:st0], norm_g) @ w_out).astype(hc.dtype)
    return y_ctx, y_lat

def moe(h, router_w, router_b, w_gate, w_up, w_down):
    shp = h.shape
    t = h.reshape(-1, D_MODEL)
    scores = jax.nn.sigmoid((t @ router_w).astype(jnp.float32))
    sel = scores + router_b.astype(jnp.float32)
    grouped = sel.reshape(-1, N_EXPERT_GROUPS, EXPERTS_PER_GROUP)
    group_score = lax.top_k(grouped, TOP_K)[0].sum(-1)
    g_idx = jnp.argmax(group_score, axis=-1)
    idx = jnp.broadcast_to(g_idx[:, None, None], (t.shape[0], 1, EXPERTS_PER_GROUP))
    in_group = jnp.take_along_axis(grouped, idx, axis=1)[:, 0]
    _, local = lax.top_k(in_group, TOP_K)
    expert_idx = g_idx[:, None] * EXPERTS_PER_GROUP + local
    wts = jnp.take_along_axis(scores, expert_idx, axis=1)
    wts = wts / jnp.sum(wts, axis=-1, keepdims=True)
    combine = jnp.sum(jax.nn.one_hot(expert_idx, N_EXPERTS, dtype=jnp.float32) * wts[..., None], axis=1)

    def expert(acc, p):
        wg, wu, wd, gate_col = p
        y = (jax.nn.silu(t @ wg) * (t @ wu)) @ wd
        return acc + gate_col[:, None] * y, None

    out, _ = lax.scan(expert, jnp.zeros(t.shape, jnp.float32), (w_gate, w_up, w_down, combine.T))
    return out.reshape(shp).astype(h.dtype)

def second_inputs(seed: int = 0) -> dict:
    key = jax.random.key(seed)
    ks = jax.random.split(key, 32)
    f32 = jnp.float32

    def dense(k, shape, fan_in, scale=1.0):
        return scale * fan_in ** -0.5 * jax.random.normal(k, shape, f32)

    def gain(k, shape):
        return 1.0 + 0.1 * jax.random.normal(k, shape, f32)

    def small(k, shape, s=0.02):
        return s * jax.random.normal(k, shape, f32)

    dt0 = jnp.exp(jax.random.uniform(ks[14], (N_EVEN, 2, SSD_HEADS), f32, np.log(1e-3), np.log(1e-1)))
    return {
        "x": jax.random.normal(ks[0], (BATCH, SEQ, D_MODEL), f32),
        "c": jax.random.normal(ks[1], (BATCH, D_MODEL), f32),
        "ctx": jax.random.normal(ks[2], (BATCH, CTX_LEN, D_MODEL), f32),
        "c_ctx": jax.random.normal(ks[3], (D_MODEL,), f32),
        "mod_w": dense(ks[4], (DEPTH_2, D_MODEL, N_MOD * D_MODEL), D_MODEL, 0.5),
        "mod_b": small(ks[5], (DEPTH_2, N_MOD * D_MODEL)),
        "norm_mix_g": gain(ks[6], (DEPTH_2, D_MODEL)),
        "norm_ffn_g": gain(ks[7], (DEPTH_2, D_MODEL)),
        "router_w": dense(ks[8], (D_MODEL, N_EXPERTS), D_MODEL),
        "router_b": small(ks[9], (N_EXPERTS,), 0.01),
        "moe_w_gate": dense(ks[10], (DEPTH_2, N_EXPERTS, D_MODEL, D_EXPERT), D_MODEL),
        "moe_w_up": dense(ks[11], (DEPTH_2, N_EXPERTS, D_MODEL, D_EXPERT), D_MODEL),
        "moe_w_down": dense(ks[12], (DEPTH_2, N_EXPERTS, D_EXPERT, D_MODEL), D_EXPERT),
        "ab_w_in": dense(ks[13], (N_EVEN, D_MODEL, AB_IN), D_MODEL),
        "ssd_conv_w": dense(ks[15], (N_EVEN, SSD_CONV, SSD_CONV_DIM), SSD_CONV),
        "ssd_conv_b": small(ks[16], (N_EVEN, SSD_CONV_DIM)),
        "ssd_dt_bias": dt0 + jnp.log(-jnp.expm1(-dt0)),
        "ssd_a_log": jnp.log(jax.random.uniform(ks[17], (N_EVEN, 2, SSD_HEADS), f32, 1.0, 16.0)),
        "ssd_d": gain(ks[18], (N_EVEN, SSD_HEADS)),
        "ssd_norm_g": gain(ks[19], (N_EVEN, SSD_INNER)),
        "cf_dw_w": dense(ks[20], (N_EVEN, CF_KERNEL, CF_CH), CF_KERNEL),
        "cf_dw_b": small(ks[21], (N_EVEN, CF_CH)),
        "cf_ln_g": gain(ks[22], (N_EVEN, CF_CH)),
        "cf_ln_b": small(ks[23], (N_EVEN, CF_CH)),
        "ab_w_out": dense(ks[24], (N_EVEN, AB_OUT, D_MODEL), AB_OUT),
        "hg_w_in": dense(ks[25], (N_ODD, D_MODEL, HG_IN), D_MODEL),
        "hg_lb": small(ks[26], (DEPTH_2, HG_KEY), 0.1),
        "hg_norm_g": gain(ks[27], (N_ODD, HG_DV)),
        "hg_w_out": dense(ks[28], (N_ODD, HG_VAL, D_MODEL), HG_VAL),
        "final_norm_g": gain(ks[29], (D_MODEL,)),
    }

def second_block(x, c, ctx, c_ctx, mod_w, mod_b, norm_mix_g, norm_ffn_g, router_w, router_b,
              moe_w_gate, moe_w_up, moe_w_down, ab_w_in, ssd_conv_w, ssd_conv_b, ssd_dt_bias,
              ssd_a_log, ssd_d, ssd_norm_g, cf_dw_w, cf_dw_b, cf_ln_g, cf_ln_b, ab_w_out,
              hg_w_in, hg_lb, hg_norm_g, hg_w_out, final_norm_g):
    rows = x.shape[1] // GRID_W
    lb_all = jnp.cumsum(jax.nn.softmax(hg_lb.astype(jnp.float32), axis=0), axis=0)
    lb_all = lb_all - lb_all[0]
    xl, xc = x, ctx
    for l in range(DEPTH_2):
        last = l == DEPTH_2 - 1
        j = l // 2
        m_l = modulation(c, mod_w[l], mod_b[l])[:, :, None, :]
        m_c = modulation(c_ctx, mod_w[l], mod_b[l])
        hl = rmsnorm(xl, norm_mix_g[l]) * (1.0 + m_l[:, 1]) + m_l[:, 0]
        hc = rmsnorm(xc, norm_mix_g[l]) * (1.0 + m_c[1]) + m_c[0]
        if l % 2 == 0:
            y_c, y_l = even_mixer(hc, hl, ab_w_in[j], ssd_conv_w[j], ssd_conv_b[j], ssd_dt_bias[j],
                                  ssd_a_log[j], ssd_d[j], ssd_norm_g[j], cf_dw_w[j], cf_dw_b[j],
                                  cf_ln_g[j], cf_ln_b[j], ab_w_out[j], rows, not last)
        else:
            y_c, y_l = odd_mixer(hc, hl, hg_w_in[j], lb_all[l], hg_norm_g[j], hg_w_out[j], rows, not last)
        xl = xl + m_l[:, 2] * y_l
        hl = rmsnorm(xl, norm_ffn_g[l]) * (1.0 + m_l[:, 4]) + m_l[:, 3]
        xl = xl + m_l[:, 5] * moe(hl, router_w, router_b, moe_w_gate[l], moe_w_up[l], moe_w_down[l])
        if not last:
            xc = xc + m_c[2] * y_c
            hc = rmsnorm(xc, norm_ffn_g[l]) * (1.0 + m_c[4]) + m_c[3]
            xc = xc + m_c[5] * moe(hc, router_w, router_b, moe_w_gate[l], moe_w_up[l], moe_w_down[l])
    return rmsnorm(xl, final_norm_g)


def setup_inputs(seed=0):
    out = dict(first_inputs(seed))
    for name, value in second_inputs(seed + 1).items():
        if name != "x":
            out[name + "_2"] = value
    return out


def reference(
    x, p, ln_pre_mix, w_in, conv_w, a_log, dt_bias, gdn_norm, w_proj_a, w_proj_b, w_out,
    ln_post_mix, ln_pre_ffn, w_ffn_gate, w_ffn_up, w_ffn_down, ln_post_ffn, w_ple, ln_ple,
    w_ple_gate, c_2, ctx_2, c_ctx_2, mod_w_2, mod_b_2, norm_mix_g_2, norm_ffn_g_2, router_w_2,
    router_b_2, moe_w_gate_2, moe_w_up_2, moe_w_down_2, ab_w_in_2, ssd_conv_w_2, ssd_conv_b_2,
    ssd_dt_bias_2, ssd_a_log_2, ssd_d_2, ssd_norm_g_2, cf_dw_w_2, cf_dw_b_2, cf_ln_g_2,
    cf_ln_b_2, ab_w_out_2, hg_w_in_2, hg_lb_2, hg_norm_g_2, hg_w_out_2, final_norm_g_2,
):
    x = first_block(
        x, p, ln_pre_mix, w_in, conv_w, a_log, dt_bias, gdn_norm, w_proj_a, w_proj_b, w_out,
        ln_post_mix, ln_pre_ffn, w_ffn_gate, w_ffn_up, w_ffn_down, ln_post_ffn, w_ple, ln_ple,
        w_ple_gate,
    )
    return second_block(
        x, c_2, ctx_2, c_ctx_2, mod_w_2, mod_b_2, norm_mix_g_2, norm_ffn_g_2, router_w_2,
        router_b_2, moe_w_gate_2, moe_w_up_2, moe_w_down_2, ab_w_in_2, ssd_conv_w_2,
        ssd_conv_b_2, ssd_dt_bias_2, ssd_a_log_2, ssd_d_2, ssd_norm_g_2, cf_dw_w_2, cf_dw_b_2,
        cf_ln_g_2, cf_ln_b_2, ab_w_out_2, hg_w_in_2, hg_lb_2, hg_norm_g_2, hg_w_out_2,
        final_norm_g_2,
    )


_drawn_inputs = setup_inputs


def setup_inputs(seed=0):
    import zlib

    import numpy as np

    out = dict(_drawn_inputs(seed))
    spreads = {}
    factors = {'ctx_2': 4.794,
     'c_ctx_2': 3.672,
     'ssd_conv_b_2': 8.0,
     'ssd_d_2': 7.697,
     'ssd_norm_g_2': 3.192,
     'cf_dw_b_2': 8.0,
     'cf_ln_g_2': 4.587,
     'cf_ln_b_2': 27.106,
     'hg_lb_2': 21.544,
     'hg_norm_g_2': 3.378}
    for name, (base, spread) in spreads.items():
        noise = np.random.default_rng([zlib.crc32(name.encode()), seed]).standard_normal(out[name].shape)
        drawn = base * np.exp(spread * noise) if base else spread * noise
        out[name] = jnp.asarray(drawn.astype(out[name].dtype))
    for name, factor in factors.items():
        out[name] = (out[name] * factor).astype(out[name].dtype)
    return out
```

```python
from contextlib import ExitStack, contextmanager

import numpy as np

import concourse.bass as bass
from concourse import mybir

F32 = mybir.dt.float32
I32 = mybir.dt.int32
ALU = mybir.AluOpType
ACT = mybir.ActivationFunctionType
AX = mybir.AxisListType

P = 128
D = 1024
DC = D // P
SEQ = 256
EPS = 1e-6
HEADS = 8
HD = 128
FF_TILES = 22
NEG = -1e30
SLOTS = 6
WIDE = 256
SLOT = 2048
S_HEADS, S_HD, S_GROUPS = 16, 64, 4
EXPERTS = 16
CHOICES = 2
ITEMS = 24
GRID_W = 64
ROWS = SEQ // GRID_W


def constant_table():
    i = np.arange(P)
    f = np.float32
    tri = (i[:, None] <= i[None, :])
    c = {}
    c["ident"] = np.eye(P, dtype=f)
    c["ones"] = np.ones((P, P), f)
    c["tri_f"] = tri.astype(f)
    c["tri_r"] = tri.T.astype(f)
    c["neg_f"] = np.where(tri, f(0), f(NEG))
    neg_r = np.where(tri.T, f(0), f(NEG))
    c["neg_qk"] = np.concatenate([neg_r, np.zeros((P, P), f), neg_r], 1)
    for n in range(7):
        b = 1 << n
        same = (i[:, None] // (2 * b)) == (i[None, :] // (2 * b))
        c[f"join{n}"] = (same & ((i[:, None] // b) % 2 == 0) & ((i[None, :] // b) % 2 == 1)).astype(f)
    rot = np.zeros((P, P), f)
    for d in range(64):
        rot[d + 64, d] = -1.0
        rot[d, d + 64] = 1.0
    c["rot"] = rot
    inv = (f(1.0) / (f(10000.0) ** (np.arange(0, HD, 2, dtype=f) / f(HD)))).astype(f)
    ang = (np.arange(SEQ, dtype=f)[None, :] * inv[:, None]).astype(f)
    c["cos"] = np.tile(np.cos(ang).astype(f), (2, 1))
    c["sin"] = np.tile(np.sin(ang).astype(f), (2, 1))
    j = np.arange(64)
    m = (j[:, None] <= j[None, :])
    c["keep_f"] = np.tile(m.astype(f), (2, 1))
    c["keep_r"] = np.tile(m.T.astype(f), (2, 1))
    t = np.arange(SEQ)
    whole = np.ones(SEQ, f)
    c["carry_f"] = np.tile(np.concatenate([whole, (t % 64 != 0).astype(f)]), (P, 1))
    c["carry_r"] = np.tile(np.concatenate([(t != SEQ - 1).astype(f), (t % 64 != 63).astype(f)]), (P, 1))
    c["count"] = np.tile(np.arange(P, dtype=f), (P, 1))
    c["slot"] = np.arange(P, dtype=f)[:, None].copy()
    k = np.arange(4)
    c["before"] = np.tile((k[None, :] < k[:, None]).astype(f).reshape(1, 16), (P, 1))
    c["notbefore"] = np.tile((k[None, :] >= k[:, None]).astype(f).reshape(1, 16), (P, 1))
    return c


CONSTANTS = constant_table()
CONST_AT = {}
_at = 0
for _name, _value in CONSTANTS.items():
    CONST_AT[_name] = (_at, _value.shape[1])
    _at += _value.shape[1]
CONST_WORDS = _at
CONST_AT["neg_r"] = (CONST_AT["neg_qk"][0], P)

VECTORS = [
    ("ln_pre_mix", 8), ("ln_post_mix", 8), ("ln_pre_ffn", 8), ("ln_post_ffn", 8), ("ln_ple", 8),
    ("gdn_norm", 1), ("c_2", 8), ("c_ctx_2", 8), ("norm_mix_g_2", 16), ("norm_ffn_g_2", 16),
    ("ssd_conv_b_2", 16), ("ssd_norm_g_2", 8), ("hg_norm_g_2", 1),
    ("cf_dw_b_2", 8), ("cf_ln_g_2", 8), ("cf_ln_b_2", 8), ("hg_lb_2", 16), ("final_norm_g_2", 8), ("ssd_d_2", 8),
    ("conv_w", 96), ("ssd_conv_w_2", 80), ("mod_b_2", 96),
    ("cf_dw_w_2", 8 * 31),
]


def vector_plan():
    pieces, cols, tile, row = [], {}, 0, 0
    for name, n in VECTORS:
        cols[name] = []
        done = 0
        while done < n:
            if row == P:
                tile, row = tile + 1, 0
            m = min(n - done, P - row)
            pieces.append((name, done, m, tile, row))
            cols[name] += [tile * P + row + q for q in range(m)]
            done += m
            row += m
    return pieces, cols, tile + 1


PIECES, COLS, VTILES = vector_plan()


class Signal:

    def __init__(self, sem):
        self.sem, self.n = sem, 0

    def by(self, instruction):
        instruction.then_inc(self.sem, 1)
        self.n += 1

    def wait(self, engine):
        engine.wait_ge(self.sem, self.n)

    def link(self, engine, instruction):
        self.by(instruction)
        self.wait(engine)


@contextmanager
def stage(nc, *names):
    with ExitStack() as held:
        sems = [held.enter_context(nc.semaphore(n)) for n in names]
        with nc.Block() as block:
            yield (block, *sems)
        with nc.Block() as tidy:
            @tidy.gpsimd
            def _(pool):
                for s in sems:
                    pool.sem_clear(s)


class Feed:

    def __init__(self, nc, hold):
        self.buf = hold(nc.sbuf_tensor("weights", [P, SLOTS, SLOT], F32))
        self.loaded = [hold(nc.semaphore(f"weights_loaded{s}")) for s in range(SLOTS)]
        self.plans = []
        self.at = 0
        self.issued = 0
        self.taken = 0

    def plan(self, iterations, per, source):
        assert iterations == 1 or per % SLOTS == 0
        self.plans.append((iterations, per, source))

    def load(self, sp, src, shift=0):
        slot = self.issued % SLOTS
        k, n = src.shape[1], src.shape[2]
        dst = self.buf[:, slot, 0:k * n].rearrange("p (k n) -> p k n", k=k)
        sp.dma_start(dst, src).then_inc(self.loaded[slot], 16)
        self.issued += 1

    def arrive(self, pe, shape, rounds=0):
        slot = self.taken % SLOTS
        pe.wait_ge(self.loaded[slot], 16 * (self.taken // SLOTS + 1) + 16 * rounds)
        self.taken += 1
        k, n = shape
        return self.buf[:, slot, 0:k * n].rearrange("p (k n) -> p k n", k=k)

    def first(self, sp):
        _, per, source = self.plans[0]
        for j in range(min(SLOTS, per)):
            self.load(sp, source(0, j))

    def run(self, sp, matmuls_done, done, per_iteration=0, before=None):
        iterations, per, source = self.plans[self.at]
        base = self.issued - min(SLOTS, per)
        if iterations == 1:
            for j in range(SLOTS, per):
                if before:
                    before(sp, 0, j)
                sp.wait_ge(matmuls_done, done[j - SLOTS])
                self.load(sp, source(0, j))
        else:
            with sp.Fori(0, iterations - 1) as i:
                for j in range(per):
                    if before:
                        before(sp, i + 1, j)
                    back = j + per - SLOTS
                    if back < per:
                        sp.wait_ge(matmuls_done, i * per_iteration + done[back])
                    else:
                        sp.wait_ge(matmuls_done, (i + 1) * per_iteration + done[back - per])
                    self.load(sp, source(i + 1, j))
            self.issued += per * (iterations - 2)

        def used_up(back):
            sp.wait_ge(matmuls_done, (back // per) * per_iteration + done[back % per])

        self.run_ahead(sp, self.issued - base, used_up)

    def run_ahead(self, sp, units, used_up):
        self.at += 1
        if self.at < len(self.plans):
            _, per, source = self.plans[self.at]
            for j in range(min(SLOTS, per)):
                if units + j >= SLOTS:
                    assert units + j - SLOTS < units
                    used_up(units + j - SLOTS)
                self.load(sp, source(0, j))


class Kit:

    def __init__(self, nc, hold):
        self.nc = nc
        self.const = hold(nc.sbuf_tensor("const", [P, CONST_WORDS], F32))
        self.vec = hold(nc.sbuf_tensor("vec", [P, VTILES * P], F32))
        self.bank = [hold(nc.psum_tensor(f"bank{b}", [P, 512], F32)) for b in range(8)]
        self.feed = Feed(nc, hold)
        self.tensors = 0

    def sb(self, name, shape):
        self.tensors += 1
        return self.nc.sbuf_tensor(f"{name}_{self.tensors}", shape, F32)

    def c(self, name, rows=P):
        at, n = CONST_AT[name]
        return self.const[0:rows, at:at + n]

    def col(self, name, k=0):
        at = COLS[name][k]
        return self.vec[:, at:at + 1]

    def cols(self, name, k, n):
        at = COLS[name][k]
        assert COLS[name][k + n - 1] == at + n - 1
        return self.vec[:, at:at + n]


def turn(kit, groups):
    nc = kit.nc
    with stage(nc, "turned", "copied_v", "copied_a") as (block, turned, copied_v, copied_a):
        @block.tensor
        def _(pe):
            for n, (sources, _) in enumerate(groups):
                if n >= 4:
                    pe.wait_ge((copied_v, copied_a)[n % 2], (n - 4) // 2 + 1)
                at = 0
                for src in sources:
                    rows, width = src.shape
                    last = pe.transpose(kit.bank[n % 4][0:width, at:at + rows], src, kit.c("ident")[0:rows, 0:rows])
                    at += rows
                last.then_inc(turned, 1)

        @block.vector
        def _(dve):
            for n, (sources, dst) in list(enumerate(groups))[0::2]:
                dve.wait_ge(turned, n + 1)
                total = sum(s.shape[0] for s in sources)
                src = kit.bank[n % 4][0:dst.shape[0], 0:total]
                if len(dst.shape) == 3:
                    src = src.rearrange("p (a b) -> p a b", a=dst.shape[1])
                dve.tensor_copy(dst, src).then_inc(copied_v, 1)

        @block.scalar
        def _(act):
            for n, (sources, dst) in list(enumerate(groups))[1::2]:
                act.wait_ge(turned, n + 1)
                total = sum(s.shape[0] for s in sources)
                src = kit.bank[n % 4][0:dst.shape[0], 0:total]
                if len(dst.shape) == 3:
                    src = src.rearrange("p (a b) -> p a b", a=dst.shape[1])
                act.copy(dst, src).then_inc(copied_a, 1)


def rmsnorm(kit, x, parts, tiles=DC, width=D, first=0):
    nc = kit.nc
    T = x.shape[2]
    with ExitStack() as mem:
        sq = mem.enter_context(kit.sb("squares", [P, 4, T]))
        rstd = mem.enter_context(kit.sb("rstd", [P, T]))
        tmp = mem.enter_context(kit.sb("normed", [P, 4, T]))
        with stage(nc, "squared", "summed", "mean_ready", "root_ready", "v") as (
                block, squared, summed, mean_ready, root_ready, vsem):
            total = kit.bank[0][:, 0:T]

            @block.scalar
            def _(act):
                for c in range(tiles):
                    if c >= 4:
                        act.wait_ge(summed, c - 3)
                    act.activation(sq[:, c % 4, :], x[:, c, :], ACT.Square).then_inc(squared, 1)
                act.wait_ge(mean_ready, 1)
                act.activation(rstd[:, :], rstd[:, :], ACT.Sqrt).then_inc(root_ready, 1)

            @block.tensor
            def _(pe):
                for c in range(tiles):
                    pe.wait_ge(squared, c + 1)
                    pe.matmul(total, kit.c("ones"), sq[:, c % 4, :], start=c == 0,
                              stop=c == tiles - 1).then_inc(summed, 1)

            @block.vector
            def _(dve):
                v = Signal(vsem)
                dve.wait_ge(summed, tiles)
                dve.tensor_scalar(rstd[:, :], total, 1.0 / width, EPS, ALU.mult, ALU.add).then_inc(mean_ready, 1)
                dve.wait_ge(root_ready, 1)
                v.link(dve, dve.reciprocal(rstd[:, :], rstd[:, :]))
                n = 0
                for c in range(tiles):
                    for (sl, out, gain, bias, residual) in parts:
                        grid = (lambda ap: ap.rearrange("p (r w) -> p r w", w=GRID_W)) if len(out(c).shape) == 3 else (lambda ap: ap)
                        xs, rs = grid(x[:, c, sl]), grid(rstd[:, sl])
                        if bias is None and residual is None:
                            v.by(dve.scalar_tensor_tensor(out(c), xs, gain(c), rs, ALU.mult, ALU.mult))
                            continue
                        t = grid(tmp[:, n % 4, sl])
                        n += 1
                        v.link(dve, dve.scalar_tensor_tensor(t, xs, gain(c), rs, ALU.mult, ALU.mult))
                        if bias is not None:
                            v.by(dve.tensor_scalar(out(c), t, bias(c), None, ALU.add))
                        else:
                            v.by(dve.tensor_tensor(out(c), t, residual(c), ALU.add))


def project(kit, x, ktiles, T, widths, evacuate, engine="vector", evac_incs=1):
    nc = kit.nc
    feed = kit.feed
    done, n = [], 0
    for w in widths:
        n += w // P
        done.append(n)
    with stage(nc, "tiles_ready", "evacuated", "step") as (block, ready, evacuated, step):
        @block.sync
        def _(sp):
            feed.run(sp, ready, done)

        @block.tensor
        def _(pe):
            n = 0
            for w in widths:
                unit = feed.arrive(pe, (ktiles, w))
                for m in range(w // P):
                    if n >= 4:
                        pe.wait_ge(evacuated, n - 3)
                    for k in range(ktiles):
                        last = pe.matmul(kit.bank[n % 4][:, 0:T], unit[:, k, m * P:(m + 1) * P], x(k),
                                         start=k == 0, stop=k == ktiles - 1)
                    last.then_inc(ready, 1)
                    n += 1

        def drain(eng):
            s = Signal(step)
            for n in range(done[-1]):
                eng.wait_ge(ready, n + 1)
                evacuate(eng, s, n, kit.bank[n % 4][:, 0:T]).then_inc(evacuated, 1)

        if engine == "vector":
            @block.vector
            def _(dve):
                drain(dve)
        else:
            @block.scalar
            def _(act):
                drain(act)


def project_loop(kit, x, T, iterations, evacuate):
    nc = kit.nc
    feed = kit.feed
    per = 2 * SLOTS
    with stage(nc, "tiles_ready", "evacuated") as (block, ready, evacuated):
        @block.sync
        def _(sp):
            feed.run(sp, ready, [2 * (j + 1) for j in range(SLOTS)], per)

        @block.tensor
        def _(pe):
            with pe.Fori(0, iterations) as i:
                n = 0
                for j in range(SLOTS):
                    unit = feed.arrive(pe, (DC, WIDE), rounds=i)
                    for m in range(2):
                        pe.wait_ge(evacuated, i * per + n + 1)
                        for k in range(DC):
                            last = pe.matmul(kit.bank[n % 4][:, 0:T], unit[:, k, m * P:(m + 1) * P], x(k),
                                             start=k == 0, stop=k == DC - 1)
                        last.then_inc(ready, 1)
                        n += 1
            feed.taken += SLOTS * (iterations - 1)

        @block.vector
        def _(dve):
            dve.sem_inc(evacuated, 4)
            with dve.Fori(0, iterations) as i:
                for n in range(per):
                    dve.wait_ge(ready, i * per + n + 1)
                    evacuate(dve, i, n, kit.bank[n % 4][:, 0:T]).then_inc(evacuated, 1)


def project_down(kit, x, T, unit_ktiles, evacuate, engine="vector"):
    nc = kit.nc
    feed = kit.feed
    units = len(unit_ktiles)
    with stage(nc, "units_used", "evacuated", "step") as (block, used, evacuated, step):
        @block.sync
        def _(sp):
            feed.run(sp, used, [u + 1 for u in range(units - 1)] + [units - 1 + DC])

        @block.tensor
        def _(pe):
            at, total = 0, sum(unit_ktiles)
            for u, kt in enumerate(unit_ktiles):
                unit = feed.arrive(pe, (kt, D))
                for m in range(DC):
                    for k in range(kt):
                        last = pe.matmul(kit.bank[m][:, 0:T], unit[:, k, m * P:(m + 1) * P], x(at + k),
                                         start=at + k == 0, stop=at + k == total - 1)
                    if u == units - 1:
                        last.then_inc(used, 1)
                if u < units - 1:
                    last.then_inc(used, 1)
                at += kt

        def drain(eng):
            s = Signal(step)
            for m in range(DC):
                eng.wait_ge(used, units + m)
                evacuate(eng, s, m, kit.bank[m][:, 0:T]).then_inc(evacuated, 1)

        if engine == "vector":
            @block.vector
            def _(dve):
                drain(dve)
        else:
            @block.scalar
            def _(act):
                drain(act)


def head_norm(kit, x, pairs, spread, pre, post=None):
    nc = kit.nc
    with ExitStack() as mem:
        sq = mem.enter_context(kit.sb("head_squares", [P, 2, 512]))
        r = mem.enter_context(kit.sb("head_roots", [P, 2, 512]))
        with stage(nc, "squared", "summed", "mean_ready", "root_ready", "scaled", "inverted") as (
                block, squared, summed, mean_ready, root_ready, scaled, inverted):
            @block.scalar
            def _(act):
                def square(n):
                    if n >= 2:
                        act.wait_ge(summed, n - 1)
                    act.activation(sq[:, n % 2, :], x(n), ACT.Square).then_inc(squared, 1)

                square(0)
                for n in range(pairs):
                    if n + 1 < pairs:
                        square(n + 1)
                    act.wait_ge(mean_ready, n + 1)
                    act.activation(r[:, n % 2, :], r[:, n % 2, :], ACT.Sqrt).then_inc(root_ready, 1)

            @block.tensor
            def _(pe):
                for n in range(pairs):
                    pe.wait_ge(squared, n + 1)
                    if n >= 2:
                        pe.wait_ge(mean_ready, n - 1)
                    pe.matmul(kit.bank[n % 2][:, :], kit.c("ones"), sq[:, n % 2, :], start=True,
                              stop=True).then_inc(summed, 1)

            @block.vector
            def _(dve):
                def mean(n):
                    if n >= 2:
                        dve.wait_ge(scaled, n - 1)
                    dve.wait_ge(summed, n + 1)
                    dve.tensor_scalar(r[:, n % 2, :], kit.bank[n % 2][:, :], spread, EPS, ALU.mult,
                                      ALU.add).then_inc(mean_ready, 1)

                mean(0)
                for n in range(pairs):
                    if n + 1 < pairs:
                        mean(n + 1)
                    dve.wait_ge(root_ready, n + 1)
                    dve.reciprocal(r[:, n % 2, :], r[:, n % 2, :]).then_inc(inverted, 1)
                    dve.wait_ge(inverted, n + 1)
                    dve.scalar_tensor_tensor(x(n), x(n), pre(n), r[:, n % 2, :], ALU.mult, ALU.mult).then_inc(scaled, 1)


def softplus(kit, x, out, n):
    nc = kit.nc
    with ExitStack() as mem:
        e = mem.enter_context(kit.sb("sp_e", [P, n]))
        u = mem.enter_context(kit.sb("sp_u", [P, n]))
        w = mem.enter_context(kit.sb("sp_w", [P, n]))
        with stage(nc, "a", "exp_ready", "one_plus", "log_ready", "v") as (block, a, exp_ready, one_plus, log_ready, vsem):
            @block.scalar
            def _(act):
                act.activation(e[:, :], x, ACT.Abs).then_inc(a, 1)
                act.wait_ge(a, 1)
                act.activation(e[:, :], e[:, :], ACT.Exp, scale=-1.0).then_inc(exp_ready, 1)
                act.wait_ge(one_plus, 1)
                act.activation(w[:, :], u[:, :], ACT.Ln).then_inc(log_ready, 1)

            @block.vector
            def _(dve):
                v = Signal(vsem)
                dve.wait_ge(exp_ready, 1)
                dve.tensor_scalar(u[:, :], e[:, :], 1.0, None, ALU.add).then_inc(one_plus, 1)
                dve.wait_ge(one_plus, 1)
                dve.wait_ge(log_ready, 1)
                v.link(dve, dve.tensor_scalar(u[:, :], u[:, :], 1.0, None, ALU.subtract))
                v.link(dve, dve.tensor_tensor(e[:, :], e[:, :], u[:, :], ALU.subtract))
                v.link(dve, dve.tensor_tensor(e[:, :], e[:, :], w[:, :], ALU.add))
                v.by(dve.scalar_tensor_tensor(out, x, 0.0, e[:, :], ALU.max, ALU.add))


def rope(kit, qk):
    nc = kit.nc
    with ExitStack() as mem:
        a = mem.enter_context(kit.sb("x_cos", [P, 2, 2, SEQ]))
        b = mem.enter_context(kit.sb("swap_sin", [P, 2, 2, SEQ]))
        cos = kit.c("cos").unsqueeze(1).broadcast_to([P, 2, SEQ])
        sin = kit.c("sin").unsqueeze(1).broadcast_to([P, 2, SEQ])
        with stage(nc, "swapped", "bank_read", "v") as (block, swapped, bank_read, vsem):
            @block.tensor
            def _(pe):
                for n in range(8):
                    if n >= 2:
                        pe.wait_ge(bank_read, n - 1)
                    pe.matmul(kit.bank[n % 2][:, :], kit.c("rot"), qk[:, 2 * n:2 * n + 2, :].rearrange("p a b -> p (a b)"),
                              start=True, stop=True).then_inc(swapped, 1)

            @block.vector
            def _(dve):
                v = Signal(vsem)
                for n in range(8):
                    x = qk[:, 2 * n:2 * n + 2, :]
                    dve.wait_ge(swapped, n + 1)
                    v.by(dve.tensor_tensor(a[:, n % 2], x, cos, ALU.mult))
                    dve.tensor_tensor(b[:, n % 2], kit.bank[n % 2][:, :].rearrange("p (a b) -> p a b", a=2), sin,
                                      ALU.mult).then_inc(bank_read, 1)
                    v.wait(dve)
                    dve.wait_ge(bank_read, n + 1)
                    v.by(dve.tensor_tensor(x, a[:, n % 2], b[:, n % 2], ALU.add))
                    if n >= 1:
                        v.wait(dve)


def moba(kit, qkv, v_tok, y):
    nc = kit.nc
    scale = HD ** -0.5
    with ExitStack() as mem:
        s = mem.enter_context(kit.sb("scores", [P, 2, 384]))
        pt = mem.enter_context(kit.sb("probs_t", [P, 2, 384]))
        small = mem.enter_context(kit.sb("softmax_small", [P, 2, 8]))
        with stage(nc, "scored", "maxed", "exped", "normed", "pt_ready", "pt_copied", "y_ready", "y_copied", "v") as (
                block, scored, maxed, exped, normed, pt_ready, pt_copied, y_ready, y_copied, vsem):
            qt = lambda h, t: qkv[:, h, t * P:(t + 1) * P]
            kt = lambda h, n: qkv[:, HEADS + h, 0:n]

            @block.tensor
            def _(pe):
                def score(h):
                    b = kit.bank[h % 2]
                    if h >= 2:
                        pe.wait_ge(maxed, h - 1)
                    pe.matmul(b[:, 0:P], qt(h, 0), kt(h, P), start=True, stop=True)
                    pe.matmul(b[:, P:3 * P], qt(h, 1), kt(h, 2 * P), start=True, stop=True).then_inc(scored, 1)

                score(0)
                for h in range(HEADS):
                    if h + 1 < HEADS:
                        score(h + 1)
                    b = kit.bank[2 + h % 2]
                    pe.wait_ge(normed, h + 1)
                    if h >= 2:
                        pe.wait_ge(pt_copied, h - 1)
                    for j in range(3):
                        last = pe.transpose(b[:, j * P:(j + 1) * P], s[:, h % 2, j * P:(j + 1) * P], kit.c("ident"))
                    last.then_inc(pt_ready, 1)
                    o = kit.bank[4 + h % 2]
                    pe.wait_ge(pt_copied, h + 1)
                    if h >= 2:
                        pe.wait_ge(y_copied, h - 1)
                    vh = lambda t: v_tok[:, t, h * P:(h + 1) * P]
                    pe.matmul(o[:, 0:P], vh(0), pt[:, h % 2, 0:P], start=True, stop=True)
                    pe.matmul(o[:, P:2 * P], vh(0), pt[:, h % 2, P:2 * P], start=True, stop=False)
                    pe.matmul(o[:, P:2 * P], vh(1), pt[:, h % 2, 2 * P:3 * P], start=False, stop=True).then_inc(y_ready, 1)

            @block.vector
            def _(dve):
                v = Signal(vsem)

                def mask_and_max(h):
                    dve.wait_ge(scored, h + 1)
                    if h >= 2:
                        dve.wait_ge(pt_ready, h - 1)
                    v.link(dve, dve.scalar_tensor_tensor(s[:, h % 2, :], kit.bank[h % 2][:, 0:384], scale,
                                                         kit.c("neg_qk"), ALU.mult, ALU.add))
                    sm = small[:, h % 2]
                    v.by(dve.tensor_reduce(sm[:, 0:1], s[:, h % 2, 0:P], AX.X, ALU.max, negate=True))
                    v.by(dve.tensor_reduce(sm[:, 1:2], s[:, h % 2, P:384], AX.X, ALU.max, negate=True))
                    v.wait(dve)
                    dve.tensor_copy(sm[:, 6:7], sm[:, 0:1]).then_inc(maxed, 1)

                def normalise(h):
                    sm = small[:, h % 2]
                    dve.wait_ge(exped, 2 * h + 2)
                    v.link(dve, dve.reciprocal(sm[:, 4:6], sm[:, 2:4]))
                    v.link(dve, dve.tensor_scalar(s[:, h % 2, 0:P], s[:, h % 2, 0:P], sm[:, 4:5], None, ALU.mult))
                    dve.tensor_scalar(s[:, h % 2, P:384], s[:, h % 2, P:384], sm[:, 5:6], None, ALU.mult).then_inc(normed, 1)

                mask_and_max(0)
                for h in range(HEADS):
                    if h + 1 < HEADS:
                        mask_and_max(h + 1)
                    normalise(h)
                    dve.wait_ge(pt_ready, h + 1)
                    dve.tensor_copy(pt[:, h % 2, :], kit.bank[2 + h % 2][:, 0:384]).then_inc(pt_copied, 1)

            @block.scalar
            def _(act):
                def exps(h):
                    sm = small[:, h % 2]
                    act.wait_ge(maxed, h + 1)
                    act.activation(s[:, h % 2, 0:P], s[:, h % 2, 0:P], ACT.Exp, bias=sm[:, 0:1],
                                   accum_out=sm[:, 2:3]).then_inc(exped, 1)
                    act.activation(s[:, h % 2, P:384], s[:, h % 2, P:384], ACT.Exp, bias=sm[:, 1:2],
                                   accum_out=sm[:, 3:4]).then_inc(exped, 1)

                exps(0)
                for h in range(HEADS):
                    if h + 1 < HEADS:
                        exps(h + 1)
                    act.wait_ge(y_ready, h + 1)
                    act.copy(y[:, h, :], kit.bank[4 + h % 2][:, 0:SEQ]).then_inc(y_copied, 1)


def conv_taps(kit, x, tiles, taps, weight, spans, finish):
    nc = kit.nc
    T = x.shape[2]
    with ExitStack() as mem:
        acc = mem.enter_context(kit.sb("conv_sum", [P, 8, T]))
        with stage(nc, "conv_ready", "finished", "v") as (block, conv_ready, finished, vsem):
            @block.vector
            def _(dve):
                v = Signal(vsem)
                for g in range(tiles // 4):
                    if g >= 2:
                        dve.wait_ge(finished, 4 * (g - 1))
                    for order, tap in enumerate(taps):
                        for j in range(4):
                            c = 4 * g + j
                            a = acc[:, c % 8, :]
                            o, i = spans(tap, a, x[:, c, :])
                            if order == 0:
                                v.by(dve.tensor_scalar(a, x[:, c, :], weight(tap, c), None, ALU.mult))
                            elif order < len(taps) - 1:
                                v.by(dve.scalar_tensor_tensor(o, i, weight(tap, c), o, ALU.mult, ALU.add))
                            else:
                                dve.scalar_tensor_tensor(o, i, weight(tap, c), o, ALU.mult, ALU.add).then_inc(conv_ready, 1)
                        v.wait(dve)

            @block.scalar
            def _(act):
                for c in range(tiles):
                    act.wait_ge(conv_ready, c + 1)
                    finish(act, c, acc[:, c % 8, :]).then_inc(finished, 1)


def gdn_scalars(kit, u, w_ba, bias, alog, mem):
    nc = kit.nc
    new = lambda name: mem.enter_context(kit.sb(name, [P, 2, HEADS]))
    raw, beta, g, gc, egc, kbe, kdec = [new(n) for n in ("ba_a", "beta", "g", "g_sum", "g_exp", "beta_exp", "k_decay")]
    b0 = kit.bank[0][:, 0:32].rearrange("p (t n) -> p t n", t=2)
    with stage(nc, "ba_ready", "beta_ready", "v") as (block, ba_ready, beta_ready, vsem):
        @block.tensor
        def _(pe):
            for t in range(2):
                for k in range(DC):
                    last = pe.matmul(b0[:, t, :], u[:, k, t * P:(t + 1) * P], w_ba[:, k, :], start=k == 0, stop=k == DC - 1)
            last.then_inc(ba_ready, 1)

        @block.scalar
        def _(act):
            act.wait_ge(ba_ready, 1)
            act.activation(beta[:, :, :], b0[:, :, 0:8], ACT.Sigmoid).then_inc(beta_ready, 1)
            act.activation(alog[:, :], alog[:, :], ACT.Exp).then_inc(beta_ready, 1)

        @block.vector
        def _(dve):
            dve.wait_ge(beta_ready, 1)
            dve.tensor_tensor(raw[:, :, :], b0[:, :, 8:16], bias[:, :].unsqueeze(1).broadcast_to([P, 2, 8]), ALU.add).then_inc(vsem, 1)
    softplus(kit, raw[:, :, :].rearrange("p a b -> p (a b)"), raw[:, :, :].rearrange("p a b -> p (a b)"), 16)
    sums = kit.bank[0][:, 0:16].rearrange("p (t n) -> p t n", t=2)
    totals = kit.bank[1][:, 0:8]
    with stage(nc, "g_ready", "sums_ready", "copied", "exp_ready", "v") as (block, g_ready, sums_ready, copied, exp_ready, vsem):
        @block.vector
        def _(dve):
            v = Signal(vsem)
            dve.scalar_tensor_tensor(g[:, :, :], raw[:, :, :], -1.0, alog[:, :].unsqueeze(1).broadcast_to([P, 2, 8]),
                                     ALU.mult, ALU.mult).then_inc(g_ready, 1)
            dve.wait_ge(sums_ready, 1)
            v.link(dve, dve.tensor_copy(gc[:, :, :], sums))
            dve.tensor_tensor(kdec[:, 0, :], totals, gc[:, 0, :], ALU.subtract).then_inc(copied, 1)
            dve.wait_ge(exp_ready, 1)
            v.by(dve.tensor_tensor(kbe[:, :, :], beta[:, :, :], egc[:, :, :], ALU.mult))

        @block.tensor
        def _(pe):
            pe.wait_ge(g_ready, 1)
            pe.matmul(totals, kit.c("ones"), g[:, 0, :], start=True, stop=True)
            pe.matmul(sums[:, 0, :], kit.c("tri_f"), g[:, 0, :], start=True, stop=True)
            pe.matmul(sums[:, 1, :], kit.c("tri_f"), g[:, 1, :], start=True, stop=True).then_inc(sums_ready, 1)

        @block.scalar
        def _(act):
            act.wait_ge(copied, 1)
            act.activation(egc[:, :, :], gc[:, :, :], ACT.Exp).then_inc(exp_ready, 1)
            act.activation(kdec[:, 0, :], kdec[:, 0, :], ACT.Exp).then_inc(exp_ready, 1)
    return beta, g, gc, kbe, kdec


def gdn_group(kit, h0, qkv, scal, out):
    nc = kit.nc
    beta, g, gc, kbe, kdec = scal
    qT = lambda h, t: qkv[:, h0 + h, t * P:(t + 1) * P]
    kT = lambda h, t: qkv[:, 8 + h0 + h, t * P:(t + 1) * P]
    q4 = lambda t: qkv[:, h0:h0 + 4, t * P:(t + 1) * P]
    k4 = lambda t: qkv[:, 8 + h0:12 + h0, t * P:(t + 1) * P]
    v1 = lambda h, t: qkv[:, 16 + h0 + h, t * P:(t + 1) * P]
    four = lambda ap: ap.rearrange("p (h n) -> p h n", h=4)
    with ExitStack() as mem:
        new = lambda name, n: mem.enter_context(kit.sb(name, [P, n, 4, P]))
        ktok, vtok = new("k_tok", 2), new("v_tok4", 2)
        at, attn = new("a_t", 2), new("attn_t", 2)
        flat = lambda ap: ap.rearrange("p h n -> p (h n)")
        turn(kit, [([kT(h, t) for h in range(4)], flat(ktok[:, t])) for t in range(2)]
             + [([v1(h, t) for h in range(4)], flat(vtok[:, t])) for t in range(2)])
        with ExitStack() as mem2:
            new2 = lambda name, n: mem2.enter_context(kit.sb(name, [P, n, 4, P]))
            qe = new("q_decayed", 1)
            dec, kb, eg = new2("decay_t", 2), new2("k_beta_t", 2), new2("exp_rows", 1)
            with stage(nc, "rows_ready", "args_ready", "exp_ready", "kb_ready", "products_ready", "v", "qe_sem") as (
                    block, rows_ready, args_ready, exp_ready, kb_ready, products_ready, vsem, qe_sem):
                @block.tensor
                def _(pe):
                    for t in range(2):
                        for h in range(4):
                            pe.matmul(kit.bank[t][:, h * P:(h + 1) * P], g[:, t, h0 + h:h0 + h + 1].broadcast_to([P, P]),
                                      kit.c("tri_f"), start=True, stop=True)
                        for h in range(4):
                            last = pe.matmul(kit.bank[2 + t][:, h * P:(h + 1) * P],
                                             beta[:, t, h0 + h:h0 + h + 1].broadcast_to([P, P]), kit.c("ident"),
                                             start=True, stop=True)
                        last.then_inc(rows_ready, 1)
                    for t in range(2):
                        for h in range(4):
                            pe.matmul(kit.bank[4 + t][:, h * P:(h + 1) * P], kT(h, t), qT(h, t), start=True, stop=True)
                    for t in range(2):
                        pe.wait_ge(kb_ready, t + 1)
                        for h in range(4):
                            last = pe.matmul(kit.bank[6 + t][:, h * P:(h + 1) * P], kT(h, t), kb[:, t, h, :],
                                             start=True, stop=True)
                        last.then_inc(products_ready, 1)

                @block.vector
                def _(dve):
                    v = Signal(vsem)
                    for t in range(2):
                        dve.wait_ge(rows_ready, t + 1)
                        for h in range(4):
                            ins = dve.scalar_tensor_tensor(dec[:, t, h, :], kit.bank[t][:, h * P:(h + 1) * P],
                                                           gc[:, t, h0 + h:h0 + h + 1], kit.c("neg_f"), ALU.subtract, ALU.add)
                            ins.then_inc(args_ready, 1)
                        dve.tensor_tensor(kb[:, t], k4(t), four(kit.bank[2 + t][:, :]), ALU.mult).then_inc(kb_ready, 1)
                        col = (lambda s: s[:, t, h0:h0 + 4].unsqueeze(2).broadcast_to([P, 4, P]))
                        v.by(dve.tensor_tensor(vtok[:, t], vtok[:, t], col(beta), ALU.mult))
                        v.by(dve.tensor_tensor(ktok[:, t], ktok[:, t], col(kdec if t == 0 else kbe), ALU.mult))
                    dve.wait_ge(exp_ready, 2)
                    v.by(dve.tensor_tensor(qe[:, 0], q4(1), eg[:, 0], ALU.mult))
                    dve.wait_ge(exp_ready, 3)
                    for t in range(2):
                        dve.wait_ge(products_ready, t + 1)
                        v.by(dve.tensor_tensor(at[:, t], four(kit.bank[6 + t][:, :]), dec[:, t], ALU.mult))
                        v.by(dve.tensor_tensor(attn[:, t], four(kit.bank[4 + t][:, :]), dec[:, t], ALU.mult))

                @block.scalar
                def _(act):
                    act.wait_ge(args_ready, 4)
                    act.activation(dec[:, 0], dec[:, 0], ACT.Exp).then_inc(exp_ready, 1)
                    act.wait_ge(args_ready, 8)
                    act.activation(eg[:, 0], four(kit.bank[1][:, :]), ACT.Exp).then_inc(exp_ready, 1)
                    act.activation(dec[:, 1], dec[:, 1], ACT.Exp).then_inc(exp_ready, 1)
        e, d, pm, am = new("inverse_t", 2), new("inverse", 2), new("below", 2), new("a_joined", 2)
        bcast = lambda name: kit.c(name).unsqueeze(1).broadcast_to([P, 4, P])
        with stage(nc, "masked", "p_ready", "p_copied", "ed_ready", "e_done", "d_done") as (
                block, masked, p_ready, p_copied, ed_ready, e_done, d_done):
            @block.tensor
            def _(pe):
                def below(level, t):
                    n = 2 * level + t
                    pe.wait_ge(masked, n + 1)
                    if level:
                        pe.wait_ge(p_copied, n - 1)
                        pe.wait_ge(d_done, n - 1)
                    for h in range(4):
                        rhs = d[:, t, h, :] if level else kit.c("ident")
                        last = pe.matmul(kit.bank[t][:, h * P:(h + 1) * P], am[:, t, h, :], rhs, start=True, stop=True)
                    last.then_inc(p_ready, 1)

                below(0, 0)
                below(0, 1)
                for level in range(1, 7):
                    for t in range(2):
                        below(level, t)
                    for t in range(2):
                        n = 2 * level + t
                        pe.wait_ge(p_copied, n + 1)
                        pe.wait_ge(e_done, n - 1)
                        for h in range(4):
                            last = pe.matmul(kit.bank[2 + t][:, h * P:(h + 1) * P], pm[:, t, h, :], e[:, t, h, :],
                                             start=True, stop=True)
                        if level < 6:
                            for h in range(4):
                                last = pe.matmul(kit.bank[4 + t][:, h * P:(h + 1) * P], e[:, t, h, :], pm[:, t, h, :],
                                                 start=True, stop=True)
                        last.then_inc(ed_ready, 1)

            @block.gpsimd
            def _(pool):
                for level in range(7):
                    for t in range(2):
                        n = 2 * level + t
                        if level:
                            pool.wait_ge(p_ready, n - 1)
                            if level == 1:
                                pool.wait_ge(e_done, n - 1)
                        pool.tensor_tensor(am[:, t], at[:, t], bcast(f"join{level}"), ALU.mult).then_inc(masked, 1)

            @block.scalar
            def _(act):
                for level in range(7):
                    for t in range(2):
                        n = 2 * level + t
                        act.wait_ge(p_ready, n + 1)
                        if level >= 2:
                            act.wait_ge(ed_ready, n - 3)
                        act.copy(pm[:, t], four(kit.bank[t][:, :])).then_inc(p_copied, 1)

            @block.vector
            def _(dve):
                for t in range(2):
                    dve.wait_ge(masked, t + 1)
                    dve.tensor_tensor(e[:, t], bcast("ident"), am[:, t], ALU.subtract).then_inc(e_done, 1)
                    dve.wait_ge(p_copied, t + 1)
                    dve.tensor_tensor(d[:, t], bcast("ident"), pm[:, t], ALU.subtract).then_inc(d_done, 1)
                for level in range(1, 7):
                    for t in range(2):
                        n = 2 * level + t
                        dve.wait_ge(ed_ready, n - 1)
                        dve.wait_ge(e_done, n - 1)
                        dve.tensor_tensor(e[:, t], e[:, t], four(kit.bank[2 + t][:, :]), ALU.subtract).then_inc(e_done, 1)
                        if level < 6:
                            dve.wait_ge(d_done, n - 1)
                            dve.tensor_tensor(d[:, t], d[:, t], four(kit.bank[4 + t][:, :]), ALU.subtract).then_inc(d_done, 1)
        vn0, nw, s1, vn1 = pm[:, 0], pm[:, 1], d[:, 0], d[:, 1]
        with stage(nc, "u_ready", "w_ready", "s_ready", "n_ready", "o_ready", "a_copied", "v_copied") as (
                block, u_ready, w_ready, s_ready, n_ready, o_ready, a_copied, v_copied):
            @block.tensor
            def _(pe):
                for h in range(4):
                    last = pe.matmul(kit.bank[0][:, h * P:(h + 1) * P], e[:, 0, h, :], vtok[:, 0, h, :], start=True, stop=True)
                last.then_inc(u_ready, 1)
                for h in range(4):
                    last = pe.matmul(kit.bank[1][:, h * P:(h + 1) * P], ktok[:, 1, h, :], e[:, 1, h, :], start=True, stop=True)
                last.then_inc(w_ready, 1)
                pe.wait_ge(a_copied, 1)
                for h in range(4):
                    last = pe.matmul(kit.bank[2][:, h * P:(h + 1) * P], ktok[:, 0, h, :], vn0[:, h, :], start=True, stop=True)
                last.then_inc(s_ready, 1)
                pe.wait_ge(v_copied, 2)
                for h in range(4):
                    b = kit.bank[3][:, h * P:(h + 1) * P]
                    pe.matmul(b, e[:, 1, h, :], vtok[:, 1, h, :], start=True, stop=False)
                    last = pe.matmul(b, nw[:, h, :], s1[:, h, :], start=False, stop=True)
                last.then_inc(n_ready, 1)
                pe.wait_ge(a_copied, 2)
                for h in range(4):
                    b = kit.bank[4 + h // 2][:, (h % 2) * SEQ:(h % 2) * SEQ + SEQ]
                    pe.matmul(b[:, 0:P], vn0[:, h, :], attn[:, 0, h, :], start=True, stop=True)
                    pe.matmul(b[:, P:SEQ], s1[:, h, :], qe[:, 0, h, :], start=True, stop=False)
                    last = pe.matmul(b[:, P:SEQ], vn1[:, h, :], attn[:, 1, h, :], start=False, stop=True)
                last.then_inc(o_ready, 1)

            @block.scalar
            def _(act):
                act.wait_ge(u_ready, 1)
                act.copy(vn0, four(kit.bank[0][:, :])).then_inc(a_copied, 1)
                act.wait_ge(n_ready, 1)
                act.copy(vn1, four(kit.bank[3][:, :])).then_inc(a_copied, 1)
                act.wait_ge(o_ready, 1)
                act.copy(out[:, h0:h0 + 2, :], kit.bank[4][:, :].rearrange("p (a b) -> p a b", a=2)).then_inc(a_copied, 1)

            @block.vector
            def _(dve):
                dve.wait_ge(w_ready, 1)
                dve.tensor_scalar(nw, four(kit.bank[1][:, :]), -1.0, None, ALU.mult).then_inc(v_copied, 1)
                dve.wait_ge(s_ready, 1)
                dve.tensor_copy(s1, four(kit.bank[2][:, :])).then_inc(v_copied, 1)
                dve.wait_ge(o_ready, 1)
                dve.tensor_copy(out[:, h0 + 2:h0 + 4, :], kit.bank[5][:, :].rearrange("p (a b) -> p a b", a=2)).then_inc(v_copied, 1)


def gated_hidden(kit, x, T, widths, hidden):
    nc = kit.nc
    feed = kit.feed
    done, m = [], 0
    for w in widths:
        m += w // P
        done += [m, m]
    with ExitStack() as mem:
        sg = mem.enter_context(kit.sb("silu_gate", [P, 2, T]))
        with stage(nc, "pair_ready", "silu_ready", "hidden_ready") as (block, pair_ready, silu_ready, hidden_ready):
            @block.sync
            def _(sp):
                feed.run(sp, pair_ready, done)

            @block.tensor
            def _(pe):
                n = 0
                for w in widths:
                    gate = feed.arrive(pe, (DC, w))
                    up = feed.arrive(pe, (DC, w))
                    for m in range(w // P):
                        for which, unit, freed in ((0, gate, silu_ready), (2, up, hidden_ready)):
                            if n >= 2:
                                pe.wait_ge(freed, n - 1)
                            for k in range(DC):
                                last = pe.matmul(kit.bank[which + n % 2][:, 0:T], unit[:, k, m * P:(m + 1) * P], x(k),
                                                 start=k == 0, stop=k == DC - 1)
                        last.then_inc(pair_ready, 1)
                        n += 1

            @block.scalar
            def _(act):
                for n in range(done[-1]):
                    act.wait_ge(pair_ready, n + 1)
                    if n >= 2:
                        act.wait_ge(hidden_ready, n - 1)
                    act.activation(sg[:, n % 2, :], kit.bank[n % 2][:, 0:T], ACT.Silu).then_inc(silu_ready, 1)

            @block.vector
            def _(dve):
                for n in range(done[-1]):
                    dve.wait_ge(silu_ready, n + 1)
                    dve.tensor_tensor(hidden[:, n, :], sg[:, n % 2, :], kit.bank[2 + n % 2][:, 0:T], ALU.mult).then_inc(hidden_ready, 1)


def rows_of(name, ap):
    if len(ap.shape) == 1:
        return ap.rearrange("(r q) -> r q", q=P)
    if len(ap.shape) == 2:
        return ap.rearrange("o (r q) -> (o r) q", q=P)
    return ap.rearrange("o t (r q) -> (o t r) q", q=P)


def load_vectors(kit, inp, const):
    nc = kit.nc
    with ExitStack() as mem:
        rows = mem.enter_context(kit.sb("vector_rows", [P, VTILES, P]))
        with stage(nc, "rows_loaded") as (block, rows_loaded):
            @block.sync
            def _(sp):
                kit.feed.first(sp)

            @block.vector
            def _(dve):
                dve.memset(rows[:, :, :], 0.0).then_inc(rows_loaded, 16)

            @block.scalar
            def _(act):
                act.dma_start(kit.const[:, :], const).then_inc(rows_loaded, 16)
                n = 2
                act.wait_ge(rows_loaded, 32)
                for name, first, count, tile, row in PIECES:
                    src = rows_of(name, inp[name])
                    dst = rows[row:row + count, tile, :]
                    act.dma_start(dst, src[first:first + count]).then_inc(rows_loaded, 16)
                    n += 1
                act.wait_ge(rows_loaded, 16 * n)
        groups = []
        for a in range(0, VTILES, 4):
            b = min(a + 4, VTILES)
            groups.append(([rows[:, t, :] for t in range(a, b)], kit.vec[:, a * P:b * P]))
        turn(kit, groups)


def load_turned(kit, src, out, tiles, name):
    nc = kit.nc
    with ExitStack() as mem:
        raw = mem.enter_context(kit.sb(name + "_tokens", [P, 2, tiles * P]))
        with stage(nc, "loaded") as (block, loaded):
            @block.scalar
            def _(act):
                act.dma_start(raw[:, :, :], src.rearrange("(t p) d -> p t d", p=P)).then_inc(loaded, 16)
                act.wait_ge(loaded, 16)
        turn(kit, [([raw[:, t, (c + j) * P:(c + j + 1) * P] for j in range(2) for t in range(2)], out(c))
                   for c in range(0, tiles, 2)])


def vector_only(kit, program):
    with stage(kit.nc, "v") as (block, vsem):
        @block.vector
        def _(dve):
            program(dve, Signal(vsem))


def first_block(kit, inp, h, mem0):
    nc = kit.nc
    pair = lambda ap: ap.rearrange("p a b -> p (a b)")
    with ExitStack() as mem:
        new = lambda name, tiles: mem.enter_context(kit.sb(name, [P, tiles, SEQ]))
        u, ya = new("u", DC), new("y_a", DC)
        rmsnorm(kit, h, [(slice(0, SEQ), lambda c: u[:, c, :], lambda c: kit.col("ln_pre_mix", c), None, None)])
        ux = lambda k: u[:, k, :]
        with ExitStack() as m2:
            qkv = m2.enter_context(kit.sb("qkv_a", [P, 24, SEQ]))
            project_loop(kit, ux, SEQ, 2, lambda e, i, n, ps: e.tensor_scalar(
                qkv[:, bass.ds(i * 12 + n, 1), :].rearrange("p a b -> p (a b)"), ps, 1.0, None, ALU.mult))
            rope(kit, qkv)
            vt = m2.enter_context(kit.sb("v_tokens", [P, 2, D]))
            turn(kit, [([qkv[:, 16 + c + j, t * P:(t + 1) * P] for j in range(4)], vt[:, t, c * P:(c + 4) * P])
                       for t in range(2) for c in (0, 4)])
            moba(kit, qkv, vt, ya)
        ob = new("o_b", DC)
        with ExitStack() as m2:
            qkv = m2.enter_context(kit.sb("qkv_b", [P, 24, SEQ]))
            project_loop(kit, ux, SEQ, 2, lambda e, i, n, ps: e.tensor_scalar(
                qkv[:, bass.ds(i * 12 + n, 1), :].rearrange("p a b -> p (a b)"), ps, 1.0, None, ALU.mult))

            def spans(tap, out, x):
                back = 3 - tap
                return out[:, back:SEQ], x[:, 0:SEQ - back]

            conv_taps(kit, qkv, 24, (3, 2, 1, 0), lambda tap, c: kit.col("conv_w", tap * 24 + c), spans,
                      lambda act, c, s: act.activation(qkv[:, c, :], s, ACT.Silu))
            head_norm(kit, lambda n: pair(qkv[:, 2 * n:2 * n + 2, :]), 8, 1.0, lambda n: HD ** -0.5 if n < 4 else 1.0)
            w_ba = m2.enter_context(kit.sb("w_ba", [P, DC, 16]))
            bias = m2.enter_context(kit.sb("dt_bias", [P, 8]))
            alog = m2.enter_context(kit.sb("a_log", [P, 8]))
            with stage(nc, "loaded") as (block, loaded):
                @block.scalar
                def _(act):
                    w3 = inp["w_in"][0].rearrange("(k p) n -> p k n", p=P)
                    act.dma_start(w_ba[:, :, :], w3[:, :, 7168:7184]).then_inc(loaded, 16)
                    act.dma_start(bias[:, :], inp["dt_bias"].broadcast_to([P, 8])).then_inc(loaded, 16)
                    act.dma_start(alog[:, :], inp["a_log"].broadcast_to([P, 8])).then_inc(loaded, 16)
                    act.wait_ge(loaded, 48)
            scal = gdn_scalars(kit, u, w_ba, bias, alog, m2)
            for h0 in (0, 4):
                gdn_group(kit, h0, qkv, scal, ob)
        head_norm(kit, lambda n: pair(ob[:, 2 * n:2 * n + 2, :]), 4, 1.0 / HD, lambda n: kit.col("gdn_norm"))
        with ExitStack() as m2:
            zg = m2.enter_context(kit.sb("z_gates", [P, 24, SEQ]))
            project(kit, ux, DC, SEQ, [WIDE] * 12,
                    lambda e, s, n, ps: e.activation(zg[:, n, :], ps, ACT.Silu if n < 8 else ACT.Sigmoid), "scalar")
            vector_only(kit, lambda dve, v: v.by(dve.tensor_tensor(pair(ob[:, :, :]), pair(ob[:, :, :]), pair(zg[:, 0:8, :]), ALU.mult)))
            merged = m2.enter_context(kit.sb("merged", [P, DC, SEQ]))
            tmp = m2.enter_context(kit.sb("gated_b", [P, 2, SEQ]))
            project(kit, lambda k: ya[:, k, :], DC, SEQ, [WIDE] * 4,
                    lambda e, s, n, ps: e.tensor_tensor(merged[:, n, :], ps, zg[:, 8 + n, :], ALU.mult))

            def add_b(e, s, n, ps):
                s.link(e, e.tensor_tensor(tmp[:, n % 2, :], ps, zg[:, 16 + n, :], ALU.mult))
                return e.tensor_tensor(merged[:, n, :], merged[:, n, :], tmp[:, n % 2, :], ALU.add)

            project(kit, lambda k: ob[:, k, :], DC, SEQ, [WIDE] * 4, add_b)
            project(kit, lambda k: merged[:, k, :], DC, SEQ, [WIDE] * 4, lambda e, s, n, ps: e.tensor_copy(ya[:, n, :], ps))
        rmsnorm(kit, ya, [(slice(0, SEQ), lambda c: h[:, c, :], lambda c: kit.col("ln_post_mix", c), None, lambda c: h[:, c, :])])
        rmsnorm(kit, h, [(slice(0, SEQ), lambda c: u[:, c, :], lambda c: kit.col("ln_pre_ffn", c), None, None)])
        with ExitStack() as m2:
            hidden = m2.enter_context(kit.sb("ffn_hidden", [P, FF_TILES, SEQ]))
            gated_hidden(kit, ux, SEQ, [WIDE] * 11, hidden)
            project_down(kit, lambda k: hidden[:, k, :], SEQ, [2] * 11, lambda e, s, m, ps: e.tensor_copy(ya[:, m, :], ps))
        rmsnorm(kit, ya, [(slice(0, SEQ), lambda c: h[:, c, :], lambda c: kit.col("ln_post_ffn", c), None, lambda c: h[:, c, :])])
        with ExitStack() as m2:
            pt = m2.enter_context(kit.sb("p_turned", [P, 2, SEQ]))
            load_turned(kit, inp["p"][0, 0], lambda c: pair(pt[:, c:c + 2, :]), 2, "p")
            project(kit, lambda k: pt[:, k, :], 2, SEQ, [1024], lambda e, s, n, ps: e.tensor_copy(ob[:, n, :], ps))
            rmsnorm(kit, ob, [(slice(0, SEQ), lambda c: ya[:, c, :], lambda c: kit.col("ln_ple", c), None, None)])
            project(kit, lambda k: h[:, k, :], DC, SEQ, [WIDE] * 4,
                    lambda e, s, n, ps: e.activation(u[:, n, :], ps, ACT.Sigmoid), "scalar")

            def add_ple(dve, v):
                v.link(dve, dve.tensor_tensor(pair(u[:, :, :]), pair(u[:, :, :]), pair(ya[:, :, :]), ALU.mult))
                v.by(dve.tensor_tensor(h, h, u[:, :, :], ALU.add))

            vector_only(kit, add_ple)


def plan_first(feed, inp):
    kpn = lambda w: w.rearrange("(k p) n -> p k n", p=P)
    w3 = kpn(inp["w_in"][0])
    wide = lambda w, base=0: (lambda i, j: w[:, :, base + WIDE * j:base + WIDE * (j + 1)])
    rounds = lambda w, base=0: (lambda i, j: w[:, :, bass.ds(i * (WIDE * SLOTS) + (base + WIDE * j), WIDE)])
    feed.plan(2, SLOTS, rounds(w3))
    feed.plan(2, SLOTS, rounds(w3, 3072))
    feed.plan(1, 12, lambda i, j: w3[:, :, 6144 + WIDE * j + (16 if j >= 4 else 0):][:, :, 0:WIDE])
    for name in ("w_proj_a", "w_proj_b", "w_out"):
        feed.plan(1, 4, wide(kpn(inp[name][0])))
    gate, up, down = kpn(inp["w_ffn_gate"][0]), kpn(inp["w_ffn_up"][0]), kpn(inp["w_ffn_down"][0])
    feed.plan(1, 22, lambda i, j: (gate, up)[j % 2][:, :, WIDE * (j // 2):WIDE * (j // 2) + WIDE])
    feed.plan(1, 11, lambda i, j: down[:, 2 * j:2 * j + 2, :])
    feed.plan(1, 1, lambda i, j: kpn(inp["w_ple"][0]))
    feed.plan(1, 4, wide(kpn(inp["w_ple_gate"][0])))


T2 = 2 * SEQ
CTX, LAT = slice(0, SEQ), slice(SEQ, T2)
AB_Z, AB_XBC, AB_DT, AB_V, AB_G, AB_END = 0, 1024, 3072, 3104, 4128, 5152
TAPS = 31
PAD = TAPS // 2
CTX_AT = PAD
LAT_AT = PAD + SEQ + PAD
LINE = LAT_AT + (GRID_W + PAD) * ROWS


def plan_modulation(feed, inp, layer):
    w = inp["mod_w_2"][layer].rearrange("(k p) n -> p k n", p=P)
    feed.plan(4, SLOTS, lambda i, j: w[:, :, bass.ds(i * (WIDE * SLOTS) + WIDE * j, WIDE)])


def expert_unit(inp, layer, e, j):
    w = inp[("moe_w_gate_2", "moe_w_up_2")[j % 2] if j < 4 else "moe_w_down_2"][layer]
    w = w[e] if isinstance(e, int) else w[bass.ds(e, 1)].rearrange("e k n -> (e k) n")
    w = w.rearrange("(k p) n -> p k n", p=P)
    return w[:, :, WIDE * (j // 2):WIDE * (j // 2 + 1)] if j < 4 else w[:, 2 * (j - 4):2 * (j - 4) + 2, :]


def plan_moe(feed, inp, layer):
    feed.plan(1, SLOTS, lambda i, j: expert_unit(inp, layer, 0, j))


def plan_second(feed, inp):
    kpn = lambda w: w.rearrange("(k p) n -> p k n", p=P)
    wide = lambda w, base=0: (lambda i, j: w[:, :, base + WIDE * j:base + WIDE * (j + 1)])
    ab = kpn(inp["ab_w_in_2"][0])
    plan_modulation(feed, inp, 0)
    feed.plan(1, 4, wide(ab, AB_G))
    feed.plan(1, 4, wide(ab, AB_V))
    feed.plan(1, 8, wide(ab, AB_XBC))
    feed.plan(1, 4, wide(ab, AB_Z))
    out = kpn(inp["ab_w_out_2"][0])
    feed.plan(1, 8, lambda i, j: out[:, 2 * j:2 * j + 2, :])
    plan_moe(feed, inp, 0)
    plan_modulation(feed, inp, 1)
    hg = kpn(inp["hg_w_in_2"][0])
    feed.plan(1, 4, wide(hg, 2048))
    feed.plan(1, 8, wide(hg, 0))
    feed.plan(1, 8, wide(hg, 3072))
    feed.plan(1, 4, wide(kpn(inp["hg_w_out_2"][0])))
    plan_moe(feed, inp, 1)


def modulation(kit, cond, mod, layer):
    base = kit.cols("mod_b_2", layer * 48, 48)

    def evacuate(dve, i, n, ps):
        return dve.tensor_scalar(mod[:, bass.ds(i * 12 + n, 1), :].rearrange("p a b -> p (a b)"), ps,
                                 base[:, bass.ds(i * 12 + n, 1)], None, ALU.add)

    project_loop(kit, lambda k: cond[:, k, :], 2, 4, evacuate)


def shifts(kit, mod, scale_at, gain_name, layer, out):
    g = kit.cols(gain_name, layer * 8, 8)

    def program(dve, v):
        for who in range(2):
            v.by(dve.scalar_tensor_tensor(out[:, :, who], mod[:, 8 * scale_at:8 * scale_at + 8, who], 1.0, g, ALU.add, ALU.mult))

    vector_only(kit, program)


def conformer(kit, hn, out):
    nc = kit.nc
    hx = lambda k: hn[:, k, :]
    grid = lambda ap: ap.rearrange("p (r w) -> p r w", w=GRID_W)
    W = LINE - 2 * PAD
    with ExitStack() as mem:
        line = mem.enter_context(kit.sb("conv_line", [P, DC, LINE]))
        ctx_of = lambda t, c, shift=0: t[:, c, CTX_AT - shift:CTX_AT - shift + SEQ]
        rows_of_grid = lambda t, c, shift=0: t[:, c, LAT_AT - shift:LAT_AT - shift + (GRID_W + PAD) * ROWS].rearrange(
            "p (r w) -> p r w", w=GRID_W + PAD)[:, :, 0:GRID_W]
        with ExitStack() as m2:
            sg = m2.enter_context(kit.sb("gate_sigmoid", [P, DC, T2]))
            project(kit, hx, DC, T2, [WIDE] * 4, lambda e, s, n, ps: e.activation(sg[:, n, :], ps, ACT.Sigmoid), "scalar")
            vector_only(kit, lambda dve, v: v.by(dve.memset(line[:, :, :], 0.0)))

            def gate(e, s, n, ps):
                s.by(e.tensor_tensor(ctx_of(line, n), ps[:, CTX], sg[:, n, CTX], ALU.mult))
                return e.tensor_tensor(rows_of_grid(line, n), grid(ps[:, LAT]), grid(sg[:, n, LAT]), ALU.mult)

            project(kit, hx, DC, T2, [WIDE] * 4, gate)
        acc = mem.enter_context(kit.sb("conv31_sum", [P, DC, (GRID_W + PAD) * ROWS + LAT_AT]))
        sums = acc[:, :, 0:W]

        def taps(dve, v):
            for tap in range(TAPS):
                for c in range(DC):
                    x, w = line[:, c, tap:tap + W], kit.col("cf_dw_w_2", tap * 8 + c)
                    if tap == 0:
                        v.by(dve.tensor_scalar(sums[:, c, :], x, w, kit.col("cf_dw_b_2", c), ALU.mult, ALU.add))
                    else:
                        v.by(dve.scalar_tensor_tensor(sums[:, c, :], x, w, sums[:, c, :], ALU.mult, ALU.add))
                v.wait(dve)

        vector_only(kit, taps)
        mean = mem.enter_context(kit.sb("ln_mean", [P, T2]))
        rstd = mem.enter_context(kit.sb("ln_rstd", [P, T2]))
        sq = mem.enter_context(kit.sb("ln_squares", [P, 4, T2]))
        with stage(nc, "summed", "mean_ready", "centred", "squared", "sq_summed", "var_ready", "root_ready", "scaled",
                   "finished", "v") as (block, summed, mean_ready, centred, squared, sq_summed, var_ready, root_ready,
                                        scaled, finished, vsem):
            @block.tensor
            def _(pe):
                for c in range(DC):
                    pe.matmul(kit.bank[0][:, CTX], kit.c("ones"), ctx_of(acc, c, PAD), start=c == 0, stop=c == DC - 1)
                for c in range(DC):
                    last = pe.matmul(kit.bank[0][:, LAT], kit.c("ones"), rows_of_grid(acc, c, PAD), start=c == 0, stop=c == DC - 1)
                last.then_inc(summed, 1)
                for c in range(DC):
                    pe.wait_ge(squared, c + 1)
                    pe.matmul(kit.bank[1][:, :], kit.c("ones"), sq[:, c % 4, :], start=c == 0, stop=c == DC - 1).then_inc(sq_summed, 1)

            @block.vector
            def _(dve):
                v = Signal(vsem)
                dve.wait_ge(summed, 1)
                v.link(dve, dve.tensor_scalar(mean[:, :], kit.bank[0][:, :], 1.0 / D, None, ALU.mult))
                for c in range(DC):
                    v.by(dve.tensor_tensor(out[:, c, CTX], ctx_of(acc, c, PAD), mean[:, CTX], ALU.subtract))
                    dve.tensor_tensor(grid(out[:, c, LAT]), rows_of_grid(acc, c, PAD), grid(mean[:, LAT]), ALU.subtract).then_inc(centred, 1)
                dve.wait_ge(sq_summed, DC)
                dve.tensor_scalar(rstd[:, :], kit.bank[1][:, :], 1.0 / D, EPS, ALU.mult, ALU.add).then_inc(var_ready, 1)
                dve.wait_ge(root_ready, 1)
                v.link(dve, dve.reciprocal(rstd[:, :], rstd[:, :]))
                dve.wait_ge(centred, DC)
                for c in range(DC):
                    dve.scalar_tensor_tensor(out[:, c, :], out[:, c, :], kit.col("cf_ln_g_2", c), rstd[:, :], ALU.mult,
                                             ALU.mult).then_inc(scaled, 1)

            @block.scalar
            def _(act):
                for c in range(DC):
                    act.wait_ge(centred, c + 1)
                    if c >= 4:
                        act.wait_ge(sq_summed, c - 3)
                    act.activation(sq[:, c % 4, :], out[:, c, :], ACT.Square).then_inc(squared, 1)
                act.wait_ge(var_ready, 1)
                act.activation(rstd[:, :], rstd[:, :], ACT.Sqrt).then_inc(root_ready, 1)
                for c in range(DC):
                    act.wait_ge(scaled, c + 1)
                    act.activation(out[:, c, :], out[:, c, :], ACT.Silu, bias=kit.col("cf_ln_b_2", c)).then_inc(finished, 1)


def ssd(kit, inp, hn, out):
    nc = kit.nc
    NT = T2 // P
    with ExitStack() as mem:
        xbc = mem.enter_context(kit.sb("xbc", [P, 16, T2]))
        y = mem.enter_context(kit.sb("y_tokens", [P, NT, D]))
        project(kit, lambda k: hn[:, k, :], DC, T2, [WIDE] * 8, lambda e, s, n, ps: e.tensor_copy(xbc[:, n, :], ps))
        two = lambda ap: ap.rearrange("p (s t) -> p s t", s=2)

        def spans(tap, o, x):
            if tap < 2:
                return two(o)[:, :, 2 - tap:SEQ], two(x)[:, :, 0:SEQ - (2 - tap)]
            return two(o)[:, :, 0:SEQ - (tap - 2)], two(x)[:, :, tap - 2:SEQ]

        conv_taps(kit, xbc, 16, (2, 0, 1, 3, 4), lambda tap, c: kit.col("ssd_conv_w_2", tap * 16 + c), spans,
                  lambda act, c, s: act.activation(xbc[:, c, :], s, ACT.Silu, bias=kit.col("ssd_conv_b_2", c)))
        with ExitStack() as m2:
            new = lambda name, *shape: m2.enter_context(kit.sb(name, [P, *shape]))
            xt, bt = out.rearrange("p c t -> p (c t)").rearrange("p (t d) -> p t d", t=NT), new("b_tokens", NT, 512)
            dt, la, acum, eac, etot, toend = [new(n, NT, 32) for n in ("dt", "log_decay", "a_sum", "a_exp", "a_total_exp", "to_end")]
            turn(kit, [([xbc[:, c + j, t * P:(t + 1) * P] for j in range(4)], xt[:, t, c * P:(c + 4) * P])
                       for t in range(NT) for c in (0, 4)]
                 + [([xbc[:, 8 + j, t * P:(t + 1) * P] for j in range(4)], bt[:, t, :]) for t in range(NT)])
            flat = lambda ap: ap.rearrange("p a b -> p (a b)")
            with ExitStack() as m3:
                w_dt = m3.enter_context(kit.sb("w_dt", [P, DC, 32]))
                bias = m3.enter_context(kit.sb("ssd_dt_bias", [P, 32]))
                alog = m3.enter_context(kit.sb("ssd_a_log", [P, 32]))
                pdt = kit.bank[0][:, 0:NT * 32].rearrange("p (t n) -> p t n", t=NT)
                with stage(nc, "loaded", "dt_ready", "a_ready", "v") as (block, loaded, dt_ready, a_ready, vsem):
                    @block.sync
                    def _(sp):
                        ab = inp["ab_w_in_2"][0].rearrange("(k p) n -> p k n", p=P)
                        sp.dma_start(w_dt[:, :, :], ab[:, :, AB_DT:AB_DT + 32]).then_inc(loaded, 16)
                        sp.dma_start(bias[:, :], inp["ssd_dt_bias_2"].rearrange("o d h -> o (d h)").broadcast_to([P, 32])).then_inc(loaded, 16)
                        sp.dma_start(alog[:, :], inp["ssd_a_log_2"].rearrange("o d h -> o (d h)").broadcast_to([P, 32])).then_inc(loaded, 16)

                    @block.tensor
                    def _(pe):
                        pe.wait_ge(loaded, 48)
                        for t in range(NT):
                            for k in range(DC):
                                last = pe.matmul(pdt[:, t, :], hn[:, k, t * P:(t + 1) * P], w_dt[:, k, :], start=k == 0, stop=k == DC - 1)
                        last.then_inc(dt_ready, 1)

                    @block.scalar
                    def _(act):
                        act.wait_ge(loaded, 48)
                        act.activation(alog[:, :], alog[:, :], ACT.Exp).then_inc(a_ready, 1)

                    @block.vector
                    def _(dve):
                        dve.wait_ge(dt_ready, 1)
                        dve.tensor_tensor(dt[:, :, :], pdt, bias[:, :].unsqueeze(1).broadcast_to([P, NT, 32]), ALU.add).then_inc(vsem, 1)
                softplus(kit, flat(dt[:, :, :]), flat(dt[:, :, :]), NT * 32)
                with stage(nc, "la_ready", "sums_ready", "copied", "finished", "v") as (block, la_ready, sums_ready, copied, finished, vsem):
                    ps = kit.bank[0][:, 0:NT * 32].rearrange("p (t n) -> p t n", t=NT)
                    pt = kit.bank[1][:, 0:NT * 32].rearrange("p (t n) -> p t n", t=NT)

                    @block.vector
                    def _(dve):
                        v = Signal(vsem)
                        dve.scalar_tensor_tensor(la[:, :, :], dt[:, :, :], -1.0, alog[:, :].unsqueeze(1).broadcast_to([P, NT, 32]),
                                                 ALU.mult, ALU.mult).then_inc(la_ready, 1)
                        dve.wait_ge(sums_ready, 1)
                        v.link(dve, dve.tensor_copy(acum[:, :, :], ps))
                        v.by(dve.tensor_copy(etot[:, :, :], pt))
                        dve.tensor_tensor(toend[:, :, :], pt, acum[:, :, :], ALU.subtract).then_inc(copied, 1)
                        dve.wait_ge(finished, 3)
                        v.by(dve.tensor_tensor(toend[:, :, :], toend[:, :, :], dt[:, :, :], ALU.mult))

                    @block.tensor
                    def _(pe):
                        pe.wait_ge(la_ready, 1)
                        pe.matmul(flat(pt), kit.c("ones"), flat(la[:, :, :]), start=True, stop=True)
                        for t in range(NT):
                            pe.matmul(ps[:, t, 0:16], kit.c("tri_f"), la[:, t, 0:16], start=True, stop=True)
                            last = pe.matmul(ps[:, t, 16:32], kit.c("tri_r"), la[:, t, 16:32], start=True, stop=True)
                        last.then_inc(sums_ready, 1)

                    @block.scalar
                    def _(act):
                        act.wait_ge(copied, 1)
                        act.activation(eac[:, :, :], acum[:, :, :], ACT.Exp).then_inc(finished, 1)
                        act.activation(toend[:, :, :], toend[:, :, :], ACT.Exp).then_inc(finished, 1)
                        act.activation(etot[:, :, :], etot[:, :, :], ACT.Exp).then_inc(finished, 1)
            by_head = lambda ap: ap.rearrange("p (h q) -> p h q", q=S_HD)
            spread = lambda ap, n: ap.unsqueeze(2).broadcast_to([P, n, S_HD])
            with ExitStack() as m3:
                xdt = m3.enter_context(kit.sb("x_dt", [P, 2, D]))
                m = m3.enter_context(kit.sb("decay_cb", [P, 2, 2, 4, P]))
                cb = m3.enter_context(kit.sb("c_dot_b", [P, 2, P]))
                with stage(nc, "cb_ready", "cb_copied", "rows_ready", "args_ready", "exp_ready", "m_ready", "xdt_ready",
                           "y_ready", "y_copied") as (block, cb_ready, cb_copied, rows_ready, args_ready, exp_ready,
                                                      m_ready, xdt_ready, y_ready, y_copied):
                    steps = [(t, g) for t in range(NT) for g in range(S_GROUPS)]

                    @block.tensor
                    def _(pe):
                        def prepare(q):
                            t, g = steps[q]
                            if q >= 2:
                                pe.wait_ge(cb_copied, q - 1)
                            pe.matmul(kit.bank[q % 2][:, 0:P], xbc[:, 8 + g, t * P:(t + 1) * P], xbc[:, 12 + g, t * P:(t + 1) * P],
                                      start=True, stop=True).then_inc(cb_ready, 1)
                            for d in range(2):
                                if q >= 2:
                                    pe.wait_ge(args_ready, 2 * (q - 2) + d + 1)
                                for j in range(4):
                                    at = d * 16 + 4 * g + j
                                    last = pe.matmul(kit.bank[2 + 2 * (q % 2) + d][:, j * P:(j + 1) * P],
                                                     la[:, t, at:at + 1].broadcast_to([P, P]), kit.c(("tri_f", "tri_r")[d]),
                                                     start=True, stop=True)
                                last.then_inc(rows_ready, 1)

                        prepare(0)
                        for q, (t, g) in enumerate(steps):
                            if q + 1 < len(steps):
                                prepare(q + 1)
                            pe.wait_ge(xdt_ready, t + 1)
                            pe.wait_ge(m_ready, 2 * q + 2)
                            if q >= 2:
                                pe.wait_ge(y_copied, q - 1)
                            for j in range(4):
                                for d in range(2):
                                    at = (4 * g + j) * S_HD
                                    last = pe.matmul(kit.bank[6 + q % 2][:, j * S_HD:(j + 1) * S_HD], m[:, q % 2, d, j, :],
                                                     xdt[:, d, at:at + S_HD], start=d == 0, stop=d == 1)
                            last.then_inc(y_ready, 1)

                    @block.vector
                    def _(dve):
                        def args(q):
                            t, g = steps[q]
                            for d in range(2):
                                dve.wait_ge(rows_ready, 2 * q + d + 1)
                                if q >= 2:
                                    dve.wait_ge(y_ready, q - 1)
                                for j in range(4):
                                    at = d * 16 + 4 * g + j
                                    ins = dve.scalar_tensor_tensor(m[:, q % 2, d, j, :], kit.bank[2 + 2 * (q % 2) + d][:, j * P:(j + 1) * P],
                                                                   acum[:, t, at:at + 1], kit.c(("neg_f", "neg_r")[d]), ALU.subtract, ALU.add)
                                ins.then_inc(args_ready, 1)

                        args(0)
                        for q, (t, g) in enumerate(steps):
                            if g == 0:
                                if t:
                                    dve.wait_ge(y_ready, q)
                                for d in range(2):
                                    ins = dve.tensor_tensor(by_head(xdt[:, d, :]), by_head(xt[:, t, :]), spread(dt[:, t, 16 * d:16 * d + 16], 16), ALU.mult)
                                ins.then_inc(xdt_ready, 1)
                            if q + 1 < len(steps):
                                args(q + 1)
                            dve.wait_ge(cb_copied, q + 1)
                            for d in range(2):
                                dve.wait_ge(exp_ready, 2 * q + d + 1)
                                dve.tensor_tensor(m[:, q % 2, d], m[:, q % 2, d], cb[:, q % 2, :].unsqueeze(1).broadcast_to([P, 4, P]),
                                                  ALU.mult).then_inc(m_ready, 1)

                    @block.scalar
                    def _(act):
                        def exps(q):
                            act.wait_ge(cb_ready, q + 1)
                            if q >= 2:
                                act.wait_ge(m_ready, 2 * (q - 2) + 2)
                            act.copy(cb[:, q % 2, :], kit.bank[q % 2][:, 0:P]).then_inc(cb_copied, 1)
                            for d in range(2):
                                act.wait_ge(args_ready, 2 * q + d + 1)
                                act.activation(m[:, q % 2, d], m[:, q % 2, d], ACT.Exp).then_inc(exp_ready, 1)

                        exps(0)
                        for q, (t, g) in enumerate(steps):
                            if q + 1 < len(steps):
                                exps(q + 1)
                            act.wait_ge(y_ready, q + 1)
                            act.copy(y[:, t, g * 256:(g + 1) * 256], kit.bank[6 + q % 2][:, 0:256]).then_inc(y_copied, 1)
            with ExitStack() as m3:
                state = m3.enter_context(kit.sb("ssd_state", [P, 2, D]))
                xe = m3.enter_context(kit.sb("x_to_end", [P, 2, D]))
                tmp = m3.enter_context(kit.sb("y_from_state", [P, 512]))
                order = [(d, k, ((0, 1, 2, 3), (1, 0, 3, 2))[d][k]) for k in range(NT) for d in range(2)]
                with stage(nc, "xe_ready", "s_ready", "off_ready", "state_ready", "v", "y_added") as (
                        block, xe_ready, s_ready, off_ready, state_ready, vsem, y_added):
                    @block.tensor
                    def _(pe):
                        for n, (d, k, t) in enumerate(order):
                            if k < NT - 1:
                                pe.wait_ge(xe_ready, n + 1)
                                if n >= 2:
                                    pe.wait_ge(state_ready, n - 1)
                                for g in range(S_GROUPS):
                                    last = pe.matmul(kit.bank[2 * (n % 2) + g // 2][:, (g % 2) * 256:(g % 2) * 256 + 256],
                                                     bt[:, t, g * P:(g + 1) * P], xe[:, d, g * 256:(g + 1) * 256], start=True, stop=True)
                                last.then_inc(s_ready, 1)
                            if k:
                                pe.wait_ge(state_ready, n - 1)
                                if n >= 4:
                                    pe.wait_ge(y_added, n - 3)
                                for g in range(S_GROUPS):
                                    last = pe.matmul(kit.bank[4 + 2 * (n % 2) + g // 2][:, (g % 2) * 256:(g % 2) * 256 + 256],
                                                     xbc[:, 12 + g, t * P:(t + 1) * P], state[:, d, g * 256:(g + 1) * 256], start=True, stop=True)
                                last.then_inc(off_ready, 1)

                    @block.vector
                    def _(dve):
                        v = Signal(vsem)
                        for n, (d, k, t) in enumerate(order):
                            if k < NT - 1:
                                if n >= 2:
                                    dve.wait_ge(s_ready, n - 1)
                                dve.tensor_tensor(by_head(xe[:, d, :]), by_head(xt[:, t, :]), spread(toend[:, t, 16 * d:16 * d + 16], 16),
                                                  ALU.mult).then_inc(xe_ready, 1)
                            if k:
                                dve.wait_ge(off_ready, n - 1)
                                for b in range(2):
                                    v.link(dve, dve.tensor_tensor(by_head(tmp[:, :]), by_head(kit.bank[4 + 2 * (n % 2) + b][:, :]),
                                                                  spread(eac[:, t, 16 * d + 8 * b:16 * d + 8 * b + 8], 8), ALU.mult))
                                    half = y[:, t, b * 512:(b + 1) * 512]
                                    added = dve.tensor_tensor(half, half, tmp[:, :], ALU.add)
                                    if b == 0:
                                        v.link(dve, added)
                                added.then_inc(y_added, 1)
                                dve.wait_ge(y_added, n - 1)
                            if k < NT - 1:
                                dve.wait_ge(s_ready, n + 1)
                                if k:
                                    v.link(dve, dve.tensor_tensor(by_head(state[:, d, :]), by_head(state[:, d, :]),
                                                                  spread(etot[:, t, 16 * d:16 * d + 16], 16), ALU.mult))
                                for b in range(2):
                                    s, ps = state[:, d, b * 512:(b + 1) * 512], kit.bank[2 * (n % 2) + b][:, :]
                                    last = dve.tensor_tensor(s, s, ps, ALU.add) if k else dve.tensor_copy(s, ps)
                                    if b == 0:
                                        v.by(last)
                                last.then_inc(state_ready, 1)
                                v.wait(dve)
                                dve.wait_ge(state_ready, n + 1)
        turn(kit, [([y[:, t, c * P:(c + 1) * P] for t in range(NT)], out[:, c, :]) for c in range(DC)])
        z = mem.enter_context(kit.sb("z_silu", [P, DC, T2]))
        project(kit, lambda k: hn[:, k, :], DC, T2, [WIDE] * 4, lambda e, s, n, ps: e.activation(z[:, n, :], ps, ACT.Silu), "scalar")

        def skip_and_gate(dve, v):
            for c in range(DC):
                v.by(dve.scalar_tensor_tensor(out[:, c, :], xbc[:, c, :], kit.col("ssd_d_2", c), out[:, c, :], ALU.mult, ALU.add))
            v.wait(dve)
            for c in range(DC):
                v.by(dve.tensor_tensor(out[:, c, :], out[:, c, :], z[:, c, :], ALU.mult))

        vector_only(kit, skip_and_gate)
    rmsnorm(kit, out, [(slice(0, T2), lambda c: out[:, c, :], lambda c: kit.col("ssd_norm_g_2", c), None, None)])


def route(kit, inp, hn, T, combine, lists, table):
    nc = kit.nc
    NT = T // P
    with ExitStack() as mem:
        new = lambda name, *shape: mem.enter_context(kit.sb(name, [P, *shape]))
        rw, rb = new("router_w", DC, EXPERTS), new("router_b", EXPERTS)
        score, sel, pick = new("scores", NT, 16), new("selection", NT * 4, 4), new("pick", NT * 4, 4)
        gt, ge = new("greater", NT * 4, 4, 4), new("greater_equal", NT * 4, 4, 4)
        gs, gp, den = new("group_score", NT * 4), new("group_pick", NT * 4), new("weight_sum", NT)
        ct = new("combine_t", T)
        chosen, weights, places = [new(n, NT, 16) for n in ("chosen", "weights", "places")]
        need, upto, start, first = [new(n, 16) for n in ("items_needed", "items_up_to", "items_before", "total_tokens")]
        member, part = new("item_of_expert", ITEMS, 16), new("item_products", NT, ITEMS, 16)
        skipped, which = new("skipped_tokens", ITEMS), new("item_expert", ITEMS)
        flat = lambda ap: ap.rearrange("p a b -> p (a b)")
        ps = kit.bank[0][:, 0:NT * 16].rearrange("p (t n) -> p t n", t=NT)

        def ranks(dve, v, s, G, rank):
            other, own = s.unsqueeze(2).broadcast_to([P, G, 4, 4]), s.unsqueeze(3).broadcast_to([P, G, 4, 4])
            table = lambda name: kit.c(name).rearrange("p (i j) -> p i j", i=4).unsqueeze(1).broadcast_to([P, G, 4, 4])
            v.by(dve.tensor_tensor(gt[:, 0:G], other, own, ALU.is_gt))
            v.by(dve.tensor_tensor(ge[:, 0:G], other, own, ALU.is_ge))
            v.wait(dve)
            v.by(dve.tensor_tensor(gt[:, 0:G], gt[:, 0:G], table("notbefore"), ALU.mult))
            v.by(dve.tensor_tensor(ge[:, 0:G], ge[:, 0:G], table("before"), ALU.mult))
            v.wait(dve)
            v.link(dve, dve.tensor_tensor(gt[:, 0:G], gt[:, 0:G], ge[:, 0:G], ALU.add))
            v.link(dve, dve.tensor_reduce(rank, gt[:, 0:G], AX.X, ALU.add))

        with stage(nc, "loaded", "scored", "sigmoid_ready", "v") as (block, loaded, scored, sigmoid_ready, vsem):
            @block.sync
            def _(sp):
                sp.dma_start(rw[:, :, :], inp["router_w_2"].rearrange("(k p) n -> p k n", p=P)).then_inc(loaded, 16)
                sp.dma_start(rb[:, :], inp["router_b_2"].rearrange("(o n) -> o n", o=1).broadcast_to([P, EXPERTS])).then_inc(loaded, 16)

            @block.tensor
            def _(pe):
                pe.wait_ge(loaded, 32)
                for t in range(NT):
                    for k in range(DC):
                        last = pe.matmul(ps[:, t, :], hn[:, k, t * P:(t + 1) * P], rw[:, k, :], start=k == 0, stop=k == DC - 1)
                last.then_inc(scored, 1)

            @block.scalar
            def _(act):
                act.wait_ge(scored, 1)
                act.activation(score[:, :, :], ps, ACT.Sigmoid).then_inc(sigmoid_ready, 1)

            @block.vector
            def _(dve):
                v = Signal(vsem)
                dve.wait_ge(sigmoid_ready, 1)
                dve.wait_ge(loaded, 32)
                v.link(dve, dve.tensor_tensor(sel[:, :, :].rearrange("p (t g) i -> p t (g i)", t=NT), score[:, :, :],
                                              rb[:, :].unsqueeze(1).broadcast_to([P, NT, 16]), ALU.add))
                ranks(dve, v, sel[:, :, :], NT * 4, pick[:, :, :])
                v.link(dve, dve.tensor_scalar(flat(pick[:, :, :]), flat(pick[:, :, :]), 1.5, None, ALU.is_lt))
                v.link(dve, dve.tensor_tensor(sel[:, :, :], sel[:, :, :], pick[:, :, :], ALU.mult))
                v.link(dve, dve.tensor_reduce(gs[:, :], sel[:, :, :], AX.X, ALU.add))
                ranks(dve, v, gs[:, :].rearrange("p (t g) -> p t g", t=NT), NT, gp[:, :].rearrange("p (t g) -> p t g", t=NT))
                v.link(dve, dve.tensor_scalar(gp[:, :], gp[:, :], 0.5, None, ALU.is_lt))
                v.link(dve, dve.tensor_tensor(pick[:, :, :], pick[:, :, :], gp[:, :].unsqueeze(2).broadcast_to([P, NT * 4, 4]), ALU.mult))
                v.link(dve, dve.tensor_tensor(score[:, :, :], score[:, :, :], pick[:, :, :].rearrange("p (t g) i -> p t (g i)", t=NT), ALU.mult))
                v.link(dve, dve.tensor_reduce(den[:, :], score[:, :, :], AX.X, ALU.add))
                v.link(dve, dve.reciprocal(den[:, :], den[:, :]))
                v.by(dve.tensor_copy(chosen[:, :, :], pick[:, :, :].rearrange("p (t g) i -> p t (g i)", t=NT)))
                v.by(dve.tensor_tensor(weights[:, :, :], score[:, :, :], den[:, :].unsqueeze(2).broadcast_to([P, NT, 16]), ALU.mult))
        with stage(nc, "counted", "v") as (block, counted, vsem):
            before = kit.bank[0][:, 0:NT * 16].rearrange("p (t n) -> p t n", t=NT)
            total = kit.bank[1][:, 0:16]

            @block.tensor
            def _(pe):
                for t in range(NT):
                    for s in range(t + 1):
                        pe.matmul(before[:, t, :], kit.c("ones") if s < t else kit.c("tri_f"), chosen[:, s, :], start=s == 0, stop=s == t)
                for t in range(NT):
                    last = pe.matmul(total, kit.c("ones"), chosen[:, t, :], start=t == 0, stop=t == NT - 1)
                last.then_inc(counted, 1)

            @block.vector
            def _(dve):
                v = Signal(vsem)
                dve.wait_ge(counted, 1)
                v.by(dve.tensor_tensor(places[:, :, :], before, chosen[:, :, :], ALU.mult))
                v.link(dve, dve.tensor_copy(first[:, :], total))
                v.by(dve.tensor_scalar(flat(places[:, :, :]), flat(places[:, :, :]), 1.0, None, ALU.subtract))
                v.link(dve, dve.memset(need[:, :], 1.0))
                for full in range(1, NT):
                    v.link(dve, dve.scalar_tensor_tensor(need[:, :], first[:, :], P * full + 0.5, need[:, :], ALU.is_gt, ALU.add))
                v.link(dve, dve.tensor_tensor_scan(upto[:, :], kit.c("ones")[:, 0:16], need[:, :], 0.0, ALU.mult, ALU.add))
                v.link(dve, dve.tensor_tensor(start[:, :], upto[:, :], need[:, :], ALU.subtract))
                number = kit.c("count")[:, 0:ITEMS]
                numbers = number.unsqueeze(2).broadcast_to([P, ITEMS, 16])
                along = lambda ap: ap.unsqueeze(1).broadcast_to([P, ITEMS, 16])
                v.by(dve.tensor_tensor(member[:, :, :], numbers, along(start[:, :]), ALU.is_ge))
                v.link(dve, dve.tensor_tensor(part[:, 0], numbers, along(upto[:, :]), ALU.is_lt))
                v.link(dve, dve.tensor_tensor(member[:, :, :], member[:, :, :], part[:, 0], ALU.mult))
                v.by(dve.tensor_tensor(part[:, 0], member[:, :, :], along(kit.c("count")[:, 0:16]), ALU.mult))
                v.link(dve, dve.tensor_tensor(part[:, 1], member[:, :, :], along(start[:, :]), ALU.mult))
                v.by(dve.tensor_reduce(which[:, :], part[:, 0], AX.X, ALU.add))
                v.link(dve, dve.tensor_reduce(skipped[:, :], part[:, 1], AX.X, ALU.add))
                v.by(dve.tensor_copy(table[:, 0:ITEMS], which[:, :]))
                v.by(dve.tensor_scalar(table[:, ITEMS:ITEMS + 1], upto[:, 15:16], 1.0, None, ALU.subtract))
                v.link(dve, dve.tensor_tensor(skipped[:, :], number, skipped[:, :], ALU.subtract))
                v.link(dve, dve.tensor_scalar(skipped[:, :], skipped[:, :], float(P), None, ALU.mult))
                for w, of_expert in enumerate((weights, places)):
                    for t in range(NT):
                        v.by(dve.tensor_tensor(part[:, t], member[:, :, :], along(of_expert[:, t, :]), ALU.mult))
                    v.wait(dve)
                    v.link(dve, dve.tensor_reduce(lists[:, :, w, :], part[:, :], AX.X, ALU.add))
                v.by(dve.tensor_tensor(lists[:, :, 1, :], lists[:, :, 1, :], skipped[:, :].unsqueeze(1).broadcast_to([P, NT, ITEMS]),
                                       ALU.subtract))
        turn(kit, [([lists[:, t].rearrange("p w i -> p (w i)") for t in range(NT)], ct[0:2 * ITEMS, :])])
        with stage(nc, "stored") as (block, stored):
            @block.scalar
            def _(act):
                act.dma_start(combine.rearrange("w i t -> (w i) t"), ct[0:2 * ITEMS, :]).then_inc(stored, 16)
                act.wait_ge(stored, 16)


def experts(kit, hn, T, combine, lists, table, add, inp, layer):
    nc = kit.nc
    feed = kit.feed
    NT, M = T // P, 4
    PER = DC + 4 + 1 + 2
    DONE = [1 + DC + n for n in (1, 2, 3, 4, 6, 7)]
    most = EXPERTS + CHOICES * NT - 1
    assert most < ITEMS
    with ExitStack() as mem:
        new = lambda name, *shape: mem.enter_context(kit.sb(name, [P, *shape]))
        tokens = new("moe_tokens", NT, D)
        rows = new("weight_and_place_rows", 2, T)
        pick, spread = new("gather_one_hot", NT, P), new("scatter_weights", T)
        xg, sg, hidden, y = new("gathered", DC, P), new("silu_gate", 512), new("expert_hidden", M, P), new("expert_out", D)
        turn(kit, [([hn[:, c + j, t * P:(t + 1) * P] for j in range(4)], tokens[:, t, c * P:(c + 4) * P])
                   for t in range(NT) for c in (0, 4)])
        last_item = lambda engine: engine.value_load(table[0:1, ITEMS:ITEMS + 1], min_val=EXPERTS - 1, max_val=most - 1)
        with stage(nc, "products", "pick_ready", "gathered", "silu_ready", "hidden_ready", "y_copied", "spread_ready",
                   "added", "rows_loaded", *[f"unit_loaded{j}" for j in range(SLOTS)]) as (
                block, products, pick_ready, gathered, silu_ready, hidden_ready, y_copied, spread_ready, added, rows_loaded,
                *unit_loaded):
            slot = [(feed.taken + j) % SLOTS for j in range(SLOTS)]

            @block.sync
            def _(sp):
                def rows_of(i):
                    row = combine[:, i:i + 1, :] if isinstance(i, int) else combine[:, bass.ds(i, 1), :]
                    sp.dma_start(rows[:, :, :], row.rearrange("w i t -> i w t").broadcast_to([P, 2, T])).then_inc(rows_loaded, 16)

                last_of_all = last_item(sp)
                rows_of(0)
                with sp.Fori(0, last_of_all) as i:
                    e = sp.value_load(table[0:1, bass.ds(i + 1, 1)], min_val=0, max_val=EXPERTS - 1)
                    sp.wait_ge(spread_ready, i + 2)
                    rows_of(i + 1)
                    for j in range(SLOTS):
                        src = expert_unit(inp, layer, e, j)
                        sp.wait_ge(products, i * PER + DONE[j])
                        dst = feed.buf[:, slot[j], :].rearrange("p (k n) -> p k n", k=src.shape[1])
                        sp.dma_start(dst, src).then_inc(unit_loaded[j], 16)
                feed.run_ahead(sp, SLOTS, lambda j: sp.wait_ge(products, last_of_all * PER + DONE[j]))

            def gather(pe):
                for c in range(DC):
                    for t in range(NT):
                        last = pe.matmul(kit.bank[2 + c // 4][:, (c % 4) * P:(c % 4 + 1) * P], tokens[:, t, c * P:(c + 1) * P],
                                         pick[:, t, :], start=t == 0, stop=t == NT - 1)
                last.then_inc(products, 1)

            def scatter(pe, i):
                pe.wait_ge(spread_ready, i + 1)
                pe.wait_ge(y_copied, i * 2 + 2)
                for m in range(DC):
                    pe.wait_ge(added, i * DC + m + 1)
                    pe.matmul(kit.bank[6 + m % 2][:, 0:T], y[:, m * P:(m + 1) * P], spread[:, :], start=True, stop=True).then_inc(products, 1)

            @block.tensor
            def _(pe):
                n = last_item(pe) + 1
                pe.wait_ge(pick_ready, 1)
                gather(pe)
                for j in range(SLOTS):
                    feed.arrive(pe, (SLOT, 1))
                    pe.sem_inc(unit_loaded[j], 16)
                with pe.Fori(0, n) as i:
                    scatter(pe, i)
                    pe.wait_ge(gathered, i * 2 + 2)
                    for j in range(4):
                        unit = feed.buf[:, slot[j], :].rearrange("p (k n) -> p k n", k=DC)
                        pe.wait_ge(unit_loaded[j], i * 16 + 16)
                        for half in range(2):
                            at = (2 * (j // 2) + half) * P
                            for k in range(DC):
                                last = pe.matmul(kit.bank[j % 2][:, at:at + P], unit[:, k, half * P:(half + 1) * P], xg[:, k, :],
                                                 start=k == 0, stop=k == DC - 1)
                        last.then_inc(products, 1)
                    pe.wait_ge(pick_ready, i + 2)
                    gather(pe)
                    pe.wait_ge(hidden_ready, i + 1)
                    for j in range(2):
                        unit = feed.buf[:, slot[4 + j], :].rearrange("p (k n) -> p k n", k=2)
                        pe.wait_ge(unit_loaded[4 + j], i * 16 + 16)
                        for half in range(2):
                            for k in range(2):
                                last = pe.matmul(kit.bank[4 + half][:, :], hidden[:, 2 * j + k, :], unit[:, k, half * 512:(half + 1) * 512],
                                                 start=j == 0 and k == 0, stop=j == 1 and k == 1)
                        last.then_inc(products, 1)
                scatter(pe, n)

            @block.scalar
            def _(act):
                def copy_gathered(signal):
                    act.wait_ge(products, signal)
                    for b in range(2):
                        act.copy(xg[:, 4 * b:4 * b + 4, :], kit.bank[2 + b][:, :].rearrange("p (a b) -> p a b", a=4)).then_inc(gathered, 1)

                n = last_item(act) + 1
                copy_gathered(1)
                with act.Fori(0, n) as i:
                    act.wait_ge(products, i * PER + 1 + DC + 3)
                    act.activation(sg[:, :], kit.bank[0][:, :], ACT.Silu).then_inc(silu_ready, 1)
                    copy_gathered(i * PER + 1 + DC + 5)
                    act.wait_ge(products, i * PER + 1 + PER)
                    for b in range(2):
                        act.copy(y[:, b * 512:(b + 1) * 512], kit.bank[4 + b][:, :]).then_inc(y_copied, 1)

            @block.vector
            def _(dve):
                def choose(i):
                    for t in range(NT):
                        at = lists[:, t, 1, i:i + 1] if isinstance(i, int) else lists[:, t, 1, bass.ds(i, 1)]
                        ins = dve.tensor_scalar(pick[:, t, :], kit.c("count"), at, None, ALU.is_equal)
                    ins.then_inc(pick_ready, 1)

                def add_scattered(i):
                    for m in range(DC):
                        dve.wait_ge(products, i * PER + m + 2)
                        add(dve, m, kit.bank[6 + m % 2][:, 0:T]).then_inc(added, 1)

                n = last_item(dve) + 1
                dve.memset(spread[:, :], 0.0).then_inc(spread_ready, 1)
                dve.memset(y[:, 0:512], 0.0).then_inc(y_copied, 1)
                dve.memset(y[:, 512:1024], 0.0).then_inc(y_copied, 1)
                dve.sem_inc(added, 2)
                choose(0)
                with dve.Fori(0, n) as i:
                    add_scattered(i)
                    dve.wait_ge(rows_loaded, i * 16 + 16)
                    dve.scalar_tensor_tensor(spread[:, :], rows[:, 1, :], kit.c("slot"), rows[:, 0, :], ALU.is_equal,
                                             ALU.mult).then_inc(spread_ready, 1)
                    dve.wait_ge(gathered, i * 2 + 2)
                    choose(i + 1)
                    dve.wait_ge(silu_ready, i + 1)
                    dve.wait_ge(products, i * PER + 1 + DC + 4)
                    dve.tensor_tensor(hidden[:, :, :].rearrange("p a b -> p (a b)"), sg[:, :], kit.bank[1][:, :], ALU.mult).then_inc(hidden_ready, 1)
                add_scattered(n)


def hgrn2(kit, x2, hn, out):
    nc = kit.nc
    C = 64
    NCH = SEQ // C
    with ExitStack() as mem:
        new = lambda name, *shape: mem.enter_context(kit.sb(name, [P, *shape]))
        vt = new("v_tokens", 4, D)
        with ExitStack() as m2:
            vf = m2.enter_context(kit.sb("v_features", [P, DC, T2]))
            project(kit, lambda k: hn[:, k, :], DC, T2, [WIDE] * 4, lambda e, s, n, ps: e.tensor_copy(vf[:, n, :], ps))
            turn(kit, [([vf[:, c + j, t * P:(t + 1) * P] for j in range(4)], vt[:, t, c * P:(c + 4) * P])
                       for t in range(4) for c in (0, 4)])
        qg = new("q_and_gate", 16, SEQ)
        project(kit, lambda k: hn[:, k, LAT], DC, SEQ, [WIDE] * 8, lambda e, s, n, ps: e.activation(qg[:, n, :], ps, ACT.Silu), "scalar")
        inner = mem.enter_context(ExitStack())
        new = lambda name, *shape: inner.enter_context(kit.sb(name, [P, *shape]))
        f = new("forget", 16, T2)
        project(kit, lambda k: hn[:, k, :], DC, T2, [WIDE] * 8, lambda e, s, n, ps: e.activation(f[:, n, :], ps, ACT.Sigmoid), "scalar")
        lb, omlb, hi, e0, e1 = [new(n, DC) for n in ("lower", "one_less_lower", "lb_max", "lb_e0", "lb_e1")]
        with stage(nc, "shifted", "exp_ready", "v") as (block, shifted, exp_ready, vsem):
            @block.vector
            def _(dve):
                v = Signal(vsem)
                r0, r1 = kit.cols("hg_lb_2", 0, 8), kit.cols("hg_lb_2", 8, 8)
                v.link(dve, dve.tensor_tensor(hi[:, :], r0, r1, ALU.max))
                dve.tensor_tensor(e0[:, :], r0, hi[:, :], ALU.subtract).then_inc(shifted, 1)
                dve.tensor_tensor(e1[:, :], r1, hi[:, :], ALU.subtract).then_inc(shifted, 1)
                dve.wait_ge(exp_ready, 2)
                v.link(dve, dve.tensor_tensor(hi[:, :], e0[:, :], e1[:, :], ALU.add))
                v.link(dve, dve.reciprocal(hi[:, :], hi[:, :]))
                v.link(dve, dve.tensor_tensor(e0[:, :], e0[:, :], hi[:, :], ALU.mult))
                v.link(dve, dve.tensor_tensor(e1[:, :], e1[:, :], hi[:, :], ALU.mult))
                v.link(dve, dve.tensor_tensor(lb[:, :], e0[:, :], e1[:, :], ALU.add))
                v.link(dve, dve.tensor_tensor(lb[:, :], lb[:, :], e0[:, :], ALU.subtract))
                v.by(dve.tensor_scalar(omlb[:, :], lb[:, :], -1.0, 1.0, ALU.mult, ALU.add))

            @block.scalar
            def _(act):
                act.wait_ge(shifted, 2)
                act.activation(e0[:, :], e0[:, :], ACT.Exp).then_inc(exp_ready, 1)
                act.activation(e1[:, :], e1[:, :], ACT.Exp).then_inc(exp_ready, 1)
        lf = new("log_forget", 2, T2)
        ex = new("exps", 2, 3, SEQ)
        rel = ex[:, :, 0, :]
        end = new("end_less_sum", 2, T2)
        ge = new("chunk_decay", 2, 2, NCH)
        qk = new("q_rel_k_rel_q_in", 2, 3, SEQ)
        kend = new("k_end", 2, T2)
        kt = new("k_end_tokens", 2, 6, P)
        st = new("states", 2, NCH, P)
        att = new("att_t", 2, 2, P)
        chunks = lambda ap: ap.rearrange("p (c t) -> p c t", c=NCH)
        with stage(nc, "f_ready", "log_ready", "rel_ready", "exp_ready", "prod_ready", "kt_ready", "kt_copied",
                   "ctx_state", "adds_ready", "att_ready", "states_ready", "o_ready", "o_copied", "zeroed", "v") as (
                block, f_ready, log_ready, rel_ready, exp_ready, prod_ready, kt_ready, kt_copied, ctx_state, adds_ready,
                att_ready, states_ready, o_ready, o_copied, zeroed, vsem):
            order = ((0, 1, 2, 3), (3, 2, 1, 0))
            mid, last_of = (C // 2 - 1, C // 2), (C - 1, 0)
            keep = lambda d, lo: kit.c(("keep_f", "keep_r")[d])

            @block.vector
            def _(dve):
                v = Signal(vsem)
                v.by(dve.memset(att[:, :, :, :], 0.0))
                dve.memset(kt[:, :, :, :], 0.0).then_inc(zeroed, 1)

                def gates(n):
                    h, d = n // 2, n % 2
                    ff = f[:, 8 * d + h, :]
                    v.link(dve, dve.tensor_scalar(ff, ff, omlb[:, h:h + 1], lb[:, h:h + 1], ALU.mult, ALU.add))
                    if n >= 2:
                        dve.wait_ge(exp_ready, 5 * (n - 1))
                        dve.wait_ge(prod_ready, n - 1)
                    dve.nop().then_inc(f_ready, 1)

                def sums(n):
                    h, d = n // 2, n % 2
                    ff, s = f[:, 8 * d + h, :], lf[:, n % 2, :]
                    dve.wait_ge(log_ready, n + 1)
                    carry = kit.c(("carry_f", "carry_r")[d])
                    v.by(dve.tensor_scalar(ff, ff, -1.0, 1.0, ALU.mult, ALU.add))
                    if d == 0:
                        v.by(dve.tensor_tensor_scan(s, carry, s, 0.0, ALU.mult, ALU.add))
                    else:
                        v.by(dve.tensor_tensor_scan(s[:, ::-1], carry[:, ::-1], s[:, ::-1], 0.0, ALU.mult, ALU.add))
                    v.wait(dve)
                    g = chunks(s[:, LAT])
                    at = lambda j: g[:, :, j:j + 1].broadcast_to([P, NCH, C])
                    v.by(dve.tensor_tensor(chunks(rel[:, n % 2, :]), g, at(mid[d]), ALU.subtract))
                    v.by(dve.tensor_tensor(chunks(end[:, n % 2, LAT]), at(last_of[d]), g, ALU.subtract))
                    v.by(dve.tensor_copy(ge[:, n % 2, 0, :], g[:, :, last_of[d]]))
                    j = (SEQ - 1, 0)[d]
                    v.by(dve.tensor_scalar(end[:, n % 2, CTX], s[:, CTX], -1.0, s[:, j:j + 1], ALU.mult, ALU.add))
                    v.wait(dve)
                    dve.nop().then_inc(rel_ready, 1)

                def prods(n):
                    h, d = n // 2, n % 2
                    k = f[:, 8 * d + h, :]
                    dve.wait_ge(exp_ready, 5 * (n + 1))
                    if n >= 2:
                        dve.wait_ge(o_ready, (n - 2) // 2 + 1)
                    v.by(dve.tensor_tensor(kend[:, n % 2, :], k, end[:, n % 2, :], ALU.mult))
                    v.by(dve.tensor_tensor(qk[:, n % 2, 0, :], qg[:, h, :], ex[:, n % 2, 0, :], ALU.mult))
                    v.by(dve.tensor_tensor(qk[:, n % 2, 1, :], k[:, LAT], ex[:, n % 2, 1, :], ALU.mult))
                    v.by(dve.tensor_tensor(qk[:, n % 2, 2, :], qg[:, h, :], ex[:, n % 2, 2, :], ALU.mult))
                    v.wait(dve)
                    dve.nop().then_inc(prod_ready, 1)

                def masks_states(n):
                    h, d = n // 2, n % 2
                    dve.wait_ge(att_ready, n + 1)
                    mask = kit.c(("keep_f", "keep_r")[d]).bitcast(I32)
                    for lo in (0, C):
                        v.by(dve.copy_predicated(att[lo:lo + C, d, :, lo:lo + C], mask[lo:lo + C].unsqueeze(1).broadcast_to([C, 2, C]),
                                                 kit.bank[2 + d][lo:lo + C, 0:2 * C].rearrange("p (a b) -> p a b", a=2)))
                    dve.wait_ge(adds_ready, n + 1)
                    b = kit.bank[4 + d]
                    v.link(dve, dve.tensor_copy(st[:, d, order[d][0], :], b[:, 0:P]))
                    for i in range(NCH - 1):
                        a, z = order[d][i], order[d][i + 1]
                        v.link(dve, dve.scalar_tensor_tensor(st[:, d, z, :], st[:, d, a, :], ge[:, n % 2, 1, a:a + 1],
                                                             b[:, (i + 1) * P:(i + 2) * P], ALU.mult, ALU.add))
                    dve.nop().then_inc(states_ready, 1)

                U = 2 * HEADS
                gates(0)
                sums(0)
                for n in range(U):
                    if n + 1 < U:
                        gates(n + 1)
                    prods(n)
                    if n + 1 < U:
                        sums(n + 1)
                    masks_states(n)

            @block.scalar
            def _(act):
                def logs(n):
                    h, d = n // 2, n % 2
                    act.wait_ge(f_ready, n + 1)
                    act.activation(lf[:, n % 2, :], f[:, 8 * d + h, :], ACT.Ln).then_inc(log_ready, 1)

                def exps(n):
                    act.wait_ge(rel_ready, n + 1)
                    if n >= 2:
                        act.wait_ge(prod_ready, n - 1)
                        act.wait_ge(states_ready, n - 1)
                    act.activation(ex[:, n % 2, 1, :], rel[:, n % 2, :], ACT.Exp, scale=-1.0).then_inc(exp_ready, 1)
                    act.wait_ge(exp_ready, 5 * n + 1)
                    act.activation(rel[:, n % 2, :], rel[:, n % 2, :], ACT.Exp).then_inc(exp_ready, 1)
                    act.activation(ex[:, n % 2, 2, :], lf[:, n % 2, LAT], ACT.Exp).then_inc(exp_ready, 1)
                    act.activation(end[:, n % 2, :], end[:, n % 2, :], ACT.Exp).then_inc(exp_ready, 1)
                    act.activation(ge[:, n % 2, 1, :], ge[:, n % 2, 0, :], ACT.Exp).then_inc(exp_ready, 1)

                U = 2 * HEADS
                act.wait_ge(zeroed, 1)
                logs(0)
                exps(0)
                for n in range(U):
                    if n + 1 < U:
                        logs(n + 1)
                    act.wait_ge(kt_ready, n + 1)
                    if n >= 2:
                        act.wait_ge(adds_ready, n - 1)
                    src = kit.bank[n % 2][:, :].rearrange("p (a b) -> p a b", a=4)
                    act.copy(kt[:, n % 2, 0:2, :], src[:, 0:2, :]).then_inc(kt_copied, 1)
                    for half in range(2):
                        lo = half * C
                        dst = kt[lo:lo + C, n % 2, 2:6, :].rearrange("p (t z) b -> p t z b", z=2)[:, :, half, :]
                        act.copy(dst, src[lo:lo + C, 2:4, :]).then_inc(kt_copied, 1)
                    if n + 1 < U:
                        exps(n + 1)
                    if n % 2:
                        act.wait_ge(o_ready, n // 2 + 1)
                        act.copy(out[:, n // 2, :], kit.bank[6 + (n // 2) % 2][:, 0:SEQ]).then_inc(o_copied, 1)

            @block.tensor
            def _(pe):
                for n in range(2 * HEADS):
                    h, d = n // 2, n % 2
                    pe.wait_ge(prod_ready, n + 1)
                    if n >= 2:
                        pe.wait_ge(kt_copied, 3 * (n - 1))
                    for t in range(4):
                        last = pe.transpose(kit.bank[n % 2][:, t * P:(t + 1) * P], kend[:, n % 2, t * P:(t + 1) * P], kit.c("ident"))
                    last.then_inc(kt_ready, 1)
                    if n >= 2:
                        pe.wait_ge(states_ready, n - 1)
                    H2 = C // 2
                    for c in range(NCH):
                        for half in range(2):
                            first, many = (0, C) if half == d else (half * H2, H2)
                            lo = (c % 2) * C + half * H2
                            last = pe.matmul(kit.bank[2 + d][lo:lo + H2, (c // 2) * C + first:(c // 2) * C + first + many],
                                             qk[:, n % 2, 1, c * C + half * H2:c * C + (half + 1) * H2],
                                             qk[:, n % 2, 0, c * C + first:c * C + first + many], start=True, stop=True)
                    last.then_inc(att_ready, 1)
                    pe.wait_ge(kt_copied, 3 * (n + 1))
                    vh = lambda t: vt[:, t, h * P:(h + 1) * P]
                    b = kit.bank[4 + d]
                    for t in range(2):
                        pe.matmul(b[:, 0:P], kt[:, n % 2, t, :], vh(t), start=t == 0, stop=t == 1)
                    for i in range(NCH - 1):
                        c = order[d][i]
                        last = pe.matmul(b[:, (i + 1) * P:(i + 2) * P], kt[:, n % 2, 2 + c, :], vh(2 + c // 2), start=True, stop=True)
                    last.then_inc(adds_ready, 1)
                    if d == 0:
                        continue
                    pe.wait_ge(states_ready, n + 1)
                    if h >= 2:
                        pe.wait_ge(o_copied, h - 1)
                    for t in range(NCH // 2):
                        o = kit.bank[6 + h % 2][:, t * P:(t + 1) * P]
                        pe.matmul(o, vh(2 + t), att[:, 0, t, :], start=True, stop=False)
                        pe.matmul(o, vh(2 + t), att[:, 1, t, :], start=False, stop=False)
                        for half in range(2):
                            c = 2 * t + half
                            for dd in range(2):
                                last = pe.matmul(o[:, half * C:(half + 1) * C], st[:, dd, c, :], qk[:, dd, 2, c * C:(c + 1) * C],
                                                 start=False, stop=half == 1 and dd == 1)
                    last.then_inc(o_ready, 1)
        inner.close()
        pair = lambda ap: ap.rearrange("p a b -> p (a b)")
        head_norm(kit, lambda n: pair(out[:, 2 * n:2 * n + 2, :]), 4, 1.0 / HD, lambda n: kit.col("hg_norm_g_2"))
        vector_only(kit, lambda dve, v: v.by(dve.tensor_tensor(pair(out[:, :, :]), pair(out[:, :, :]), pair(qg[:, 8:16, :]), ALU.mult)))


def second_block(kit, inp, x2, out_dram, scratch):
    nc = kit.nc
    with ExitStack() as mem:
        new = lambda name, *shape: mem.enter_context(kit.sb(name, [P, *shape]))
        cond, mod = new("cond", DC, 2), new("mod", 48, 2)
        gain = new("mod_gain", DC, 2)
        with stage(nc, "silu") as (block, silu):
            @block.scalar
            def _(act):
                act.activation(cond[:, :, 0], kit.cols("c_ctx_2", 0, 8), ACT.Silu).then_inc(silu, 1)
                act.activation(cond[:, :, 1], kit.cols("c_2", 0, 8), ACT.Silu).then_inc(silu, 1)
        m = lambda v, c, who: mod[:, 8 * v + c, who:who + 1]
        hn = new("hn", DC, T2)
        modulation(kit, cond, mod, 0)
        gn = lambda who: (lambda c: gain[:, c, who:who + 1])

        def norm_both(shift_at):
            rmsnorm(kit, x2, [(CTX, lambda c: hn[:, c, CTX], gn(0), lambda c: m(shift_at, c, 0), None),
                              (LAT, lambda c: hn[:, c, LAT], gn(1), lambda c: m(shift_at, c, 1), None)])

        shifts(kit, mod, 1, "norm_mix_g_2", 0, gain)
        norm_both(0)
        with ExitStack() as m2:
            cf = m2.enter_context(kit.sb("conformer_out", [P, DC, T2]))
            conformer(kit, hn, cf)
            so = m2.enter_context(kit.sb("ssd_out", [P, DC, T2]))
            ssd(kit, inp, hn, so)

            def residual(e, s, c, ps):
                s.by(e.scalar_tensor_tensor(x2[:, c, CTX], ps[:, CTX], m(2, c, 0), x2[:, c, CTX], ALU.mult, ALU.add))
                return e.scalar_tensor_tensor(x2[:, c, LAT], ps[:, LAT], m(2, c, 1), x2[:, c, LAT], ALU.mult, ALU.add)

            project_down(kit, lambda k: so[:, k, :] if k < DC else cf[:, k - DC, :], T2, [2] * 8, residual)
        shifts(kit, mod, 4, "norm_ffn_g_2", 0, gain)
        norm_both(3)
        lists, table = new("item_lists", T2 // P, 2, ITEMS), mem.enter_context(nc.sbuf_tensor("item_table", [P, ITEMS + 1], I32))
        route(kit, inp, hn[:, :, :], T2, scratch[0], lists, table)

        def add_both(e, c, ps):
            e.scalar_tensor_tensor(x2[:, c, CTX], ps[:, CTX], m(5, c, 0), x2[:, c, CTX], ALU.mult, ALU.add)
            return e.scalar_tensor_tensor(x2[:, c, LAT], ps[:, LAT], m(5, c, 1), x2[:, c, LAT], ALU.mult, ALU.add)

        experts(kit, hn[:, :, :], T2, scratch[0], lists, table, add_both, inp, 0)
        modulation(kit, cond, mod, 1)
        shifts(kit, mod, 1, "norm_mix_g_2", 1, gain)
        turned_out = lambda ap: ap.rearrange("p (w r) -> p r w", r=ROWS)
        turned_in = lambda ap: ap.rearrange("p (r w) -> p r w", w=GRID_W)
        rmsnorm(kit, x2, [(CTX, lambda c: hn[:, c, CTX], gn(0), lambda c: m(0, c, 0), None),
                          (LAT, lambda c: turned_out(hn[:, c, LAT]), gn(1), lambda c: m(0, c, 1), None)])
        with ExitStack() as m2:
            o = m2.enter_context(kit.sb("hgrn2_out", [P, DC, SEQ]))
            hgrn2(kit, x2, hn, o)

            def residual(e, s, c, ps):
                x = turned_in(x2[:, c, LAT])
                return e.scalar_tensor_tensor(x, turned_out(ps), m(2, c, 1), x, ALU.mult, ALU.add)

            project(kit, lambda k: o[:, k, :], DC, SEQ, [WIDE] * 4, residual)
        shifts(kit, mod, 4, "norm_ffn_g_2", 1, gain)
        x = x2[:, :, LAT]
        rmsnorm(kit, x, [(slice(0, SEQ), lambda c: hn[:, c, 0:SEQ], gn(1), lambda c: m(3, c, 1), None)])
        route(kit, inp, hn[:, :, 0:SEQ], SEQ, scratch[1], lists[:, 0:SEQ // P], table)
        experts(kit, hn[:, :, 0:SEQ], SEQ, scratch[1], lists, table,
                lambda e, c, ps: e.scalar_tensor_tensor(x[:, c, :], ps, m(5, c, 1), x[:, c, :], ALU.mult, ALU.add), inp, 1)
        rmsnorm(kit, x, [(slice(0, SEQ), lambda c: hn[:, c, 0:SEQ], lambda c: kit.col("final_norm_g_2", c), None, None)])
        rows = new("out_tokens", 2, D)
        turn(kit, [([hn[:, c + j, t * P:(t + 1) * P] for j in range(4)], rows[:, t, c * P:(c + 4) * P])
                   for t in range(2) for c in (0, 4)])
        with stage(nc, "stored") as (block, stored):
            @block.sync
            def _(sp):
                sp.dma_start(out_dram[0].rearrange("(t p) d -> p t d", p=P), rows[:, :, :]).then_inc(stored, 16)
                sp.wait_ge(stored, 16)


def build(nc, inp, const, out):
    scratch = [nc.dram_tensor(f"combine{n}", (2, ITEMS, t), F32, kind="Internal").ap() for n, t in enumerate((T2, SEQ))]
    with ExitStack() as mem:
        kit = Kit(nc, mem.enter_context)
        plan_first(kit.feed, inp)
        plan_second(kit.feed, inp)
        x2 = mem.enter_context(kit.sb("x_both", [P, DC, 2 * SEQ]))
        h = x2[:, :, SEQ:2 * SEQ]
        load_vectors(kit, inp, const)
        load_turned(kit, inp["x"][0], lambda c: h[:, c:c + 2, :], DC, "x")
        load_turned(kit, inp["ctx_2"][0], lambda c: x2[:, c:c + 2, 0:SEQ], DC, "ctx")
        first_block(kit, inp, h, mem)
        second_block(kit, inp, x2, out, scratch)


INPUTS = ["x", "p", "ln_pre_mix", "w_in", "conv_w", "a_log", "dt_bias", "gdn_norm", "w_proj_a", "w_proj_b", "w_out",
          "ln_post_mix", "ln_pre_ffn", "w_ffn_gate", "w_ffn_up", "w_ffn_down", "ln_post_ffn", "w_ple", "ln_ple",
          "w_ple_gate", "c_2", "ctx_2", "c_ctx_2", "mod_w_2", "mod_b_2", "norm_mix_g_2", "norm_ffn_g_2", "router_w_2",
          "router_b_2", "moe_w_gate_2", "moe_w_up_2", "moe_w_down_2", "ab_w_in_2", "ssd_conv_w_2", "ssd_conv_b_2",
          "ssd_dt_bias_2", "ssd_a_log_2", "ssd_d_2", "ssd_norm_g_2", "cf_dw_w_2", "cf_dw_b_2", "cf_ln_g_2",
          "cf_ln_b_2", "ab_w_out_2", "hg_w_in_2", "hg_lb_2", "hg_norm_g_2", "hg_w_out_2", "final_norm_g_2"]


def kernel(**inputs):
    from concourse import bacc
    from concourse.bass_utils import run_bass_kernel_spmd

    nc = bacc.Bacc("TRN2", target_bir_lowering=False, num_devices=1)
    arrays, aps = {}, {}
    for name in INPUTS:
        a = np.ascontiguousarray(inputs[name])
        if name == "ssd_d_2":
            a = np.ascontiguousarray(np.repeat(a, S_HD, axis=1))
        arrays[f"in_{name}"] = a
        aps[name] = nc.dram_tensor(f"in_{name}", a.shape, mybir.dt.from_np(a.dtype), kind="ExternalInput").ap()
    table = np.concatenate(list(CONSTANTS.values()), axis=1)
    arrays["constants"] = table
    const = nc.dram_tensor("constants", table.shape, F32, kind="ExternalInput").ap()
    out = nc.dram_tensor("out", (1, SEQ, D), F32, kind="ExternalOutput").ap()
    build(nc, aps, const, out)
    r = run_bass_kernel_spmd(nc, [arrays], core_ids=[0])
    return r.results[0]["out"]
```

```python
from contextlib import ExitStack, contextmanager

import numpy as np

import concourse.bass as bass
from concourse import mybir

F32 = mybir.dt.float32
I32 = mybir.dt.int32
ALU = mybir.AluOpType
ACT = mybir.ActivationFunctionType
AX = mybir.AxisListType

P = 128
D = 1024
DC = D // P
SEQ = 256
EPS = 1e-6
HEADS = 8
HD = 128
FF_TILES = 22
NEG = -1e30
SLOTS = 6
WIDE = 256
SLOT = 2048
S_HEADS, S_HD, S_GROUPS = 16, 64, 4
EXPERTS = 16
CHOICES = 2
CAP = 128
ITEMS = 24
GRID_W = 64
ROWS = SEQ // GRID_W


def constant_table():
    i = np.arange(P)
    f = np.float32
    tri = (i[:, None] <= i[None, :])
    c = {}
    c["ident"] = np.eye(P, dtype=f)
    c["ones"] = np.ones((P, P), f)
    c["tri_f"] = tri.astype(f)
    c["tri_r"] = tri.T.astype(f)
    c["neg_f"] = np.where(tri, f(0), f(NEG))
    neg_r = np.where(tri.T, f(0), f(NEG))
    c["neg_qk"] = np.concatenate([neg_r, np.zeros((P, P), f), neg_r], 1)
    for n in range(7):
        b = 1 << n
        same = (i[:, None] // (2 * b)) == (i[None, :] // (2 * b))
        c[f"join{n}"] = (same & ((i[:, None] // b) % 2 == 0) & ((i[None, :] // b) % 2 == 1)).astype(f)
    rot = np.zeros((P, P), f)
    for d in range(64):
        rot[d + 64, d] = -1.0
        rot[d, d + 64] = 1.0
    c["rot"] = rot
    inv = (f(1.0) / (f(10000.0) ** (np.arange(0, HD, 2, dtype=f) / f(HD)))).astype(f)
    ang = (np.arange(SEQ, dtype=f)[None, :] * inv[:, None]).astype(f)
    c["cos"] = np.tile(np.cos(ang).astype(f), (2, 1))
    c["sin"] = np.tile(np.sin(ang).astype(f), (2, 1))
    j = np.arange(64)
    m = (j[:, None] <= j[None, :])
    c["keep_f"] = np.tile(m.astype(f), (2, 1))
    c["keep_r"] = np.tile(m.T.astype(f), (2, 1))
    t = np.arange(SEQ)
    whole = np.ones(SEQ, f)
    c["carry_f"] = np.tile(np.concatenate([whole, (t % 64 != 0).astype(f)]), (P, 1))
    c["carry_r"] = np.tile(np.concatenate([(t != SEQ - 1).astype(f), (t % 64 != 63).astype(f)]), (P, 1))
    c["count"] = np.tile(np.arange(P, dtype=f), (P, 1))
    c["slot"] = np.arange(P, dtype=f)[:, None].copy()
    k = np.arange(4)
    c["before"] = np.tile((k[None, :] < k[:, None]).astype(f).reshape(1, 16), (P, 1))
    c["notbefore"] = np.tile((k[None, :] >= k[:, None]).astype(f).reshape(1, 16), (P, 1))
    return c


FIRST_BLOCK_ONLY = ("rot", "cos", "sin", *[f"join{n}" for n in range(7)])
CONSTANTS = constant_table()
CONSTANTS.update({n: CONSTANTS.pop(n) for n in FIRST_BLOCK_ONLY})
CONST_AT = {}
_at = 0
for _name, _value in CONSTANTS.items():
    CONST_AT[_name] = (_at, _value.shape[1])
    _at += _value.shape[1]
CONST_WORDS = _at
KEPT_WORDS = CONST_AT[FIRST_BLOCK_ONLY[0]][0]
CONST_AT["neg_r"] = (CONST_AT["neg_qk"][0], P)

VECTORS = [
    ("ln_pre_mix", 8), ("ln_post_mix", 8), ("ln_pre_ffn", 8), ("ln_post_ffn", 8), ("ln_ple", 8),
    ("gdn_norm", 1), ("c_2", 8), ("c_ctx_2", 8), ("norm_mix_g_2", 16), ("norm_ffn_g_2", 16),
    ("ssd_conv_b_2", 16), ("ssd_norm_g_2", 8), ("hg_norm_g_2", 1),
    ("cf_dw_b_2", 8), ("cf_ln_g_2", 8), ("cf_ln_b_2", 8), ("hg_lb_2", 16), ("final_norm_g_2", 8), ("ssd_d_2", 8),
    ("conv_w", 96), ("ssd_conv_w_2", 80), ("mod_b_2", 96),
    ("cf_dw_w_2", 8 * 31),
]


def vector_plan():
    pieces, cols, tile, row = [], {}, 0, 0
    for name, n in VECTORS:
        cols[name] = []
        done = 0
        while done < n:
            if row == P:
                tile, row = tile + 1, 0
            m = min(n - done, P - row)
            pieces.append((name, done, m, tile, row))
            cols[name] += [tile * P + row + q for q in range(m)]
            done += m
            row += m
    return pieces, cols, tile + 1


PIECES, COLS, VTILES = vector_plan()


class Signal:

    def __init__(self, sem):
        self.sem, self.n = sem, 0

    def by(self, instruction):
        instruction.then_inc(self.sem, 1)
        self.n += 1

    def wait(self, engine):
        engine.wait_ge(self.sem, self.n)

    def link(self, engine, instruction):
        self.by(instruction)
        self.wait(engine)


@contextmanager
def stage(nc, *names):
    with ExitStack() as held:
        sems = [held.enter_context(nc.semaphore(n)) for n in names]
        with nc.Block() as block:
            yield (block, *sems)
        with nc.Block() as tidy:
            @tidy.gpsimd
            def _(pool):
                for s in sems:
                    pool.sem_clear(s)


class Feed:

    def __init__(self, nc, hold):
        self.buf = hold(nc.sbuf_tensor("weights", [P, SLOTS, SLOT], F32))
        self.loaded = [hold(nc.semaphore(f"weights_loaded{s}")) for s in range(SLOTS)]
        self.plans = []
        self.at = 0
        self.issued = 0
        self.taken = 0

    def plan(self, iterations, per, source):
        assert iterations == 1 or per % SLOTS == 0
        self.plans.append((iterations, per, source))

    def load(self, sp, src, shift=0):
        slot = self.issued % SLOTS
        k, n = src.shape[1], src.shape[2]
        dst = self.buf[:, slot, 0:k * n].rearrange("p (k n) -> p k n", k=k)
        sp.dma_start(dst, src).then_inc(self.loaded[slot], 16)
        self.issued += 1

    def arrive(self, pe, shape, rounds=0):
        slot = self.taken % SLOTS
        pe.wait_ge(self.loaded[slot], 16 * (self.taken // SLOTS + 1) + 16 * rounds)
        self.taken += 1
        k, n = shape
        return self.buf[:, slot, 0:k * n].rearrange("p (k n) -> p k n", k=k)

    def first(self, sp):
        _, per, source = self.plans[0]
        for j in range(min(SLOTS, per)):
            self.load(sp, source(0, j))

    def run(self, sp, matmuls_done, done, per_iteration=0, before=None):
        iterations, per, source = self.plans[self.at]
        base = self.issued - min(SLOTS, per)
        if iterations == 1:
            for j in range(SLOTS, per):
                if before:
                    before(sp, 0, j)
                sp.wait_ge(matmuls_done, done[j - SLOTS])
                self.load(sp, source(0, j))
        else:
            with sp.Fori(0, iterations - 1) as i:
                for j in range(per):
                    if before:
                        before(sp, i + 1, j)
                    back = j + per - SLOTS
                    if back < per:
                        sp.wait_ge(matmuls_done, i * per_iteration + done[back])
                    else:
                        sp.wait_ge(matmuls_done, (i + 1) * per_iteration + done[back - per])
                    self.load(sp, source(i + 1, j))
            self.issued += per * (iterations - 2)

        def used_up(back):
            sp.wait_ge(matmuls_done, (back // per) * per_iteration + done[back % per])

        self.run_ahead(sp, self.issued - base, used_up)

    def run_ahead(self, sp, units, used_up):
        self.at += 1
        if self.at < len(self.plans):
            _, per, source = self.plans[self.at]
            for j in range(min(SLOTS, per)):
                if units + j >= SLOTS:
                    assert units + j - SLOTS < units
                    used_up(units + j - SLOTS)
                self.load(sp, source(0, j))


class Kit:

    def __init__(self, nc, hold):
        self.nc = nc
        self.const = hold(nc.sbuf_tensor("const", [P, KEPT_WORDS], F32))
        self.const_first = None
        self.vec = hold(nc.sbuf_tensor("vec", [P, VTILES * P], F32))
        self.bank = [hold(nc.psum_tensor(f"bank{b}", [P, 512], F32)) for b in range(8)]
        self.feed = Feed(nc, hold)
        self.tensors = 0
        self.small = {}
        self.small_loaded = hold(nc.semaphore("small_loaded"))

    def sb(self, name, shape):
        self.tensors += 1
        return self.nc.sbuf_tensor(f"{name}_{self.tensors}", shape, F32)

    def wait_small(self, engine):
        engine.wait_ge(self.small_loaded, 16 * len(self.small))

    def c(self, name, rows=P):
        at, n = CONST_AT[name]
        if name in FIRST_BLOCK_ONLY:
            return self.const_first[0:rows, at - KEPT_WORDS:at - KEPT_WORDS + n]
        return self.const[0:rows, at:at + n]

    def col(self, name, k=0):
        at = COLS[name][k]
        return self.vec[:, at:at + 1]

    def cols(self, name, k, n):
        at = COLS[name][k]
        assert COLS[name][k + n - 1] == at + n - 1
        return self.vec[:, at:at + n]


def turn(kit, groups):
    nc = kit.nc
    with stage(nc, "turned", "copied_v", "copied_a") as (block, turned, copied_v, copied_a):
        @block.tensor
        def _(pe):
            for n, (sources, _) in enumerate(groups):
                if n >= 4:
                    pe.wait_ge((copied_v, copied_a)[n % 2], (n - 4) // 2 + 1)
                at = 0
                for src in sources:
                    rows, width = src.shape
                    last = pe.transpose(kit.bank[n % 4][0:width, at:at + rows], src, kit.c("ident")[0:rows, 0:rows])
                    at += rows
                last.then_inc(turned, 1)

        @block.vector
        def _(dve):
            for n, (sources, dst) in list(enumerate(groups))[0::2]:
                dve.wait_ge(turned, n + 1)
                total = sum(s.shape[0] for s in sources)
                src = kit.bank[n % 4][0:dst.shape[0], 0:total]
                if len(dst.shape) == 3:
                    src = src.rearrange("p (a b) -> p a b", a=dst.shape[1])
                dve.tensor_copy(dst, src).then_inc(copied_v, 1)

        @block.scalar
        def _(act):
            for n, (sources, dst) in list(enumerate(groups))[1::2]:
                act.wait_ge(turned, n + 1)
                total = sum(s.shape[0] for s in sources)
                src = kit.bank[n % 4][0:dst.shape[0], 0:total]
                if len(dst.shape) == 3:
                    src = src.rearrange("p (a b) -> p a b", a=dst.shape[1])
                act.copy(dst, src).then_inc(copied_a, 1)


def rmsnorm(kit, x, parts, tiles=DC, width=D, first=0):
    nc = kit.nc
    T = x.shape[2]
    with ExitStack() as mem:
        sq = mem.enter_context(kit.sb("squares", [P, 4, T]))
        rstd = mem.enter_context(kit.sb("rstd", [P, T]))
        tmp = mem.enter_context(kit.sb("normed", [P, 4, T]))
        biased = [p for p in parts if p[3] is not None]
        assert len(biased) in (0, len(parts))
        grid_like = lambda out: (lambda ap: ap.rearrange("p (r w) -> p r w", w=GRID_W)) if len(out.shape) == 3 else (lambda ap: ap)
        with stage(nc, "squared", "summed", "mean_ready", "root_ready", "scaled", "finished", "v") as (
                block, squared, summed, mean_ready, root_ready, scaled, finished, vsem):
            total = kit.bank[0][:, 0:T]

            @block.scalar
            def _(act):
                for c in range(tiles):
                    if c >= 4:
                        act.wait_ge(summed, c - 3)
                    act.activation(sq[:, c % 4, :], x[:, c, :], ACT.Square).then_inc(squared, 1)
                act.wait_ge(mean_ready, 1)
                act.activation(rstd[:, :], rstd[:, :], ACT.Sqrt).then_inc(root_ready, 1)
                if biased:
                    for c in range(tiles):
                        act.wait_ge(scaled, c + 1)
                        for (sl, out, gain, bias, _) in parts:
                            ins = act.activation(out(c), grid_like(out(c))(tmp[:, c % 4, sl]), ACT.Identity, bias=bias(c), scale=gain(c))
                        ins.then_inc(finished, 1)

            @block.tensor
            def _(pe):
                for c in range(tiles):
                    pe.wait_ge(squared, c + 1)
                    pe.matmul(total, kit.c("ones"), sq[:, c % 4, :], start=c == 0,
                              stop=c == tiles - 1).then_inc(summed, 1)

            @block.vector
            def _(dve):
                v = Signal(vsem)
                dve.wait_ge(summed, tiles)
                dve.tensor_scalar(rstd[:, :], total, 1.0 / width, EPS, ALU.mult, ALU.add).then_inc(mean_ready, 1)
                dve.wait_ge(root_ready, 1)
                v.link(dve, dve.reciprocal(rstd[:, :], rstd[:, :]))
                n = 0
                for c in range(tiles):
                    if biased:
                        if c >= 4:
                            dve.wait_ge(finished, c - 3)
                        dve.tensor_tensor(tmp[:, c % 4, :], x[:, c, :], rstd[:, :], ALU.mult).then_inc(scaled, 1)
                        continue
                    for (sl, out, gain, _, residual) in parts:
                        grid = grid_like(out(c))
                        xs, rs = grid(x[:, c, sl]), grid(rstd[:, sl])
                        if residual is None:
                            v.by(dve.scalar_tensor_tensor(out(c), xs, gain(c), rs, ALU.mult, ALU.mult))
                            continue
                        t = grid(tmp[:, n % 4, sl])
                        n += 1
                        v.link(dve, dve.scalar_tensor_tensor(t, xs, gain(c), rs, ALU.mult, ALU.mult))
                        v.by(dve.tensor_tensor(out(c), t, residual(c), ALU.add))


def project_programs(kit, x, ktiles, T, widths, evacuate):
    feed = kit.feed
    done, n = [], 0
    for w in widths:
        n += w // P
        done.append(n)

    def sync(sp, ready):
        feed.run(sp, ready, done)

    def tensor(pe, ready, evacuated):
        n = 0
        for w in widths:
            unit = feed.arrive(pe, (ktiles, w))
            for m in range(w // P):
                if n >= 4:
                    pe.wait_ge(evacuated, n - 3)
                for k in range(ktiles):
                    last = pe.matmul(kit.bank[n % 4][:, 0:T], unit[:, k, m * P:(m + 1) * P], x(k),
                                     start=k == 0, stop=k == ktiles - 1)
                last.then_inc(ready, 1)
                n += 1

    def drain(eng, ready, evacuated, step, between=None):
        s = Signal(step)
        for n in range(done[-1]):
            eng.wait_ge(ready, n + 1)
            evacuate(eng, s, n, kit.bank[n % 4][:, 0:T]).then_inc(evacuated, 1)
            if between:
                between(n)

    return sync, tensor, drain


def project(kit, x, ktiles, T, widths, evacuate, engine="vector"):
    sync, tensor, drain = project_programs(kit, x, ktiles, T, widths, evacuate)
    with stage(kit.nc, "tiles_ready", "evacuated", "step") as (block, ready, evacuated, step):
        @block.sync
        def _(sp):
            sync(sp, ready)

        @block.tensor
        def _(pe):
            tensor(pe, ready, evacuated)

        if engine == "vector":
            @block.vector
            def _(dve):
                drain(dve, ready, evacuated, step)
        else:
            @block.scalar
            def _(act):
                drain(act, ready, evacuated, step)


def project_loop(kit, x, T, iterations, evacuate):
    nc = kit.nc
    feed = kit.feed
    per = 2 * SLOTS
    with stage(nc, "tiles_ready", "evacuated") as (block, ready, evacuated):
        @block.sync
        def _(sp):
            feed.run(sp, ready, [2 * (j + 1) for j in range(SLOTS)], per)

        @block.tensor
        def _(pe):
            with pe.Fori(0, iterations) as i:
                n = 0
                for j in range(SLOTS):
                    unit = feed.arrive(pe, (DC, WIDE), rounds=i)
                    for m in range(2):
                        pe.wait_ge(evacuated, i * per + n + 1)
                        for k in range(DC):
                            last = pe.matmul(kit.bank[n % 4][:, 0:T], unit[:, k, m * P:(m + 1) * P], x(k),
                                             start=k == 0, stop=k == DC - 1)
                        last.then_inc(ready, 1)
                        n += 1
            feed.taken += SLOTS * (iterations - 1)

        @block.vector
        def _(dve):
            dve.sem_inc(evacuated, 4)
            with dve.Fori(0, iterations) as i:
                for n in range(per):
                    dve.wait_ge(ready, i * per + n + 1)
                    evacuate(dve, i, n, kit.bank[n % 4][:, 0:T]).then_inc(evacuated, 1)


def project_down(kit, x, T, unit_ktiles, evacuate, engine="vector"):
    nc = kit.nc
    feed = kit.feed
    units = len(unit_ktiles)
    with stage(nc, "units_used", "evacuated", "step") as (block, used, evacuated, step):
        @block.sync
        def _(sp):
            feed.run(sp, used, [u + 1 for u in range(units - 1)] + [units - 1 + DC])

        @block.tensor
        def _(pe):
            at, total = 0, sum(unit_ktiles)
            for u, kt in enumerate(unit_ktiles):
                unit = feed.arrive(pe, (kt, D))
                for m in range(DC):
                    for k in range(kt):
                        last = pe.matmul(kit.bank[m][:, 0:T], unit[:, k, m * P:(m + 1) * P], x(at + k),
                                         start=at + k == 0, stop=at + k == total - 1)
                    if u == units - 1:
                        last.then_inc(used, 1)
                if u < units - 1:
                    last.then_inc(used, 1)
                at += kt

        def drain(eng):
            s = Signal(step)
            for m in range(DC):
                eng.wait_ge(used, units + m)
                evacuate(eng, s, m, kit.bank[m][:, 0:T]).then_inc(evacuated, 1)

        if engine == "vector":
            @block.vector
            def _(dve):
                drain(dve)
        else:
            @block.scalar
            def _(act):
                drain(act)


def head_norm(kit, x, pairs, spread, pre, post=None):
    nc = kit.nc
    with ExitStack() as mem:
        sq = mem.enter_context(kit.sb("head_squares", [P, 2, 512]))
        r = mem.enter_context(kit.sb("head_roots", [P, 2, 512]))
        with stage(nc, "squared", "summed", "mean_ready", "root_ready", "scaled", "inverted") as (
                block, squared, summed, mean_ready, root_ready, scaled, inverted):
            @block.scalar
            def _(act):
                def square(n):
                    if n >= 2:
                        act.wait_ge(summed, n - 1)
                    act.activation(sq[:, n % 2, :], x(n), ACT.Square).then_inc(squared, 1)

                square(0)
                for n in range(pairs):
                    if n + 1 < pairs:
                        square(n + 1)
                    act.wait_ge(mean_ready, n + 1)
                    act.activation(r[:, n % 2, :], r[:, n % 2, :], ACT.Sqrt).then_inc(root_ready, 1)

            @block.tensor
            def _(pe):
                for n in range(pairs):
                    pe.wait_ge(squared, n + 1)
                    if n >= 2:
                        pe.wait_ge(mean_ready, n - 1)
                    pe.matmul(kit.bank[n % 2][:, :], kit.c("ones"), sq[:, n % 2, :], start=True,
                              stop=True).then_inc(summed, 1)

            @block.vector
            def _(dve):
                def mean(n):
                    if n >= 2:
                        dve.wait_ge(scaled, n - 1)
                    dve.wait_ge(summed, n + 1)
                    dve.tensor_scalar(r[:, n % 2, :], kit.bank[n % 2][:, :], spread, EPS, ALU.mult,
                                      ALU.add).then_inc(mean_ready, 1)

                mean(0)
                for n in range(pairs):
                    if n + 1 < pairs:
                        mean(n + 1)
                    dve.wait_ge(root_ready, n + 1)
                    dve.reciprocal(r[:, n % 2, :], r[:, n % 2, :]).then_inc(inverted, 1)
                    dve.wait_ge(inverted, n + 1)
                    dve.scalar_tensor_tensor(x(n), x(n), pre(n), r[:, n % 2, :], ALU.mult, ALU.mult).then_inc(scaled, 1)


def softplus(kit, x, out, n):
    nc = kit.nc
    with ExitStack() as mem:
        e = mem.enter_context(kit.sb("sp_e", [P, n]))
        u = mem.enter_context(kit.sb("sp_u", [P, n]))
        w = mem.enter_context(kit.sb("sp_w", [P, n]))
        with stage(nc, "a", "exp_ready", "one_plus", "log_ready", "v") as (block, a, exp_ready, one_plus, log_ready, vsem):
            @block.scalar
            def _(act):
                act.activation(e[:, :], x, ACT.Abs).then_inc(a, 1)
                act.wait_ge(a, 1)
                act.activation(e[:, :], e[:, :], ACT.Exp, scale=-1.0).then_inc(exp_ready, 1)
                act.wait_ge(one_plus, 1)
                act.activation(w[:, :], u[:, :], ACT.Ln).then_inc(log_ready, 1)

            @block.vector
            def _(dve):
                v = Signal(vsem)
                dve.wait_ge(exp_ready, 1)
                dve.tensor_scalar(u[:, :], e[:, :], 1.0, None, ALU.add).then_inc(one_plus, 1)
                dve.wait_ge(one_plus, 1)
                dve.wait_ge(log_ready, 1)
                v.link(dve, dve.tensor_scalar(u[:, :], u[:, :], 1.0, None, ALU.subtract))
                v.link(dve, dve.tensor_tensor(e[:, :], e[:, :], u[:, :], ALU.subtract))
                v.link(dve, dve.tensor_tensor(e[:, :], e[:, :], w[:, :], ALU.add))
                v.by(dve.scalar_tensor_tensor(out, x, 0.0, e[:, :], ALU.max, ALU.add))


def rope(kit, qk):
    nc = kit.nc
    with ExitStack() as mem:
        a = mem.enter_context(kit.sb("x_cos", [P, 2, 2, SEQ]))
        b = mem.enter_context(kit.sb("swap_sin", [P, 2, 2, SEQ]))
        cos = kit.c("cos").unsqueeze(1).broadcast_to([P, 2, SEQ])
        sin = kit.c("sin").unsqueeze(1).broadcast_to([P, 2, SEQ])
        with stage(nc, "swapped", "bank_read", "v") as (block, swapped, bank_read, vsem):
            @block.tensor
            def _(pe):
                for n in range(8):
                    if n >= 2:
                        pe.wait_ge(bank_read, n - 1)
                    pe.matmul(kit.bank[n % 2][:, :], kit.c("rot"), qk[:, 2 * n:2 * n + 2, :].rearrange("p a b -> p (a b)"),
                              start=True, stop=True).then_inc(swapped, 1)

            @block.vector
            def _(dve):
                v = Signal(vsem)
                for n in range(8):
                    x = qk[:, 2 * n:2 * n + 2, :]
                    dve.wait_ge(swapped, n + 1)
                    v.by(dve.tensor_tensor(a[:, n % 2], x, cos, ALU.mult))
                    dve.tensor_tensor(b[:, n % 2], kit.bank[n % 2][:, :].rearrange("p (a b) -> p a b", a=2), sin,
                                      ALU.mult).then_inc(bank_read, 1)
                    v.wait(dve)
                    dve.wait_ge(bank_read, n + 1)
                    v.by(dve.tensor_tensor(x, a[:, n % 2], b[:, n % 2], ALU.add))
                    if n >= 1:
                        v.wait(dve)


def moba(kit, qkv, v_tok, y):
    nc = kit.nc
    scale = HD ** -0.5
    with ExitStack() as mem:
        s = mem.enter_context(kit.sb("scores", [P, 2, 384]))
        pt = mem.enter_context(kit.sb("probs_t", [P, 2, 384]))
        small = mem.enter_context(kit.sb("softmax_small", [P, 2, 8]))
        with stage(nc, "scored", "maxed", "exped", "normed", "pt_ready", "pt_copied", "y_ready", "y_copied", "v") as (
                block, scored, maxed, exped, normed, pt_ready, pt_copied, y_ready, y_copied, vsem):
            qt = lambda h, t: qkv[:, h, t * P:(t + 1) * P]
            kt = lambda h, n: qkv[:, HEADS + h, 0:n]

            @block.tensor
            def _(pe):
                def score(h):
                    b = kit.bank[h % 2]
                    if h >= 2:
                        pe.wait_ge(maxed, h - 1)
                    pe.matmul(b[:, 0:P], qt(h, 0), kt(h, P), start=True, stop=True)
                    pe.matmul(b[:, P:3 * P], qt(h, 1), kt(h, 2 * P), start=True, stop=True).then_inc(scored, 1)

                def transpose(h):
                    b = kit.bank[2 + h % 2]
                    pe.wait_ge(normed, h + 1)
                    if h >= 2:
                        pe.wait_ge(pt_copied, h - 1)
                    for j in range(3):
                        last = pe.transpose(b[:, j * P:(j + 1) * P], s[:, h % 2, j * P:(j + 1) * P], kit.c("ident"))
                    last.then_inc(pt_ready, 1)

                def output(h):
                    o = kit.bank[4 + h % 2]
                    pe.wait_ge(pt_copied, h + 1)
                    if h >= 2:
                        pe.wait_ge(y_copied, h - 1)
                    vh = lambda t: v_tok[:, t, h * P:(h + 1) * P]
                    pe.matmul(o[:, 0:P], vh(0), pt[:, h % 2, 0:P], start=True, stop=True)
                    pe.matmul(o[:, P:2 * P], vh(0), pt[:, h % 2, P:2 * P], start=True, stop=False)
                    pe.matmul(o[:, P:2 * P], vh(1), pt[:, h % 2, 2 * P:3 * P], start=False, stop=True).then_inc(y_ready, 1)

                score(0)
                for h in range(HEADS):
                    if h + 1 < HEADS:
                        score(h + 1)
                    transpose(h)
                    if h >= 1:
                        output(h - 1)
                output(HEADS - 1)

            @block.vector
            def _(dve):
                v = Signal(vsem)

                def mask_and_max(h):
                    dve.wait_ge(scored, h + 1)
                    if h >= 2:
                        dve.wait_ge(pt_ready, h - 1)
                    v.link(dve, dve.scalar_tensor_tensor(s[:, h % 2, :], kit.bank[h % 2][:, 0:384], scale,
                                                         kit.c("neg_qk"), ALU.mult, ALU.add))
                    sm = small[:, h % 2]
                    v.by(dve.tensor_reduce(sm[:, 0:1], s[:, h % 2, 0:P], AX.X, ALU.max, negate=True))
                    v.by(dve.tensor_reduce(sm[:, 1:2], s[:, h % 2, P:384], AX.X, ALU.max, negate=True))
                    v.wait(dve)
                    dve.tensor_copy(sm[:, 6:7], sm[:, 0:1]).then_inc(maxed, 1)

                def normalise(h):
                    sm = small[:, h % 2]
                    dve.wait_ge(exped, 2 * h + 2)
                    v.link(dve, dve.reciprocal(sm[:, 4:6], sm[:, 2:4]))
                    v.link(dve, dve.tensor_scalar(s[:, h % 2, 0:P], s[:, h % 2, 0:P], sm[:, 4:5], None, ALU.mult))
                    dve.tensor_scalar(s[:, h % 2, P:384], s[:, h % 2, P:384], sm[:, 5:6], None, ALU.mult).then_inc(normed, 1)

                def copy_turned(h):
                    dve.wait_ge(pt_ready, h + 1)
                    if h >= 2:
                        dve.wait_ge(y_ready, h - 1)
                    dve.tensor_copy(pt[:, h % 2, :], kit.bank[2 + h % 2][:, 0:384]).then_inc(pt_copied, 1)

                mask_and_max(0)
                for h in range(HEADS):
                    if h >= 1:
                        copy_turned(h - 1)
                    if h + 1 < HEADS:
                        mask_and_max(h + 1)
                    normalise(h)
                copy_turned(HEADS - 1)

            @block.scalar
            def _(act):
                def exps(h):
                    sm = small[:, h % 2]
                    act.wait_ge(maxed, h + 1)
                    act.activation(s[:, h % 2, 0:P], s[:, h % 2, 0:P], ACT.Exp, bias=sm[:, 0:1],
                                   accum_out=sm[:, 2:3]).then_inc(exped, 1)
                    act.activation(s[:, h % 2, P:384], s[:, h % 2, P:384], ACT.Exp, bias=sm[:, 1:2],
                                   accum_out=sm[:, 3:4]).then_inc(exped, 1)

                def copy_output(h):
                    act.wait_ge(y_ready, h + 1)
                    act.copy(y[:, h, :], kit.bank[4 + h % 2][:, 0:SEQ]).then_inc(y_copied, 1)

                exps(0)
                for h in range(HEADS):
                    if h + 1 < HEADS:
                        exps(h + 1)
                    if h >= 1:
                        copy_output(h - 1)
                copy_output(HEADS - 1)


def conv_beside_project(kit, x, tiles, taps, weight, spans, finish, projection):
    nc = kit.nc
    T = x.shape[2]
    sync, tensor, drain = projection
    with ExitStack() as mem:
        acc = mem.enter_context(kit.sb("conv_sum", [P, 8, T]))
        with stage(nc, "tiles_ready", "evacuated", "step", "conv_ready", "finished", "v") as (
                block, ready, evacuated, step, conv_ready, finished, vsem):
            @block.sync
            def _(sp):
                sync(sp, ready)

            @block.tensor
            def _(pe):
                tensor(pe, ready, evacuated)

            @block.vector
            def _(dve):
                v = Signal(vsem)
                for g in range(tiles // 4):
                    if g >= 2:
                        dve.wait_ge(finished, 4 * (g - 1))
                    for order, tap in enumerate(taps):
                        for j in range(4):
                            c = 4 * g + j
                            a = acc[:, c % 8, :]
                            o, i = spans(tap, a, x[:, c, :])
                            if order == 0:
                                v.by(dve.tensor_scalar(a, x[:, c, :], weight(tap, c), None, ALU.mult))
                            elif order < len(taps) - 1:
                                v.by(dve.scalar_tensor_tensor(o, i, weight(tap, c), o, ALU.mult, ALU.add))
                            else:
                                dve.scalar_tensor_tensor(o, i, weight(tap, c), o, ALU.mult, ALU.add).then_inc(conv_ready, 1)
                        v.wait(dve)

            @block.scalar
            def _(act):
                def finish_two(n):
                    for c in range(2 * n, min(2 * n + 2, tiles)):
                        act.wait_ge(conv_ready, c + 1)
                        finish(act, c, acc[:, c % 8, :]).then_inc(finished, 1)

                drain(act, ready, evacuated, step, finish_two)


def gdn_scalars(kit, u, w_ba, bias, alog, mem):
    nc = kit.nc
    new = lambda name: mem.enter_context(kit.sb(name, [P, 2, HEADS]))
    raw, beta, g, gc, egc, kbe, kdec = [new(n) for n in ("ba_a", "beta", "g", "g_sum", "g_exp", "beta_exp", "k_decay")]
    b0 = kit.bank[0][:, 0:32].rearrange("p (t n) -> p t n", t=2)
    with stage(nc, "ba_ready", "beta_ready", "v") as (block, ba_ready, beta_ready, vsem):
        @block.tensor
        def _(pe):
            kit.wait_small(pe)
            for t in range(2):
                for k in range(DC):
                    last = pe.matmul(b0[:, t, :], u[:, k, t * P:(t + 1) * P], w_ba[:, k, :], start=k == 0, stop=k == DC - 1)
            last.then_inc(ba_ready, 1)

        @block.scalar
        def _(act):
            act.wait_ge(ba_ready, 1)
            act.activation(beta[:, :, :], b0[:, :, 0:8], ACT.Sigmoid).then_inc(beta_ready, 1)
            act.activation(alog[:, :], alog[:, :], ACT.Exp).then_inc(beta_ready, 1)

        @block.vector
        def _(dve):
            dve.wait_ge(beta_ready, 1)
            dve.tensor_tensor(raw[:, :, :], b0[:, :, 8:16], bias[:, :].unsqueeze(1).broadcast_to([P, 2, 8]), ALU.add).then_inc(vsem, 1)
    softplus(kit, raw[:, :, :].rearrange("p a b -> p (a b)"), raw[:, :, :].rearrange("p a b -> p (a b)"), 16)
    sums = kit.bank[0][:, 0:16].rearrange("p (t n) -> p t n", t=2)
    totals = kit.bank[1][:, 0:8]
    with stage(nc, "g_ready", "sums_ready", "copied", "exp_ready", "v") as (block, g_ready, sums_ready, copied, exp_ready, vsem):
        @block.vector
        def _(dve):
            v = Signal(vsem)
            dve.scalar_tensor_tensor(g[:, :, :], raw[:, :, :], -1.0, alog[:, :].unsqueeze(1).broadcast_to([P, 2, 8]),
                                     ALU.mult, ALU.mult).then_inc(g_ready, 1)
            dve.wait_ge(sums_ready, 1)
            v.link(dve, dve.tensor_copy(gc[:, :, :], sums))
            dve.tensor_tensor(kdec[:, 0, :], totals, gc[:, 0, :], ALU.subtract).then_inc(copied, 1)
            dve.wait_ge(exp_ready, 1)
            v.by(dve.tensor_tensor(kbe[:, :, :], beta[:, :, :], egc[:, :, :], ALU.mult))

        @block.tensor
        def _(pe):
            pe.wait_ge(g_ready, 1)
            pe.matmul(totals, kit.c("ones"), g[:, 0, :], start=True, stop=True)
            pe.matmul(sums[:, 0, :], kit.c("tri_f"), g[:, 0, :], start=True, stop=True)
            pe.matmul(sums[:, 1, :], kit.c("tri_f"), g[:, 1, :], start=True, stop=True).then_inc(sums_ready, 1)

        @block.scalar
        def _(act):
            act.wait_ge(copied, 1)
            act.activation(egc[:, :, :], gc[:, :, :], ACT.Exp).then_inc(exp_ready, 1)
            act.activation(kdec[:, 0, :], kdec[:, 0, :], ACT.Exp).then_inc(exp_ready, 1)
    return beta, g, gc, kbe, kdec


def gdn_group(kit, h0, qkv, scal, out):
    nc = kit.nc
    beta, g, gc, kbe, kdec = scal
    qT = lambda h, t: qkv[:, h0 + h, t * P:(t + 1) * P]
    kT = lambda h, t: qkv[:, 8 + h0 + h, t * P:(t + 1) * P]
    q4 = lambda t: qkv[:, h0:h0 + 4, t * P:(t + 1) * P]
    k4 = lambda t: qkv[:, 8 + h0:12 + h0, t * P:(t + 1) * P]
    v1 = lambda h, t: qkv[:, 16 + h0 + h, t * P:(t + 1) * P]
    four = lambda ap: ap.rearrange("p (h n) -> p h n", h=4)
    with ExitStack() as mem:
        new = lambda name, n: mem.enter_context(kit.sb(name, [P, n, 4, P]))
        ktok, vtok = new("k_tok", 2), new("v_tok4", 2)
        at, attn = new("a_t", 2), new("attn_t", 2)
        flat = lambda ap: ap.rearrange("p h n -> p (h n)")
        turn(kit, [([kT(h, t) for h in range(4)], flat(ktok[:, t])) for t in range(2)]
             + [([v1(h, t) for h in range(4)], flat(vtok[:, t])) for t in range(2)])
        with ExitStack() as mem2:
            new2 = lambda name, n: mem2.enter_context(kit.sb(name, [P, n, 4, P]))
            qe = new("q_decayed", 1)
            dec, kb, eg = new2("decay_t", 2), new2("k_beta_t", 2), new2("exp_rows", 1)
            with stage(nc, "rows_ready", "args_ready", "exp_ready", "kb_ready", "products_ready", "v", "qe_sem") as (
                    block, rows_ready, args_ready, exp_ready, kb_ready, products_ready, vsem, qe_sem):
                @block.tensor
                def _(pe):
                    for t in range(2):
                        for h in range(4):
                            pe.matmul(kit.bank[t][:, h * P:(h + 1) * P], g[:, t, h0 + h:h0 + h + 1].broadcast_to([P, P]),
                                      kit.c("tri_f"), start=True, stop=True)
                        for h in range(4):
                            last = pe.matmul(kit.bank[2 + t][:, h * P:(h + 1) * P],
                                             beta[:, t, h0 + h:h0 + h + 1].broadcast_to([P, P]), kit.c("ident"),
                                             start=True, stop=True)
                        last.then_inc(rows_ready, 1)
                    for t in range(2):
                        for h in range(4):
                            pe.matmul(kit.bank[4 + t][:, h * P:(h + 1) * P], kT(h, t), qT(h, t), start=True, stop=True)
                    for t in range(2):
                        pe.wait_ge(kb_ready, t + 1)
                        for h in range(4):
                            last = pe.matmul(kit.bank[6 + t][:, h * P:(h + 1) * P], kT(h, t), kb[:, t, h, :],
                                             start=True, stop=True)
                        last.then_inc(products_ready, 1)

                @block.vector
                def _(dve):
                    v = Signal(vsem)
                    for t in range(2):
                        dve.wait_ge(rows_ready, t + 1)
                        for h in range(4):
                            ins = dve.scalar_tensor_tensor(dec[:, t, h, :], kit.bank[t][:, h * P:(h + 1) * P],
                                                           gc[:, t, h0 + h:h0 + h + 1], kit.c("neg_f"), ALU.subtract, ALU.add)
                            ins.then_inc(args_ready, 1)
                        dve.tensor_tensor(kb[:, t], k4(t), four(kit.bank[2 + t][:, :]), ALU.mult).then_inc(kb_ready, 1)
                        col = (lambda s: s[:, t, h0:h0 + 4].unsqueeze(2).broadcast_to([P, 4, P]))
                        v.by(dve.tensor_tensor(vtok[:, t], vtok[:, t], col(beta), ALU.mult))
                        v.by(dve.tensor_tensor(ktok[:, t], ktok[:, t], col(kdec if t == 0 else kbe), ALU.mult))
                    dve.wait_ge(exp_ready, 2)
                    v.by(dve.tensor_tensor(qe[:, 0], q4(1), eg[:, 0], ALU.mult))
                    dve.wait_ge(exp_ready, 3)
                    for t in range(2):
                        dve.wait_ge(products_ready, t + 1)
                        v.by(dve.tensor_tensor(at[:, t], four(kit.bank[6 + t][:, :]), dec[:, t], ALU.mult))
                        v.by(dve.tensor_tensor(attn[:, t], four(kit.bank[4 + t][:, :]), dec[:, t], ALU.mult))

                @block.scalar
                def _(act):
                    act.wait_ge(args_ready, 4)
                    act.activation(dec[:, 0], dec[:, 0], ACT.Exp).then_inc(exp_ready, 1)
                    act.wait_ge(args_ready, 8)
                    act.activation(eg[:, 0], four(kit.bank[1][:, :]), ACT.Exp).then_inc(exp_ready, 1)
                    act.activation(dec[:, 1], dec[:, 1], ACT.Exp).then_inc(exp_ready, 1)
        e, d, pm, am = new("inverse_t", 2), new("inverse", 2), new("below", 2), new("a_joined", 2)
        bcast = lambda name: kit.c(name).unsqueeze(1).broadcast_to([P, 4, P])
        with stage(nc, "masked", "p_ready", "p_copied", "ed_ready", "e_done", "d_done") as (
                block, masked, p_ready, p_copied, ed_ready, e_done, d_done):
            @block.tensor
            def _(pe):
                def below(level, t):
                    n = 2 * level + t
                    pe.wait_ge(masked, n + 1)
                    if level:
                        pe.wait_ge(p_copied, n - 1)
                        pe.wait_ge(d_done, n - 1)
                    for h in range(4):
                        rhs = d[:, t, h, :] if level else kit.c("ident")
                        last = pe.matmul(kit.bank[t][:, h * P:(h + 1) * P], am[:, t, h, :], rhs, start=True, stop=True)
                    last.then_inc(p_ready, 1)

                below(0, 0)
                below(0, 1)
                for level in range(1, 7):
                    for t in range(2):
                        below(level, t)
                    for t in range(2):
                        n = 2 * level + t
                        pe.wait_ge(p_copied, n + 1)
                        pe.wait_ge(e_done, n - 1)
                        for h in range(4):
                            last = pe.matmul(kit.bank[2 + t][:, h * P:(h + 1) * P], pm[:, t, h, :], e[:, t, h, :],
                                             start=True, stop=True)
                        if level < 6:
                            for h in range(4):
                                last = pe.matmul(kit.bank[4 + t][:, h * P:(h + 1) * P], e[:, t, h, :], pm[:, t, h, :],
                                                 start=True, stop=True)
                        last.then_inc(ed_ready, 1)

            @block.gpsimd
            def _(pool):
                for level in range(7):
                    for t in range(2):
                        n = 2 * level + t
                        if level:
                            pool.wait_ge(p_ready, n - 1)
                            if level == 1:
                                pool.wait_ge(e_done, n - 1)
                        pool.tensor_tensor(am[:, t], at[:, t], bcast(f"join{level}"), ALU.mult).then_inc(masked, 1)

            @block.scalar
            def _(act):
                for level in range(7):
                    for t in range(2):
                        n = 2 * level + t
                        act.wait_ge(p_ready, n + 1)
                        if level >= 2:
                            act.wait_ge(ed_ready, n - 3)
                        act.copy(pm[:, t], four(kit.bank[t][:, :])).then_inc(p_copied, 1)

            @block.vector
            def _(dve):
                for t in range(2):
                    dve.wait_ge(masked, t + 1)
                    dve.tensor_tensor(e[:, t], bcast("ident"), am[:, t], ALU.subtract).then_inc(e_done, 1)
                    dve.wait_ge(p_copied, t + 1)
                    dve.tensor_tensor(d[:, t], bcast("ident"), pm[:, t], ALU.subtract).then_inc(d_done, 1)
                for level in range(1, 7):
                    for t in range(2):
                        n = 2 * level + t
                        dve.wait_ge(ed_ready, n - 1)
                        dve.wait_ge(e_done, n - 1)
                        dve.tensor_tensor(e[:, t], e[:, t], four(kit.bank[2 + t][:, :]), ALU.subtract).then_inc(e_done, 1)
                        if level < 6:
                            dve.wait_ge(d_done, n - 1)
                            dve.tensor_tensor(d[:, t], d[:, t], four(kit.bank[4 + t][:, :]), ALU.subtract).then_inc(d_done, 1)
        vn0, nw, s1, vn1 = pm[:, 0], pm[:, 1], d[:, 0], d[:, 1]
        with stage(nc, "u_ready", "w_ready", "s_ready", "n_ready", "o_ready", "a_copied", "v_copied") as (
                block, u_ready, w_ready, s_ready, n_ready, o_ready, a_copied, v_copied):
            @block.tensor
            def _(pe):
                for h in range(4):
                    last = pe.matmul(kit.bank[0][:, h * P:(h + 1) * P], e[:, 0, h, :], vtok[:, 0, h, :], start=True, stop=True)
                last.then_inc(u_ready, 1)
                for h in range(4):
                    last = pe.matmul(kit.bank[1][:, h * P:(h + 1) * P], ktok[:, 1, h, :], e[:, 1, h, :], start=True, stop=True)
                last.then_inc(w_ready, 1)
                pe.wait_ge(a_copied, 1)
                for h in range(4):
                    last = pe.matmul(kit.bank[2][:, h * P:(h + 1) * P], ktok[:, 0, h, :], vn0[:, h, :], start=True, stop=True)
                last.then_inc(s_ready, 1)
                pe.wait_ge(v_copied, 2)
                for h in range(4):
                    b = kit.bank[3][:, h * P:(h + 1) * P]
                    pe.matmul(b, e[:, 1, h, :], vtok[:, 1, h, :], start=True, stop=False)
                    last = pe.matmul(b, nw[:, h, :], s1[:, h, :], start=False, stop=True)
                last.then_inc(n_ready, 1)
                pe.wait_ge(a_copied, 2)
                for h in range(4):
                    b = kit.bank[4 + h // 2][:, (h % 2) * SEQ:(h % 2) * SEQ + SEQ]
                    pe.matmul(b[:, 0:P], vn0[:, h, :], attn[:, 0, h, :], start=True, stop=True)
                    pe.matmul(b[:, P:SEQ], s1[:, h, :], qe[:, 0, h, :], start=True, stop=False)
                    last = pe.matmul(b[:, P:SEQ], vn1[:, h, :], attn[:, 1, h, :], start=False, stop=True)
                last.then_inc(o_ready, 1)

            @block.scalar
            def _(act):
                act.wait_ge(u_ready, 1)
                act.copy(vn0, four(kit.bank[0][:, :])).then_inc(a_copied, 1)
                act.wait_ge(n_ready, 1)
                act.copy(vn1, four(kit.bank[3][:, :])).then_inc(a_copied, 1)
                act.wait_ge(o_ready, 1)
                act.copy(out[:, h0:h0 + 2, :], kit.bank[4][:, :].rearrange("p (a b) -> p a b", a=2)).then_inc(a_copied, 1)

            @block.vector
            def _(dve):
                dve.wait_ge(w_ready, 1)
                dve.tensor_scalar(nw, four(kit.bank[1][:, :]), -1.0, None, ALU.mult).then_inc(v_copied, 1)
                dve.wait_ge(s_ready, 1)
                dve.tensor_copy(s1, four(kit.bank[2][:, :])).then_inc(v_copied, 1)
                dve.wait_ge(o_ready, 1)
                dve.tensor_copy(out[:, h0 + 2:h0 + 4, :], kit.bank[5][:, :].rearrange("p (a b) -> p a b", a=2)).then_inc(v_copied, 1)


def gated_hidden(kit, x, T, widths, hidden):
    nc = kit.nc
    feed = kit.feed
    done, m = [], 0
    for w in widths:
        m += w // P
        done += [m, m]
    with ExitStack() as mem:
        sg = mem.enter_context(kit.sb("silu_gate", [P, 2, T]))
        with stage(nc, "pair_ready", "silu_ready", "hidden_ready") as (block, pair_ready, silu_ready, hidden_ready):
            @block.sync
            def _(sp):
                feed.run(sp, pair_ready, done)

            @block.tensor
            def _(pe):
                n = 0
                for w in widths:
                    gate = feed.arrive(pe, (DC, w))
                    up = feed.arrive(pe, (DC, w))
                    for m in range(w // P):
                        for which, unit, freed in ((0, gate, silu_ready), (2, up, hidden_ready)):
                            if n >= 2:
                                pe.wait_ge(freed, n - 1)
                            for k in range(DC):
                                last = pe.matmul(kit.bank[which + n % 2][:, 0:T], unit[:, k, m * P:(m + 1) * P], x(k),
                                                 start=k == 0, stop=k == DC - 1)
                        last.then_inc(pair_ready, 1)
                        n += 1

            @block.scalar
            def _(act):
                for n in range(done[-1]):
                    act.wait_ge(pair_ready, n + 1)
                    if n >= 2:
                        act.wait_ge(hidden_ready, n - 1)
                    act.activation(sg[:, n % 2, :], kit.bank[n % 2][:, 0:T], ACT.Silu).then_inc(silu_ready, 1)

            @block.vector
            def _(dve):
                for n in range(done[-1]):
                    dve.wait_ge(silu_ready, n + 1)
                    dve.tensor_tensor(hidden[:, n, :], sg[:, n % 2, :], kit.bank[2 + n % 2][:, 0:T], ALU.mult).then_inc(hidden_ready, 1)


def rows_of(name, ap):
    if len(ap.shape) == 1:
        return ap.rearrange("(r q) -> r q", q=P)
    if len(ap.shape) == 2:
        return ap.rearrange("o (r q) -> (o r) q", q=P)
    return ap.rearrange("o t (r q) -> (o t r) q", q=P)


def start(kit, inp, const, x_out, ctx_out, small):
    nc = kit.nc
    with ExitStack() as mem:
        rows = mem.enter_context(kit.sb("vector_rows", [P, VTILES, P]))
        x, ctx = [mem.enter_context(kit.sb(n, [P, 2, D])) for n in ("x_tokens", "ctx_tokens")]
        with stage(nc, "rows_zeroed", "rows_loaded", "others_loaded") as (block, rows_zeroed, rows_loaded, others_loaded):
            @block.sync
            def _(sp):
                sp.dma_start(kit.const[:, :], const[:, 0:KEPT_WORDS]).then_inc(others_loaded, 16)
                for dst, src in ((x, inp["x"]), (ctx, inp["ctx_2"])):
                    sp.dma_start(dst[:, :, :], src[0].rearrange("(t p) d -> p t d", p=P)).then_inc(others_loaded, 16)
                sp.dma_start(kit.const_first[:, :], const[:, KEPT_WORDS:CONST_WORDS]).then_inc(others_loaded, 16)
                sp.wait_ge(others_loaded, 64)
                sp.wait_ge(rows_loaded, 16 * len(PIECES))
                kit.feed.first(sp)

            @block.vector
            def _(dve):
                dve.memset(rows[:, :, :], 0.0).then_inc(rows_zeroed, 1)

            @block.scalar
            def _(act):
                act.wait_ge(rows_zeroed, 1)
                for name, first, count, tile, row in PIECES:
                    src = rows_of(name, inp[name])
                    act.dma_start(rows[row:row + count, tile, :], src[first:first + count]).then_inc(rows_loaded, 16)
                for name, (tensor, src) in small.items():
                    act.dma_start(tensor[:, :, :] if len(tensor.shape) == 3 else tensor[:, :], src).then_inc(kit.small_loaded, 16)
                act.wait_ge(rows_loaded, 16 * len(PIECES))
        groups = []
        for a in range(0, VTILES, 4):
            b = min(a + 4, VTILES)
            groups.append(([rows[:, t, :] for t in range(a, b)], kit.vec[:, a * P:b * P]))
        for raw, out in ((x, x_out), (ctx, ctx_out)):
            groups += [([raw[:, t, (c + j) * P:(c + j + 1) * P] for j in range(2) for t in range(2)], out(c))
                       for c in range(0, DC, 2)]
        turn(kit, groups)


def load_turned(kit, src, out, tiles, name):
    nc = kit.nc
    with ExitStack() as mem:
        raw = mem.enter_context(kit.sb(name + "_tokens", [P, 2, tiles * P]))
        with stage(nc, "loaded") as (block, loaded):
            @block.scalar
            def _(act):
                act.dma_start(raw[:, :, :], src.rearrange("(t p) d -> p t d", p=P)).then_inc(loaded, 16)
                act.wait_ge(loaded, 16)
        turn(kit, [([raw[:, t, (c + j) * P:(c + j + 1) * P] for j in range(2) for t in range(2)], out(c))
                   for c in range(0, tiles, 2)])


def vector_only(kit, program):
    with stage(kit.nc, "v") as (block, vsem):
        @block.vector
        def _(dve):
            program(dve, Signal(vsem))


def first_block(kit, inp, h, mem0):
    nc = kit.nc
    pair = lambda ap: ap.rearrange("p a b -> p (a b)")
    with ExitStack() as mem:
        new = lambda name, tiles: mem.enter_context(kit.sb(name, [P, tiles, SEQ]))
        u, ya = new("u", DC), new("y_a", DC)
        rmsnorm(kit, h, [(slice(0, SEQ), lambda c: u[:, c, :], lambda c: kit.col("ln_pre_mix", c), None, None)])
        ux = lambda k: u[:, k, :]
        with ExitStack() as m2:
            qkv = m2.enter_context(kit.sb("qkv_a", [P, 24, SEQ]))
            project_loop(kit, ux, SEQ, 2, lambda e, i, n, ps: e.tensor_scalar(
                qkv[:, bass.ds(i * 12 + n, 1), :].rearrange("p a b -> p (a b)"), ps, 1.0, None, ALU.mult))
            rope(kit, qkv)
            vt = m2.enter_context(kit.sb("v_tokens", [P, 2, D]))
            turn(kit, [([qkv[:, 16 + c + j, t * P:(t + 1) * P] for j in range(4)], vt[:, t, c * P:(c + 4) * P])
                       for t in range(2) for c in (0, 4)])
            moba(kit, qkv, vt, ya)
        ob, zg = new("o_b", DC), new("z_gates", 24)
        with ExitStack() as m2:
            qkv = m2.enter_context(kit.sb("qkv_b", [P, 24, SEQ]))
            project_loop(kit, ux, SEQ, 2, lambda e, i, n, ps: e.tensor_scalar(
                qkv[:, bass.ds(i * 12 + n, 1), :].rearrange("p a b -> p (a b)"), ps, 1.0, None, ALU.mult))

            def spans(tap, out, x):
                back = 3 - tap
                return out[:, back:SEQ], x[:, 0:SEQ - back]

            conv_beside_project(kit, qkv, 24, (3, 2, 1, 0), lambda tap, c: kit.col("conv_w", tap * 24 + c), spans,
                                lambda act, c, s: act.activation(qkv[:, c, :], s, ACT.Silu),
                                project_programs(kit, ux, DC, SEQ, [WIDE] * 12, lambda e, s, n, ps: e.activation(
                                    zg[:, n, :], ps, ACT.Silu if n < 8 else ACT.Sigmoid)))
            head_norm(kit, lambda n: pair(qkv[:, 2 * n:2 * n + 2, :]), 8, 1.0, lambda n: HD ** -0.5 if n < 4 else 1.0)
            scal = gdn_scalars(kit, u, kit.small["w_ba"], kit.small["dt_bias"], kit.small["a_log"], m2)
            for h0 in (0, 4):
                gdn_group(kit, h0, qkv, scal, ob)
        head_norm(kit, lambda n: pair(ob[:, 2 * n:2 * n + 2, :]), 4, 1.0 / HD, lambda n: kit.col("gdn_norm"))
        with ExitStack() as m2:
            vector_only(kit, lambda dve, v: v.by(dve.tensor_tensor(pair(ob[:, :, :]), pair(ob[:, :, :]), pair(zg[:, 0:8, :]), ALU.mult)))
            merged = m2.enter_context(kit.sb("merged", [P, DC, SEQ]))
            tmp = m2.enter_context(kit.sb("gated_b", [P, 2, SEQ]))
            project(kit, lambda k: ya[:, k, :], DC, SEQ, [WIDE] * 4,
                    lambda e, s, n, ps: e.tensor_tensor(merged[:, n, :], ps, zg[:, 8 + n, :], ALU.mult))

            def add_b(e, s, n, ps):
                s.link(e, e.tensor_tensor(tmp[:, n % 2, :], ps, zg[:, 16 + n, :], ALU.mult))
                return e.tensor_tensor(merged[:, n, :], merged[:, n, :], tmp[:, n % 2, :], ALU.add)

            project(kit, lambda k: ob[:, k, :], DC, SEQ, [WIDE] * 4, add_b)
            project(kit, lambda k: merged[:, k, :], DC, SEQ, [WIDE] * 4, lambda e, s, n, ps: e.tensor_copy(ya[:, n, :], ps))
        rmsnorm(kit, ya, [(slice(0, SEQ), lambda c: h[:, c, :], lambda c: kit.col("ln_post_mix", c), None, lambda c: h[:, c, :])])
        rmsnorm(kit, h, [(slice(0, SEQ), lambda c: u[:, c, :], lambda c: kit.col("ln_pre_ffn", c), None, None)])
        with ExitStack() as m2:
            hidden = m2.enter_context(kit.sb("ffn_hidden", [P, FF_TILES, SEQ]))
            gated_hidden(kit, ux, SEQ, [WIDE] * 11, hidden)
            project_down(kit, lambda k: hidden[:, k, :], SEQ, [2] * 11, lambda e, s, m, ps: e.tensor_copy(ya[:, m, :], ps))
        rmsnorm(kit, ya, [(slice(0, SEQ), lambda c: h[:, c, :], lambda c: kit.col("ln_post_ffn", c), None, lambda c: h[:, c, :])])
        with ExitStack() as m2:
            pt = m2.enter_context(kit.sb("p_turned", [P, 2, SEQ]))
            load_turned(kit, inp["p"][0, 0], lambda c: pair(pt[:, c:c + 2, :]), 2, "p")
            project(kit, lambda k: pt[:, k, :], 2, SEQ, [1024], lambda e, s, n, ps: e.tensor_copy(ob[:, n, :], ps))
            rmsnorm(kit, ob, [(slice(0, SEQ), lambda c: ya[:, c, :], lambda c: kit.col("ln_ple", c), None, None)])
            project(kit, lambda k: h[:, k, :], DC, SEQ, [WIDE] * 4,
                    lambda e, s, n, ps: e.activation(u[:, n, :], ps, ACT.Sigmoid), "scalar")

            def add_ple(dve, v):
                v.link(dve, dve.tensor_tensor(pair(u[:, :, :]), pair(u[:, :, :]), pair(ya[:, :, :]), ALU.mult))
                v.by(dve.tensor_tensor(h, h, u[:, :, :], ALU.add))

            vector_only(kit, add_ple)


def plan_first(feed, inp):
    kpn = lambda w: w.rearrange("(k p) n -> p k n", p=P)
    w3 = kpn(inp["w_in"][0])
    wide = lambda w, base=0: (lambda i, j: w[:, :, base + WIDE * j:base + WIDE * (j + 1)])
    rounds = lambda w, base=0: (lambda i, j: w[:, :, bass.ds(i * (WIDE * SLOTS) + (base + WIDE * j), WIDE)])
    feed.plan(2, SLOTS, rounds(w3))
    feed.plan(2, SLOTS, rounds(w3, 3072))
    feed.plan(1, 12, lambda i, j: w3[:, :, 6144 + WIDE * j + (16 if j >= 4 else 0):][:, :, 0:WIDE])
    for name in ("w_proj_a", "w_proj_b", "w_out"):
        feed.plan(1, 4, wide(kpn(inp[name][0])))
    gate, up, down = kpn(inp["w_ffn_gate"][0]), kpn(inp["w_ffn_up"][0]), kpn(inp["w_ffn_down"][0])
    feed.plan(1, 22, lambda i, j: (gate, up)[j % 2][:, :, WIDE * (j // 2):WIDE * (j // 2) + WIDE])
    feed.plan(1, 11, lambda i, j: down[:, 2 * j:2 * j + 2, :])
    feed.plan(1, 1, lambda i, j: kpn(inp["w_ple"][0]))
    feed.plan(1, 4, wide(kpn(inp["w_ple_gate"][0])))


T2 = 2 * SEQ
CTX, LAT = slice(0, SEQ), slice(SEQ, T2)
AB_Z, AB_XBC, AB_DT, AB_V, AB_G, AB_END = 0, 1024, 3072, 3104, 4128, 5152
TAPS = 31
PAD = TAPS // 2
CTX_AT = PAD
LAT_AT = PAD + SEQ + PAD
LINE = LAT_AT + (GRID_W + PAD) * ROWS


def plan_modulation(feed, inp, layer):
    w = inp["mod_w_2"][layer].rearrange("(k p) n -> p k n", p=P)
    feed.plan(1, 6 * D // WIDE, lambda i, j: w[:, :, WIDE * j:WIDE * (j + 1)])


def expert_unit(inp, layer, e, j):
    w = inp[("moe_w_gate_2", "moe_w_up_2")[j % 2] if j < 4 else "moe_w_down_2"][layer]
    w = w[e] if isinstance(e, int) else w[bass.ds(e, 1)].rearrange("e k n -> (e k) n")
    w = w.rearrange("(k p) n -> p k n", p=P)
    return w[:, :, WIDE * (j // 2):WIDE * (j // 2 + 1)] if j < 4 else w[:, 2 * (j - 4):2 * (j - 4) + 2, :]


def plan_moe(feed, inp, layer):
    feed.plan(1, SLOTS, lambda i, j: expert_unit(inp, layer, 0, j))


def plan_second(feed, inp):
    kpn = lambda w: w.rearrange("(k p) n -> p k n", p=P)
    wide = lambda w, base=0: (lambda i, j: w[:, :, base + WIDE * j:base + WIDE * (j + 1)])
    ab = kpn(inp["ab_w_in_2"][0])
    plan_modulation(feed, inp, 0)
    feed.plan(1, 4, wide(ab, AB_G))
    feed.plan(1, 4, wide(ab, AB_V))
    plan_modulation(feed, inp, 1)
    feed.plan(1, 8, wide(ab, AB_XBC))
    feed.plan(1, 4, wide(ab, AB_Z))
    out = kpn(inp["ab_w_out_2"][0])
    feed.plan(1, 8, lambda i, j: out[:, 2 * j:2 * j + 2, :])
    plan_moe(feed, inp, 0)
    hg = kpn(inp["hg_w_in_2"][0])
    feed.plan(1, 4, wide(hg, 2048))
    feed.plan(1, 8, wide(hg, 0))
    feed.plan(1, 8, wide(hg, 3072))
    feed.plan(1, 4, wide(kpn(inp["hg_w_out_2"][0])))
    plan_moe(feed, inp, 1)


def modulation_programs(kit, cond, staged, rows):
    feed = kit.feed
    chunks = 6 * D // 512
    bank = lambda b: kit.bank[4 + b % 3][0:2, :]

    def sync(sp, used):
        feed.run(sp, used, [j + 1 for j in range(2 * chunks)])

    def tensor(pe, used, copied):
        for b in range(chunks):
            if b >= 3:
                pe.wait_ge(copied, b - 2)
            for half in range(2):
                unit = feed.arrive(pe, (DC, WIDE))
                for k in range(DC):
                    last = pe.matmul(bank(b)[:, half * WIDE:(half + 1) * WIDE], cond[:, k, :], unit[:, k, :], start=k == 0, stop=k == DC - 1)
                last.then_inc(used, 1)

    def drain(act, used, copied, moved):
        for b in range(chunks):
            act.wait_ge(used, 2 * b + 2)
            if b >= 2:
                act.wait_ge(moved[b % 2], 16 * (b // 2))
            act.copy(staged[0:2, b % 2, :], bank(b)).then_inc(copied, 1)
            act.wait_ge(copied, b + 1)
            act.dma_start(rows[8 * b:8 * b + 8, :], staged[0:2, b % 2, :].rearrange("w (c q) -> w c q", q=P)).then_inc(moved[b % 2], 16)
        for m in moved:
            act.wait_ge(m, 16 * (chunks // 2))

    return sync, tensor, drain


def modulation_columns(kit, rows, turned, mod, layer):
    turn(kit, [([rows[0:96, :]], turned[:, 0:96])])
    base = kit.cols("mod_b_2", layer * 48, 48).rearrange("p (b c) -> p b c", c=4)

    def program(dve, v):
        for who in range(2):
            v.by(dve.tensor_tensor(mod[:, :, who].rearrange("p (b c) -> p b c", c=4),
                                   turned[:, 0:96].rearrange("p (b w c) -> p b w c", w=2, c=4)[:, :, who, :], base, ALU.add))

    vector_only(kit, program)


def shifts(kit, mod, scale_at, gain_name, layer, out):
    g = kit.cols(gain_name, layer * 8, 8)

    def program(dve, v):
        for who in range(2):
            v.by(dve.scalar_tensor_tensor(out[:, :, who], mod[:, 8 * scale_at:8 * scale_at + 8, who], 1.0, g, ALU.add, ALU.mult))

    vector_only(kit, program)


def conformer(kit, hn, out, other_programs):
    nc = kit.nc
    hx = lambda k: hn[:, k, :]
    grid = lambda ap: ap.rearrange("p (r w) -> p r w", w=GRID_W)
    W = LINE - 2 * PAD
    with ExitStack() as mem:
        line = mem.enter_context(kit.sb("conv_line", [P, DC, LINE]))
        ctx_of = lambda t, c, shift=0: t[:, c, CTX_AT - shift:CTX_AT - shift + SEQ]
        rows_of_grid = lambda t, c, shift=0: t[:, c, LAT_AT - shift:LAT_AT - shift + (GRID_W + PAD) * ROWS].rearrange(
            "p (r w) -> p r w", w=GRID_W + PAD)[:, :, 0:GRID_W]
        with ExitStack() as m2:
            sg = m2.enter_context(kit.sb("gate_sigmoid", [P, DC, T2]))
            project(kit, hx, DC, T2, [WIDE] * 4, lambda e, s, n, ps: e.activation(sg[:, n, :], ps, ACT.Sigmoid), "scalar")
            vector_only(kit, lambda dve, v: v.by(dve.memset(line[:, :, :], 0.0)))

            def gate(e, s, n, ps):
                s.by(e.tensor_tensor(ctx_of(line, n), ps[:, CTX], sg[:, n, CTX], ALU.mult))
                return e.tensor_tensor(rows_of_grid(line, n), grid(ps[:, LAT]), grid(sg[:, n, LAT]), ALU.mult)

            project(kit, hx, DC, T2, [WIDE] * 4, gate)
        acc = mem.enter_context(kit.sb("conv31_sum", [P, DC, (GRID_W + PAD) * ROWS + LAT_AT]))
        sums = acc[:, :, 0:W]

        modulate, project_xbc = other_programs
        with stage(nc, "units_used", "copied", "moved_even", "moved_odd", "tiles_ready", "evacuated", "step", "v") as (
                block, used, copied, moved_even, moved_odd, ready, evacuated, step, vsem):
            @block.vector
            def _(dve):
                v = Signal(vsem)
                for tap in range(TAPS):
                    for c in range(DC):
                        x, w = line[:, c, tap:tap + W], kit.col("cf_dw_w_2", tap * 8 + c)
                        if tap == 0:
                            v.by(dve.tensor_scalar(sums[:, c, :], x, w, kit.col("cf_dw_b_2", c), ALU.mult, ALU.add))
                        else:
                            v.by(dve.scalar_tensor_tensor(sums[:, c, :], x, w, sums[:, c, :], ALU.mult, ALU.add))
                    v.wait(dve)

            @block.sync
            def _(sp):
                modulate[0](sp, used)
                project_xbc[0](sp, ready)

            @block.tensor
            def _(pe):
                modulate[1](pe, used, copied)
                project_xbc[1](pe, ready, evacuated)

            @block.scalar
            def _(act):
                modulate[2](act, used, copied, (moved_even, moved_odd))
                project_xbc[2](act, ready, evacuated, step)

        mean, rstd, sq = line[:, 4, 0:T2], line[:, 5, 0:T2], line[:, 0:4, 0:T2]
        with stage(nc, "summed", "mean_ready", "centred", "squared", "sq_summed", "var_ready", "root_ready", "scaled",
                   "finished", "v") as (block, summed, mean_ready, centred, squared, sq_summed, var_ready, root_ready,
                                        scaled, finished, vsem):
            @block.tensor
            def _(pe):
                for c in range(DC):
                    pe.matmul(kit.bank[0][:, CTX], kit.c("ones"), ctx_of(acc, c, PAD), start=c == 0, stop=c == DC - 1)
                for c in range(DC):
                    last = pe.matmul(kit.bank[0][:, LAT], kit.c("ones"), rows_of_grid(acc, c, PAD), start=c == 0, stop=c == DC - 1)
                last.then_inc(summed, 1)
                for c in range(DC):
                    pe.wait_ge(squared, c + 1)
                    pe.matmul(kit.bank[1][:, :], kit.c("ones"), sq[:, c % 4, :], start=c == 0, stop=c == DC - 1).then_inc(sq_summed, 1)

            @block.vector
            def _(dve):
                v = Signal(vsem)
                dve.wait_ge(summed, 1)
                v.link(dve, dve.tensor_scalar(mean[:, :], kit.bank[0][:, :], 1.0 / D, None, ALU.mult))
                for c in range(DC):
                    v.by(dve.tensor_tensor(out[:, c, CTX], ctx_of(acc, c, PAD), mean[:, CTX], ALU.subtract))
                    dve.tensor_tensor(grid(out[:, c, LAT]), rows_of_grid(acc, c, PAD), grid(mean[:, LAT]), ALU.subtract).then_inc(centred, 1)
                dve.wait_ge(sq_summed, DC)
                dve.tensor_scalar(rstd[:, :], kit.bank[1][:, :], 1.0 / D, EPS, ALU.mult, ALU.add).then_inc(var_ready, 1)
                dve.wait_ge(root_ready, 1)
                v.link(dve, dve.reciprocal(rstd[:, :], rstd[:, :]))
                dve.wait_ge(centred, DC)
                for c in range(DC):
                    dve.scalar_tensor_tensor(out[:, c, :], out[:, c, :], kit.col("cf_ln_g_2", c), rstd[:, :], ALU.mult,
                                             ALU.mult).then_inc(scaled, 1)

            @block.scalar
            def _(act):
                for c in range(DC):
                    act.wait_ge(centred, c + 1)
                    if c >= 4:
                        act.wait_ge(sq_summed, c - 3)
                    act.activation(sq[:, c % 4, :], out[:, c, :], ACT.Square).then_inc(squared, 1)
                act.wait_ge(var_ready, 1)
                act.activation(rstd[:, :], rstd[:, :], ACT.Sqrt).then_inc(root_ready, 1)
                for c in range(DC):
                    act.wait_ge(scaled, c + 1)
                    act.activation(out[:, c, :], out[:, c, :], ACT.Silu, bias=kit.col("cf_ln_b_2", c)).then_inc(finished, 1)


def ssd(kit, inp, hn, xbc, out):
    nc = kit.nc
    NT = T2 // P
    with ExitStack() as mem:
        y = hn.rearrange("p c t -> p (c t)").rearrange("p (t d) -> p t d", t=NT)
        z = mem.enter_context(kit.sb("z_silu", [P, DC, T2]))
        two = lambda ap: ap.rearrange("p (s t) -> p s t", s=2)

        def spans(tap, o, x):
            if tap < 2:
                return two(o)[:, :, 2 - tap:SEQ], two(x)[:, :, 0:SEQ - (2 - tap)]
            return two(o)[:, :, 0:SEQ - (tap - 2)], two(x)[:, :, tap - 2:SEQ]

        conv_beside_project(kit, xbc, 16, (2, 0, 1, 3, 4), lambda tap, c: kit.col("ssd_conv_w_2", tap * 16 + c), spans,
                            lambda act, c, s: act.activation(xbc[:, c, :], s, ACT.Silu, bias=kit.col("ssd_conv_b_2", c)),
                            project_programs(kit, lambda k: hn[:, k, :], DC, T2, [WIDE] * 4,
                                             lambda e, s, n, ps: e.activation(z[:, n, :], ps, ACT.Silu)))
        with ExitStack() as m2:
            new = lambda name, *shape: m2.enter_context(kit.sb(name, [P, *shape]))
            xt, bt = out.rearrange("p c t -> p (c t)").rearrange("p (t d) -> p t d", t=NT), new("b_tokens", NT, 512)
            dt, la, acum, eac, etot, toend = [new(n, NT, 32) for n in ("dt", "log_decay", "a_sum", "a_exp", "a_total_exp", "to_end")]
            turn(kit, [([xbc[:, c + j, t * P:(t + 1) * P] for j in range(4)], xt[:, t, c * P:(c + 4) * P])
                       for t in range(NT) for c in (0, 4)]
                 + [([xbc[:, 8 + j, t * P:(t + 1) * P] for j in range(4)], bt[:, t, :]) for t in range(NT)])
            flat = lambda ap: ap.rearrange("p a b -> p (a b)")
            with ExitStack() as m3:
                w_dt, bias, alog = [kit.small[n] for n in ("w_dt", "ssd_dt_bias", "ssd_a_log")]
                pdt = kit.bank[0][:, 0:NT * 32].rearrange("p (t n) -> p t n", t=NT)
                with stage(nc, "dt_ready", "a_ready", "v") as (block, dt_ready, a_ready, vsem):
                    @block.tensor
                    def _(pe):
                        kit.wait_small(pe)
                        for t in range(NT):
                            for k in range(DC):
                                last = pe.matmul(pdt[:, t, :], hn[:, k, t * P:(t + 1) * P], w_dt[:, k, :], start=k == 0, stop=k == DC - 1)
                        last.then_inc(dt_ready, 1)

                    @block.scalar
                    def _(act):
                        kit.wait_small(act)
                        act.activation(alog[:, :], alog[:, :], ACT.Exp).then_inc(a_ready, 1)

                    @block.vector
                    def _(dve):
                        dve.wait_ge(dt_ready, 1)
                        dve.tensor_tensor(dt[:, :, :], pdt, bias[:, :].unsqueeze(1).broadcast_to([P, NT, 32]), ALU.add).then_inc(vsem, 1)
                softplus(kit, flat(dt[:, :, :]), flat(dt[:, :, :]), NT * 32)
                with stage(nc, "la_ready", "sums_ready", "copied", "finished", "v") as (block, la_ready, sums_ready, copied, finished, vsem):
                    ps = kit.bank[0][:, 0:NT * 32].rearrange("p (t n) -> p t n", t=NT)
                    pt = kit.bank[1][:, 0:NT * 32].rearrange("p (t n) -> p t n", t=NT)

                    @block.vector
                    def _(dve):
                        v = Signal(vsem)
                        dve.scalar_tensor_tensor(la[:, :, :], dt[:, :, :], -1.0, alog[:, :].unsqueeze(1).broadcast_to([P, NT, 32]),
                                                 ALU.mult, ALU.mult).then_inc(la_ready, 1)
                        dve.wait_ge(sums_ready, 1)
                        v.link(dve, dve.tensor_copy(acum[:, :, :], ps))
                        v.by(dve.tensor_copy(etot[:, :, :], pt))
                        dve.tensor_tensor(toend[:, :, :], pt, acum[:, :, :], ALU.subtract).then_inc(copied, 1)
                        dve.wait_ge(finished, 3)
                        v.by(dve.tensor_tensor(toend[:, :, :], toend[:, :, :], dt[:, :, :], ALU.mult))

                    @block.tensor
                    def _(pe):
                        pe.wait_ge(la_ready, 1)
                        pe.matmul(flat(pt), kit.c("ones"), flat(la[:, :, :]), start=True, stop=True)
                        for t in range(NT):
                            pe.matmul(ps[:, t, 0:16], kit.c("tri_f"), la[:, t, 0:16], start=True, stop=True)
                            last = pe.matmul(ps[:, t, 16:32], kit.c("tri_r"), la[:, t, 16:32], start=True, stop=True)
                        last.then_inc(sums_ready, 1)

                    @block.scalar
                    def _(act):
                        act.wait_ge(copied, 1)
                        act.activation(eac[:, :, :], acum[:, :, :], ACT.Exp).then_inc(finished, 1)
                        act.activation(toend[:, :, :], toend[:, :, :], ACT.Exp).then_inc(finished, 1)
                        act.activation(etot[:, :, :], etot[:, :, :], ACT.Exp).then_inc(finished, 1)
            by_head = lambda ap: ap.rearrange("p (h q) -> p h q", q=S_HD)
            spread = lambda ap, n: ap.unsqueeze(2).broadcast_to([P, n, S_HD])
            with ExitStack() as m3:
                xdt = m3.enter_context(kit.sb("x_dt", [P, 2, D]))
                m = m3.enter_context(kit.sb("decay_cb", [P, 2, 2, 4, P]))
                cb = m3.enter_context(kit.sb("c_dot_b", [P, 2, P]))
                with stage(nc, "cb_ready", "cb_copied", "rows_ready", "args_ready", "exp_ready", "m_ready", "xdt_ready",
                           "y_ready", "y_copied") as (block, cb_ready, cb_copied, rows_ready, args_ready, exp_ready,
                                                      m_ready, xdt_ready, y_ready, y_copied):
                    steps = [(t, g) for t in range(NT) for g in range(S_GROUPS)]

                    @block.tensor
                    def _(pe):
                        def prepare(q):
                            t, g = steps[q]
                            if q >= 2:
                                pe.wait_ge(cb_copied, q - 1)
                            pe.matmul(kit.bank[q % 2][:, 0:P], xbc[:, 8 + g, t * P:(t + 1) * P], xbc[:, 12 + g, t * P:(t + 1) * P],
                                      start=True, stop=True).then_inc(cb_ready, 1)
                            for d in range(2):
                                if q >= 2:
                                    pe.wait_ge(args_ready, 2 * (q - 2) + d + 1)
                                for j in range(4):
                                    at = d * 16 + 4 * g + j
                                    last = pe.matmul(kit.bank[2 + 2 * (q % 2) + d][:, j * P:(j + 1) * P],
                                                     la[:, t, at:at + 1].broadcast_to([P, P]), kit.c(("tri_f", "tri_r")[d]),
                                                     start=True, stop=True)
                                last.then_inc(rows_ready, 1)

                        prepare(0)
                        prepare(1)
                        for q, (t, g) in enumerate(steps):
                            if q + 2 < len(steps):
                                prepare(q + 2)
                            pe.wait_ge(xdt_ready, t + 1)
                            pe.wait_ge(m_ready, 2 * q + 2)
                            if q >= 2:
                                pe.wait_ge(y_copied, q - 1)
                            for j in range(4):
                                for d in range(2):
                                    at = (4 * g + j) * S_HD
                                    last = pe.matmul(kit.bank[6 + q % 2][:, j * S_HD:(j + 1) * S_HD], m[:, q % 2, d, j, :],
                                                     xdt[:, d, at:at + S_HD], start=d == 0, stop=d == 1)
                            last.then_inc(y_ready, 1)

                    @block.vector
                    def _(dve):
                        def args(q):
                            t, g = steps[q]
                            for d in range(2):
                                dve.wait_ge(rows_ready, 2 * q + d + 1)
                                if q >= 2:
                                    dve.wait_ge(y_ready, q - 1)
                                for j in range(4):
                                    at = d * 16 + 4 * g + j
                                    ins = dve.scalar_tensor_tensor(m[:, q % 2, d, j, :], kit.bank[2 + 2 * (q % 2) + d][:, j * P:(j + 1) * P],
                                                                   acum[:, t, at:at + 1], kit.c(("neg_f", "neg_r")[d]), ALU.subtract, ALU.add)
                                ins.then_inc(args_ready, 1)

                        args(0)
                        for q, (t, g) in enumerate(steps):
                            if g == 0:
                                if t:
                                    dve.wait_ge(y_ready, q)
                                for d in range(2):
                                    ins = dve.tensor_tensor(by_head(xdt[:, d, :]), by_head(xt[:, t, :]), spread(dt[:, t, 16 * d:16 * d + 16], 16), ALU.mult)
                                ins.then_inc(xdt_ready, 1)
                            dve.wait_ge(cb_copied, q + 1)
                            for d in range(2):
                                dve.wait_ge(exp_ready, 2 * q + d + 1)
                                dve.tensor_tensor(m[:, q % 2, d], m[:, q % 2, d], cb[:, q % 2, :].unsqueeze(1).broadcast_to([P, 4, P]),
                                                  ALU.mult).then_inc(m_ready, 1)
                            if q + 1 < len(steps):
                                args(q + 1)

                    @block.scalar
                    def _(act):
                        def exps(q):
                            act.wait_ge(cb_ready, q + 1)
                            if q >= 2:
                                act.wait_ge(m_ready, 2 * (q - 2) + 2)
                            act.copy(cb[:, q % 2, :], kit.bank[q % 2][:, 0:P]).then_inc(cb_copied, 1)
                            for d in range(2):
                                act.wait_ge(args_ready, 2 * q + d + 1)
                                act.activation(m[:, q % 2, d], m[:, q % 2, d], ACT.Exp).then_inc(exp_ready, 1)

                        exps(0)
                        for q, (t, g) in enumerate(steps):
                            if q + 1 < len(steps):
                                exps(q + 1)
                            act.wait_ge(y_ready, q + 1)
                            act.copy(y[:, t, g * 256:(g + 1) * 256], kit.bank[6 + q % 2][:, 0:256]).then_inc(y_copied, 1)
            with ExitStack() as m3:
                state = m3.enter_context(kit.sb("ssd_state", [P, 2, D]))
                xe = m3.enter_context(kit.sb("x_to_end", [P, 2, D]))
                tmp = m3.enter_context(kit.sb("y_from_state", [P, 512]))
                order = [(d, k, ((0, 1, 2, 3), (1, 0, 3, 2))[d][k]) for k in range(NT) for d in range(2)]
                with stage(nc, "xe_ready", "s_ready", "off_ready", "state_ready", "v", "y_added") as (
                        block, xe_ready, s_ready, off_ready, state_ready, vsem, y_added):
                    @block.tensor
                    def _(pe):
                        def chunk_state(n):
                            d, k, t = order[n]
                            if k < NT - 1:
                                pe.wait_ge(xe_ready, n + 1)
                                if n >= 2:
                                    pe.wait_ge(state_ready, n - 1)
                                for g in range(S_GROUPS):
                                    last = pe.matmul(kit.bank[2 * (n % 2) + g // 2][:, (g % 2) * 256:(g % 2) * 256 + 256],
                                                     bt[:, t, g * P:(g + 1) * P], xe[:, d, g * 256:(g + 1) * 256], start=True, stop=True)
                                last.then_inc(s_ready, 1)

                        chunk_state(0)
                        for n, (d, k, t) in enumerate(order):
                            if n + 1 < len(order):
                                chunk_state(n + 1)
                            if k:
                                pe.wait_ge(state_ready, n - 1)
                                if n >= 4:
                                    pe.wait_ge(y_added, n - 3)
                                for g in range(S_GROUPS):
                                    last = pe.matmul(kit.bank[4 + 2 * (n % 2) + g // 2][:, (g % 2) * 256:(g % 2) * 256 + 256],
                                                     xbc[:, 12 + g, t * P:(t + 1) * P], state[:, d, g * 256:(g + 1) * 256], start=True, stop=True)
                                last.then_inc(off_ready, 1)

                    @block.vector
                    def _(dve):
                        v = Signal(vsem)

                        def x_to_end(n):
                            d, k, t = order[n]
                            if k < NT - 1:
                                if n >= 2:
                                    dve.wait_ge(s_ready, n - 1)
                                dve.tensor_tensor(by_head(xe[:, d, :]), by_head(xt[:, t, :]), spread(toend[:, t, 16 * d:16 * d + 16], 16),
                                                  ALU.mult).then_inc(xe_ready, 1)

                        x_to_end(0)
                        for n, (d, k, t) in enumerate(order):
                            if n + 1 < len(order):
                                x_to_end(n + 1)
                            if k:
                                dve.wait_ge(off_ready, n - 1)
                                for b in range(2):
                                    v.link(dve, dve.tensor_tensor(by_head(tmp[:, :]), by_head(kit.bank[4 + 2 * (n % 2) + b][:, :]),
                                                                  spread(eac[:, t, 16 * d + 8 * b:16 * d + 8 * b + 8], 8), ALU.mult))
                                    half = y[:, t, b * 512:(b + 1) * 512]
                                    added = dve.tensor_tensor(half, half, tmp[:, :], ALU.add)
                                    if b == 0:
                                        v.link(dve, added)
                                added.then_inc(y_added, 1)
                                dve.wait_ge(y_added, n - 1)
                            if k < NT - 1:
                                dve.wait_ge(s_ready, n + 1)
                                if k:
                                    v.link(dve, dve.tensor_tensor(by_head(state[:, d, :]), by_head(state[:, d, :]),
                                                                  spread(etot[:, t, 16 * d:16 * d + 16], 16), ALU.mult))
                                for b in range(2):
                                    s, ps = state[:, d, b * 512:(b + 1) * 512], kit.bank[2 * (n % 2) + b][:, :]
                                    last = dve.tensor_tensor(s, s, ps, ALU.add) if k else dve.tensor_copy(s, ps)
                                    if b == 0:
                                        v.by(last)
                                last.then_inc(state_ready, 1)
                                v.wait(dve)
                                dve.wait_ge(state_ready, n + 1)
        turn(kit, [([y[:, t, c * P:(c + 1) * P] for t in range(NT)], out[:, c, :]) for c in range(DC)])

        def skip_and_gate(dve, v):
            for c in range(DC):
                v.by(dve.scalar_tensor_tensor(out[:, c, :], xbc[:, c, :], kit.col("ssd_d_2", c), out[:, c, :], ALU.mult, ALU.add))
            v.wait(dve)
            for c in range(DC):
                v.by(dve.tensor_tensor(out[:, c, :], out[:, c, :], z[:, c, :], ALU.mult))

        vector_only(kit, skip_and_gate)
    rmsnorm(kit, out, [(slice(0, T2), lambda c: out[:, c, :], lambda c: kit.col("ssd_norm_g_2", c), None, None)])


def route(kit, inp, hn, T, combine, lists, table):
    nc = kit.nc
    NT = T // P
    with ExitStack() as mem:
        new = lambda name, *shape: mem.enter_context(kit.sb(name, [P, *shape]))
        rw, rb = kit.small["router_w"], kit.small["router_b"]
        score, sel, pick = new("scores", NT, 16), new("selection", NT * 4, 4), new("pick", NT * 4, 4)
        gt, ge = new("greater", NT * 4, 4, 4), new("greater_equal", NT * 4, 4, 4)
        gs, gp, den = new("group_score", NT * 4), new("group_pick", NT * 4), new("weight_sum", NT)
        ct = new("combine_t", T)
        chosen, weights, places = [new(n, NT, 16) for n in ("chosen", "weights", "places")]
        need, upto, start, first = [new(n, 16) for n in ("items_needed", "items_up_to", "items_before", "total_tokens")]
        member, part = new("item_of_expert", ITEMS, 16), new("item_products", NT, ITEMS, 16)
        skipped, which = new("skipped_tokens", ITEMS), new("item_expert", ITEMS)
        flat = lambda ap: ap.rearrange("p a b -> p (a b)")
        ps = kit.bank[0][:, 0:NT * 16].rearrange("p (t n) -> p t n", t=NT)

        def ranks(dve, v, s, G, rank):
            other, own = s.unsqueeze(2).broadcast_to([P, G, 4, 4]), s.unsqueeze(3).broadcast_to([P, G, 4, 4])
            table = lambda name: kit.c(name).rearrange("p (i j) -> p i j", i=4).unsqueeze(1).broadcast_to([P, G, 4, 4])
            v.by(dve.tensor_tensor(gt[:, 0:G], other, own, ALU.is_gt))
            v.by(dve.tensor_tensor(ge[:, 0:G], other, own, ALU.is_ge))
            v.wait(dve)
            v.by(dve.tensor_tensor(gt[:, 0:G], gt[:, 0:G], table("notbefore"), ALU.mult))
            v.by(dve.tensor_tensor(ge[:, 0:G], ge[:, 0:G], table("before"), ALU.mult))
            v.wait(dve)
            v.link(dve, dve.tensor_tensor(gt[:, 0:G], gt[:, 0:G], ge[:, 0:G], ALU.add))
            v.link(dve, dve.tensor_reduce(rank, gt[:, 0:G], AX.X, ALU.add))

        with stage(nc, "scored", "sigmoid_ready", "v") as (block, scored, sigmoid_ready, vsem):
            @block.tensor
            def _(pe):
                kit.wait_small(pe)
                for t in range(NT):
                    for k in range(DC):
                        last = pe.matmul(ps[:, t, :], hn[:, k, t * P:(t + 1) * P], rw[:, k, :], start=k == 0, stop=k == DC - 1)
                last.then_inc(scored, 1)

            @block.scalar
            def _(act):
                act.wait_ge(scored, 1)
                act.activation(score[:, :, :], ps, ACT.Sigmoid).then_inc(sigmoid_ready, 1)

            @block.vector
            def _(dve):
                v = Signal(vsem)
                dve.wait_ge(sigmoid_ready, 1)
                kit.wait_small(dve)
                v.link(dve, dve.tensor_tensor(sel[:, :, :].rearrange("p (t g) i -> p t (g i)", t=NT), score[:, :, :],
                                              rb[:, :].unsqueeze(1).broadcast_to([P, NT, 16]), ALU.add))
                ranks(dve, v, sel[:, :, :], NT * 4, pick[:, :, :])
                v.link(dve, dve.tensor_scalar(flat(pick[:, :, :]), flat(pick[:, :, :]), 1.5, None, ALU.is_lt))
                v.link(dve, dve.tensor_tensor(sel[:, :, :], sel[:, :, :], pick[:, :, :], ALU.mult))
                v.link(dve, dve.tensor_reduce(gs[:, :], sel[:, :, :], AX.X, ALU.add))
                ranks(dve, v, gs[:, :].rearrange("p (t g) -> p t g", t=NT), NT, gp[:, :].rearrange("p (t g) -> p t g", t=NT))
                v.link(dve, dve.tensor_scalar(gp[:, :], gp[:, :], 0.5, None, ALU.is_lt))
                v.link(dve, dve.tensor_tensor(pick[:, :, :], pick[:, :, :], gp[:, :].unsqueeze(2).broadcast_to([P, NT * 4, 4]), ALU.mult))
                v.link(dve, dve.tensor_tensor(score[:, :, :], score[:, :, :], pick[:, :, :].rearrange("p (t g) i -> p t (g i)", t=NT), ALU.mult))
                v.link(dve, dve.tensor_reduce(den[:, :], score[:, :, :], AX.X, ALU.add))
                v.link(dve, dve.reciprocal(den[:, :], den[:, :]))
                v.by(dve.tensor_copy(chosen[:, :, :], pick[:, :, :].rearrange("p (t g) i -> p t (g i)", t=NT)))
                v.by(dve.tensor_tensor(weights[:, :, :], score[:, :, :], den[:, :].unsqueeze(2).broadcast_to([P, NT, 16]), ALU.mult))
        with stage(nc, "counted", "v") as (block, counted, vsem):
            before = kit.bank[0][:, 0:NT * 16].rearrange("p (t n) -> p t n", t=NT)
            total = kit.bank[1][:, 0:16]

            @block.tensor
            def _(pe):
                for t in range(NT):
                    for s in range(t + 1):
                        pe.matmul(before[:, t, :], kit.c("ones") if s < t else kit.c("tri_f"), chosen[:, s, :], start=s == 0, stop=s == t)
                for t in range(NT):
                    last = pe.matmul(total, kit.c("ones"), chosen[:, t, :], start=t == 0, stop=t == NT - 1)
                last.then_inc(counted, 1)

            @block.vector
            def _(dve):
                v = Signal(vsem)
                dve.wait_ge(counted, 1)
                v.by(dve.tensor_tensor(places[:, :, :], before, chosen[:, :, :], ALU.mult))
                v.link(dve, dve.tensor_copy(first[:, :], total))
                v.by(dve.tensor_scalar(flat(places[:, :, :]), flat(places[:, :, :]), 1.0, None, ALU.subtract))
                v.link(dve, dve.memset(need[:, :], 1.0))
                for full in range(1, -(-T // CAP)):
                    v.link(dve, dve.scalar_tensor_tensor(need[:, :], first[:, :], CAP * full + 0.5, need[:, :], ALU.is_gt, ALU.add))
                v.link(dve, dve.tensor_tensor_scan(upto[:, :], kit.c("ones")[:, 0:16], need[:, :], 0.0, ALU.mult, ALU.add))
                v.link(dve, dve.tensor_tensor(start[:, :], upto[:, :], need[:, :], ALU.subtract))
                number = kit.c("count")[:, 0:ITEMS]
                numbers = number.unsqueeze(2).broadcast_to([P, ITEMS, 16])
                along = lambda ap: ap.unsqueeze(1).broadcast_to([P, ITEMS, 16])
                v.by(dve.tensor_tensor(member[:, :, :], numbers, along(start[:, :]), ALU.is_ge))
                v.link(dve, dve.tensor_tensor(part[:, 0], numbers, along(upto[:, :]), ALU.is_lt))
                v.link(dve, dve.tensor_tensor(member[:, :, :], member[:, :, :], part[:, 0], ALU.mult))
                v.by(dve.tensor_tensor(part[:, 0], member[:, :, :], along(kit.c("count")[:, 0:16]), ALU.mult))
                v.link(dve, dve.tensor_tensor(part[:, 1], member[:, :, :], along(start[:, :]), ALU.mult))
                v.by(dve.tensor_reduce(which[:, :], part[:, 0], AX.X, ALU.add))
                v.link(dve, dve.tensor_reduce(skipped[:, :], part[:, 1], AX.X, ALU.add))
                v.by(dve.tensor_copy(table[:, 0:ITEMS], which[:, :]))
                v.by(dve.tensor_scalar(table[:, ITEMS:ITEMS + 1], upto[:, 15:16], 1.0, None, ALU.subtract))
                v.link(dve, dve.tensor_tensor(skipped[:, :], number, skipped[:, :], ALU.subtract))
                v.link(dve, dve.tensor_scalar(skipped[:, :], skipped[:, :], float(CAP), None, ALU.mult))
                for w, of_expert in enumerate((weights, places)):
                    for t in range(NT):
                        v.by(dve.tensor_tensor(part[:, t], member[:, :, :], along(of_expert[:, t, :]), ALU.mult))
                    v.wait(dve)
                    v.link(dve, dve.tensor_reduce(lists[:, :, w, :], part[:, :], AX.X, ALU.add))
                v.by(dve.tensor_tensor(lists[:, :, 1, :], lists[:, :, 1, :], skipped[:, :].unsqueeze(1).broadcast_to([P, NT, ITEMS]),
                                       ALU.subtract))
        turn(kit, [([lists[:, t].rearrange("p w i -> p (w i)") for t in range(NT)], ct[0:2 * ITEMS, :])])
        with stage(nc, "stored") as (block, stored):
            @block.scalar
            def _(act):
                act.dma_start(combine.rearrange("w i t -> (w i) t"), ct[0:2 * ITEMS, :]).then_inc(stored, 16)
                act.wait_ge(stored, 16)


def experts(kit, hn, T, combine, lists, table, add, inp, layer):
    nc = kit.nc
    feed = kit.feed
    NT, M = T // P, 4
    flat = lambda ap: ap.rearrange("p a b -> p (a b)")
    PER = 15
    UNIT = [1 + n for n in (1, 4, 7, 10, 14, 15)]
    SCATTERED = [1 + 3 * (m // 2) + 2 + m % 2 for m in range(DC)]
    GATHERED = 1 + 13
    most = EXPERTS + (CHOICES * T - 1) // CAP
    assert most < ITEMS
    with ExitStack() as mem:
        new = lambda name, *shape: mem.enter_context(kit.sb(name, [P, *shape]))
        tokens = new("moe_tokens", NT, D)
        rows = new("weight_and_place_rows", 2, T)
        pick, spread = new("gather_one_hot", NT, CAP), new("scatter_weights", T)
        xg, sg, hidden, y = new("gathered", DC, CAP), new("silu_gate", M, CAP), new("expert_hidden", M, CAP), new("expert_out", D)
        turn(kit, [([hn[:, c + j, t * P:(t + 1) * P] for j in range(4)], tokens[:, t, c * P:(c + 4) * P])
                   for t in range(NT) for c in (0, 4)])
        last_item = lambda engine: engine.value_load(table[0:1, ITEMS:ITEMS + 1], min_val=EXPERTS - 1, max_val=most - 1)
        with stage(nc, "products", "pick_ready", "gathered", "silu_ready", "hidden_ready", "y_copied", "spread_ready",
                   "added", "rows_loaded", *[f"unit_loaded{j}" for j in range(SLOTS)]) as (
                block, products, pick_ready, gathered, silu_ready, hidden_ready, y_copied, spread_ready, added, rows_loaded,
                *unit_loaded):
            slot = [(feed.taken + j) % SLOTS for j in range(SLOTS)]

            @block.sync
            def _(sp):
                def rows_of(i):
                    row = combine[:, i:i + 1, :] if isinstance(i, int) else combine[:, bass.ds(i, 1), :]
                    sp.dma_start(rows[:, :, :], row.rearrange("w i t -> i w t").broadcast_to([P, 2, T])).then_inc(rows_loaded, 16)

                last_of_all = last_item(sp)
                rows_of(0)
                with sp.Fori(0, last_of_all) as i:
                    e = sp.value_load(table[0:1, bass.ds(i + 1, 1)], min_val=0, max_val=EXPERTS - 1)
                    for j in range(SLOTS):
                        src = expert_unit(inp, layer, e, j)
                        sp.wait_ge(products, i * PER + UNIT[j])
                        dst = feed.buf[:, slot[j], :].rearrange("p (k n) -> p k n", k=src.shape[1])
                        sp.dma_start(dst, src).then_inc(unit_loaded[j], 16)
                        if j == 3:
                            sp.wait_ge(spread_ready, i + 2)
                            rows_of(i + 1)
                feed.run_ahead(sp, SLOTS, lambda j: sp.wait_ge(products, last_of_all * PER + UNIT[j]))

            def gather(pe):
                for c in range(DC):
                    for t in range(NT):
                        last = pe.matmul(kit.bank[2 + c // 4][:, (c % 4) * CAP:(c % 4 + 1) * CAP], tokens[:, t, c * P:(c + 1) * P],
                                         pick[:, t, :], start=t == 0, stop=t == NT - 1)
                last.then_inc(products, 1)

            def scatter(pe, i, m):
                pe.wait_ge(added, i * DC + m + 1)
                pe.matmul(kit.bank[6 + m % 2][:, 0:T], y[0:CAP, m * P:(m + 1) * P], spread[0:CAP, :], start=True, stop=True).then_inc(products, 1)

            def scatter_ready(pe, i):
                pe.wait_ge(spread_ready, i + 1)
                pe.wait_ge(y_copied, i * 2 + 2)

            @block.tensor
            def _(pe):
                n = last_item(pe) + 1
                pe.wait_ge(pick_ready, 1)
                gather(pe)
                for j in range(SLOTS):
                    feed.arrive(pe, (SLOT, 1))
                    pe.sem_inc(unit_loaded[j], 16)
                with pe.Fori(0, n) as i:
                    pe.wait_ge(gathered, i * 2 + 2)
                    for j in range(4):
                        unit = feed.buf[:, slot[j], :].rearrange("p (k n) -> p k n", k=DC)
                        pe.wait_ge(unit_loaded[j], i * 16 + 16)
                        for half in range(2):
                            at = (2 * (j // 2) + half) * CAP
                            for k in range(DC):
                                last = pe.matmul(kit.bank[j % 2][:, at:at + CAP], unit[:, k, half * P:(half + 1) * P], xg[:, k, :],
                                                 start=k == 0, stop=k == DC - 1)
                        last.then_inc(products, 1)
                        if j == 0:
                            scatter_ready(pe, i)
                        for m in (2 * j, 2 * j + 1):
                            scatter(pe, i, m)
                    pe.wait_ge(pick_ready, i + 2)
                    gather(pe)
                    pe.wait_ge(hidden_ready, i + 1)
                    for j in range(2):
                        unit = feed.buf[:, slot[4 + j], :].rearrange("p (k n) -> p k n", k=2)
                        pe.wait_ge(unit_loaded[4 + j], i * 16 + 16)
                        for half in range(2):
                            for k in range(2):
                                last = pe.matmul(kit.bank[4 + half][0:CAP, :], hidden[:, 2 * j + k, :], unit[:, k, half * 512:(half + 1) * 512],
                                                 start=j == 0 and k == 0, stop=j == 1 and k == 1)
                        last.then_inc(products, 1)
                scatter_ready(pe, n)
                for m in range(DC):
                    scatter(pe, n, m)

            @block.scalar
            def _(act):
                def copy_gathered(signal):
                    act.wait_ge(products, signal)
                    for b in range(2):
                        act.copy(xg[:, 4 * b:4 * b + 4, :], kit.bank[2 + b][:, 0:4 * CAP].rearrange("p (a b) -> p a b", a=4)).then_inc(gathered, 1)

                n = last_item(act) + 1
                copy_gathered(1)
                with act.Fori(0, n) as i:
                    act.wait_ge(products, i * PER + UNIT[2])
                    act.activation(flat(sg[:, :, :]), kit.bank[0][:, 0:M * CAP], ACT.Silu).then_inc(silu_ready, 1)
                    copy_gathered(i * PER + GATHERED)
                    act.wait_ge(products, i * PER + UNIT[5])
                    for b in range(2):
                        act.copy(y[0:CAP, b * 512:(b + 1) * 512], kit.bank[4 + b][0:CAP, :]).then_inc(y_copied, 1)

            @block.vector
            def _(dve):
                def choose(i):
                    for t in range(NT):
                        at = lists[:, t, 1, i:i + 1] if isinstance(i, int) else lists[:, t, 1, bass.ds(i, 1)]
                        ins = dve.tensor_scalar(pick[:, t, :], kit.c("count")[:, 0:CAP], at, None, ALU.is_equal)
                    ins.then_inc(pick_ready, 1)

                def add_scattered(i, signals):
                    for m in range(DC):
                        dve.wait_ge(products, i * PER + signals[m])
                        add(dve, m, kit.bank[6 + m % 2][:, 0:T]).then_inc(added, 1)

                n = last_item(dve) + 1
                dve.memset(spread[:, :], 0.0).then_inc(spread_ready, 1)
                dve.memset(y[:, 0:512], 0.0).then_inc(y_copied, 1)
                dve.memset(y[:, 512:1024], 0.0).then_inc(y_copied, 1)
                dve.sem_inc(added, 2)
                choose(0)
                with dve.Fori(0, n) as i:
                    dve.wait_ge(gathered, i * 2 + 2)
                    choose(i + 1)
                    add_scattered(i, SCATTERED)
                    dve.wait_ge(silu_ready, i + 1)
                    dve.tensor_tensor(flat(hidden[:, :, :]), flat(sg[:, :, :]), kit.bank[1][:, 0:M * CAP], ALU.mult).then_inc(hidden_ready, 1)
                    dve.wait_ge(rows_loaded, i * 16 + 16)
                    dve.scalar_tensor_tensor(spread[:, :], rows[:, 1, :], kit.c("slot"), rows[:, 0, :], ALU.is_equal,
                                             ALU.mult).then_inc(spread_ready, 1)
                add_scattered(n, [1 + m + 1 for m in range(DC)])


def hgrn2(kit, x2, hn, out):
    nc = kit.nc
    C = 64
    NCH = SEQ // C
    with ExitStack() as mem:
        new = lambda name, *shape: mem.enter_context(kit.sb(name, [P, *shape]))
        vt = new("v_tokens", 4, D)
        with ExitStack() as m2:
            vf = m2.enter_context(kit.sb("v_features", [P, DC, T2]))
            project(kit, lambda k: hn[:, k, :], DC, T2, [WIDE] * 4, lambda e, s, n, ps: e.tensor_copy(vf[:, n, :], ps))
            turn(kit, [([vf[:, c + j, t * P:(t + 1) * P] for j in range(4)], vt[:, t, c * P:(c + 4) * P])
                       for t in range(4) for c in (0, 4)])
        qg = new("q_and_gate", 16, SEQ)
        project(kit, lambda k: hn[:, k, LAT], DC, SEQ, [WIDE] * 8, lambda e, s, n, ps: e.activation(qg[:, n, :], ps, ACT.Silu), "scalar")
        inner = mem.enter_context(ExitStack())
        new = lambda name, *shape: inner.enter_context(kit.sb(name, [P, *shape]))
        f = new("forget", 16, T2)
        project(kit, lambda k: hn[:, k, :], DC, T2, [WIDE] * 8, lambda e, s, n, ps: e.activation(f[:, n, :], ps, ACT.Sigmoid), "scalar")
        lb, omlb, hi, e0, e1 = [new(n, DC) for n in ("lower", "one_less_lower", "lb_max", "lb_e0", "lb_e1")]
        with stage(nc, "shifted", "exp_ready", "v") as (block, shifted, exp_ready, vsem):
            @block.vector
            def _(dve):
                v = Signal(vsem)
                r0, r1 = kit.cols("hg_lb_2", 0, 8), kit.cols("hg_lb_2", 8, 8)
                v.link(dve, dve.tensor_tensor(hi[:, :], r0, r1, ALU.max))
                dve.tensor_tensor(e0[:, :], r0, hi[:, :], ALU.subtract).then_inc(shifted, 1)
                dve.tensor_tensor(e1[:, :], r1, hi[:, :], ALU.subtract).then_inc(shifted, 1)
                dve.wait_ge(exp_ready, 2)
                v.link(dve, dve.tensor_tensor(hi[:, :], e0[:, :], e1[:, :], ALU.add))
                v.link(dve, dve.reciprocal(hi[:, :], hi[:, :]))
                v.link(dve, dve.tensor_tensor(e0[:, :], e0[:, :], hi[:, :], ALU.mult))
                v.link(dve, dve.tensor_tensor(e1[:, :], e1[:, :], hi[:, :], ALU.mult))
                v.link(dve, dve.tensor_tensor(lb[:, :], e0[:, :], e1[:, :], ALU.add))
                v.link(dve, dve.tensor_tensor(lb[:, :], lb[:, :], e0[:, :], ALU.subtract))
                v.by(dve.tensor_scalar(omlb[:, :], lb[:, :], -1.0, 1.0, ALU.mult, ALU.add))

            @block.scalar
            def _(act):
                act.wait_ge(shifted, 2)
                act.activation(e0[:, :], e0[:, :], ACT.Exp).then_inc(exp_ready, 1)
                act.activation(e1[:, :], e1[:, :], ACT.Exp).then_inc(exp_ready, 1)
        lf = new("log_forget", 2, T2)
        ex = new("exps", 2, 3, SEQ)
        rel = ex[:, :, 0, :]
        end = new("end_less_sum", 2, T2)
        ge = new("chunk_decay", 2, 2, NCH)
        spare = hn.rearrange("p c t -> p (c t)")
        qk = spare[:, 0:12 * SEQ].rearrange("p (n w t) -> p n w t", n=4, w=3)
        kend = new("k_end", 2, T2)
        kt = new("k_end_tokens", 2, 6, P)
        st = new("states", 4, NCH, P)
        att = spare[:, 12 * SEQ:16 * SEQ].rearrange("p (n t l) -> p n t l", n=4, t=2)
        chunks = lambda ap: ap.rearrange("p (c t) -> p c t", c=NCH)
        with stage(nc, "f_ready", "log_ready", "rel_ready", "exp_ready", "prod_ready", "kt_ready", "kt_copied",
                   "ctx_state", "adds_ready", "att_ready", "states_ready", "o_ready", "o_copied", "zeroed", "v") as (
                block, f_ready, log_ready, rel_ready, exp_ready, prod_ready, kt_ready, kt_copied, ctx_state, adds_ready,
                att_ready, states_ready, o_ready, o_copied, zeroed, vsem):
            order = ((0, 1, 2, 3), (3, 2, 1, 0))
            mid, last_of = (C // 2 - 1, C // 2), (C - 1, 0)
            keep = lambda d, lo: kit.c(("keep_f", "keep_r")[d])

            @block.vector
            def _(dve):
                v = Signal(vsem)
                v.by(dve.memset(att[:, :, :, :], 0.0))
                dve.memset(kt[:, :, :, :], 0.0).then_inc(zeroed, 1)

                def gates(n):
                    h, d = n // 2, n % 2
                    ff = f[:, 8 * d + h, :]
                    v.link(dve, dve.tensor_scalar(ff, ff, omlb[:, h:h + 1], lb[:, h:h + 1], ALU.mult, ALU.add))
                    if n >= 2:
                        dve.wait_ge(exp_ready, 5 * (n - 1))
                        dve.wait_ge(prod_ready, n - 1)
                    dve.nop().then_inc(f_ready, 1)

                def sums(n):
                    h, d = n // 2, n % 2
                    ff, s = f[:, 8 * d + h, :], lf[:, n % 2, :]
                    dve.wait_ge(log_ready, n + 1)
                    carry = kit.c(("carry_f", "carry_r")[d])
                    v.by(dve.tensor_scalar(ff, ff, -1.0, 1.0, ALU.mult, ALU.add))
                    if d == 0:
                        v.by(dve.tensor_tensor_scan(s, carry, s, 0.0, ALU.mult, ALU.add))
                    else:
                        v.by(dve.tensor_tensor_scan(s[:, ::-1], carry[:, ::-1], s[:, ::-1], 0.0, ALU.mult, ALU.add))
                    v.wait(dve)
                    g = chunks(s[:, LAT])
                    at = lambda j: g[:, :, j:j + 1].broadcast_to([P, NCH, C])
                    v.by(dve.tensor_tensor(chunks(rel[:, n % 2, :]), g, at(mid[d]), ALU.subtract))
                    v.by(dve.tensor_tensor(chunks(end[:, n % 2, LAT]), at(last_of[d]), g, ALU.subtract))
                    v.by(dve.tensor_copy(ge[:, n % 2, 0, :], g[:, :, last_of[d]]))
                    j = (SEQ - 1, 0)[d]
                    v.by(dve.tensor_scalar(end[:, n % 2, CTX], s[:, CTX], -1.0, s[:, j:j + 1], ALU.mult, ALU.add))
                    v.wait(dve)
                    dve.nop().then_inc(rel_ready, 1)

                def prods(n):
                    h, d = n // 2, n % 2
                    k = f[:, 8 * d + h, :]
                    dve.wait_ge(exp_ready, 5 * n + 4)
                    if n >= 2:
                        dve.wait_ge(kt_ready, n - 1)
                    if n >= 4:
                        dve.wait_ge(o_ready, h - 1)
                    v.by(dve.tensor_tensor(kend[:, n % 2, :], k, end[:, n % 2, :], ALU.mult))
                    v.by(dve.tensor_tensor(qk[:, n % 4, 0, :], qg[:, h, :], ex[:, n % 2, 0, :], ALU.mult))
                    v.by(dve.tensor_tensor(qk[:, n % 4, 1, :], k[:, LAT], ex[:, n % 2, 1, :], ALU.mult))
                    v.by(dve.tensor_tensor(qk[:, n % 4, 2, :], qg[:, h, :], ex[:, n % 2, 2, :], ALU.mult))
                    v.wait(dve)
                    dve.nop().then_inc(prod_ready, 1)

                def masks_states(n):
                    h, d = n // 2, n % 2
                    dve.wait_ge(att_ready, n + 1)
                    if n >= 4:
                        dve.wait_ge(o_ready, h - 1)
                    mask = kit.c(("keep_f", "keep_r")[d]).bitcast(I32)
                    for lo in (0, C):
                        v.by(dve.copy_predicated(att[lo:lo + C, n % 4, :, lo:lo + C], mask[lo:lo + C].unsqueeze(1).broadcast_to([C, 2, C]),
                                                 kit.bank[2 + d][lo:lo + C, 0:2 * C].rearrange("p (a b) -> p a b", a=2)))
                    dve.wait_ge(adds_ready, n + 1)
                    dve.wait_ge(exp_ready, 5 * (n + 1))
                    b = kit.bank[4 + d]
                    v.link(dve, dve.tensor_copy(st[:, n % 4, order[d][0], :], b[:, 0:P]))
                    for i in range(NCH - 1):
                        a, z = order[d][i], order[d][i + 1]
                        v.link(dve, dve.scalar_tensor_tensor(st[:, n % 4, z, :], st[:, n % 4, a, :], ge[:, n % 2, 1, a:a + 1],
                                                             b[:, (i + 1) * P:(i + 2) * P], ALU.mult, ALU.add))
                    dve.nop().then_inc(states_ready, 1)

                U = 2 * HEADS
                gates(0)
                sums(0)
                gates(1)
                prods(0)
                sums(1)
                for n in range(U):
                    if n + 2 < U:
                        gates(n + 2)
                    if n + 1 < U:
                        prods(n + 1)
                    if n + 2 < U:
                        sums(n + 2)
                    masks_states(n)

            @block.scalar
            def _(act):
                def logs(n):
                    h, d = n // 2, n % 2
                    act.wait_ge(f_ready, n + 1)
                    act.activation(lf[:, n % 2, :], f[:, 8 * d + h, :], ACT.Ln).then_inc(log_ready, 1)

                def exps(n):
                    act.wait_ge(rel_ready, n + 1)
                    if n >= 2:
                        act.wait_ge(prod_ready, n - 1)
                    act.activation(ex[:, n % 2, 1, :], rel[:, n % 2, :], ACT.Exp, scale=-1.0).then_inc(exp_ready, 1)
                    act.wait_ge(exp_ready, 5 * n + 1)
                    act.activation(rel[:, n % 2, :], rel[:, n % 2, :], ACT.Exp).then_inc(exp_ready, 1)
                    act.activation(ex[:, n % 2, 2, :], lf[:, n % 2, LAT], ACT.Exp).then_inc(exp_ready, 1)
                    act.activation(end[:, n % 2, :], end[:, n % 2, :], ACT.Exp).then_inc(exp_ready, 1)
                    if n >= 2:
                        act.wait_ge(states_ready, n - 1)
                    act.activation(ge[:, n % 2, 1, :], ge[:, n % 2, 0, :], ACT.Exp).then_inc(exp_ready, 1)

                def copy_output(h):
                    act.wait_ge(o_ready, h + 1)
                    act.copy(out[:, h, :], kit.bank[6 + h % 2][:, 0:SEQ]).then_inc(o_copied, 1)

                U = 2 * HEADS
                act.wait_ge(zeroed, 1)
                logs(0)
                exps(0)
                logs(1)
                exps(1)
                for n in range(U):
                    if n + 2 < U:
                        logs(n + 2)
                    act.wait_ge(kt_ready, n + 1)
                    if n >= 2:
                        act.wait_ge(adds_ready, n - 1)
                    src = kit.bank[n % 2][:, :].rearrange("p (a b) -> p a b", a=4)
                    act.copy(kt[:, n % 2, 0:2, :], src[:, 0:2, :]).then_inc(kt_copied, 1)
                    for half in range(2):
                        lo = half * C
                        dst = kt[lo:lo + C, n % 2, 2:6, :].rearrange("p (t z) b -> p t z b", z=2)[:, :, half, :]
                        act.copy(dst, src[lo:lo + C, 2:4, :]).then_inc(kt_copied, 1)
                    if n + 2 < U:
                        exps(n + 2)
                    if n % 2 and n >= 3:
                        copy_output((n - 3) // 2)
                copy_output(HEADS - 1)

            @block.tensor
            def _(pe):
                def transposes_scores(n):
                    d = n % 2
                    pe.wait_ge(prod_ready, n + 1)
                    if n >= 2:
                        pe.wait_ge(kt_copied, 3 * (n - 1))
                    for t in range(4):
                        last = pe.transpose(kit.bank[n % 2][:, t * P:(t + 1) * P], kend[:, n % 2, t * P:(t + 1) * P], kit.c("ident"))
                    last.then_inc(kt_ready, 1)
                    if n >= 2:
                        pe.wait_ge(states_ready, n - 1)
                    H2 = C // 2
                    for c in range(NCH):
                        for half in range(2):
                            first, many = (0, C) if half == d else (half * H2, H2)
                            lo = (c % 2) * C + half * H2
                            last = pe.matmul(kit.bank[2 + d][lo:lo + H2, (c // 2) * C + first:(c // 2) * C + first + many],
                                             qk[:, n % 4, 1, c * C + half * H2:c * C + (half + 1) * H2],
                                             qk[:, n % 4, 0, c * C + first:c * C + first + many], start=True, stop=True)
                    last.then_inc(att_ready, 1)

                vh = lambda h, t: vt[:, t, h * P:(h + 1) * P]

                def chunk_states(n):
                    h, d = n // 2, n % 2
                    pe.wait_ge(kt_copied, 3 * (n + 1))
                    b = kit.bank[4 + d]
                    for t in range(2):
                        pe.matmul(b[:, 0:P], kt[:, n % 2, t, :], vh(h, t), start=t == 0, stop=t == 1)
                    for i in range(NCH - 1):
                        c = order[d][i]
                        last = pe.matmul(b[:, (i + 1) * P:(i + 2) * P], kt[:, n % 2, 2 + c, :], vh(h, 2 + c // 2), start=True, stop=True)
                    last.then_inc(adds_ready, 1)

                def outputs(h):
                    pe.wait_ge(states_ready, 2 * h + 2)
                    if h >= 2:
                        pe.wait_ge(o_copied, h - 1)
                    ring = (2 * h % 4, (2 * h + 1) % 4)
                    for t in range(NCH // 2):
                        o = kit.bank[6 + h % 2][:, t * P:(t + 1) * P]
                        pe.matmul(o, vh(h, 2 + t), att[:, ring[0], t, :], start=True, stop=False)
                        pe.matmul(o, vh(h, 2 + t), att[:, ring[1], t, :], start=False, stop=False)
                        for half in range(2):
                            c = 2 * t + half
                            for r in ring:
                                last = pe.matmul(o[:, half * C:(half + 1) * C], st[:, r, c, :], qk[:, r, 2, c * C:(c + 1) * C],
                                                 start=False, stop=half == 1 and r == ring[1])
                    last.then_inc(o_ready, 1)

                U = 2 * HEADS
                transposes_scores(0)
                for n in range(U):
                    chunk_states(n)
                    if n + 1 < U:
                        transposes_scores(n + 1)
                    if n >= 2 and n % 2 == 0:
                        outputs(n // 2 - 1)
                outputs(HEADS - 1)
        inner.close()
        pair = lambda ap: ap.rearrange("p a b -> p (a b)")
        head_norm(kit, lambda n: pair(out[:, 2 * n:2 * n + 2, :]), 4, 1.0 / HD, lambda n: kit.col("hg_norm_g_2"))
        vector_only(kit, lambda dve, v: v.by(dve.tensor_tensor(pair(out[:, :, :]), pair(out[:, :, :]), pair(qg[:, 8:16, :]), ALU.mult)))


def second_block(kit, inp, x2, out_dram, scratch):
    nc = kit.nc
    with ExitStack() as mem:
        new = lambda name, *shape: mem.enter_context(kit.sb(name, [P, *shape]))
        cond, mod = new("cond", DC, 2), new("mod", 48, 2)
        gain = new("mod_gain", DC, 2)
        with stage(nc, "silu") as (block, silu):
            @block.scalar
            def _(act):
                act.activation(cond[:, :, 0], kit.cols("c_ctx_2", 0, 8), ACT.Silu).then_inc(silu, 1)
                act.activation(cond[:, :, 1], kit.cols("c_2", 0, 8), ACT.Silu).then_inc(silu, 1)
        m = lambda v, c, who: mod[:, 8 * v + c, who:who + 1]
        hn = new("hn", DC, T2)
        rows0, rows1 = new("mod_rows_0", P), new("mod_rows_1", P)
        with ExitStack() as m2:
            staged = m2.enter_context(kit.sb("mod_staged", [P, 2, 512]))
            sync, tensor, drain = modulation_programs(kit, cond, staged, rows0)
            with stage(nc, "units_used", "copied", "moved_even", "moved_odd") as (block, used, copied, moved_even, moved_odd):
                @block.sync
                def _(sp):
                    sync(sp, used)

                @block.tensor
                def _(pe):
                    tensor(pe, used, copied)

                @block.scalar
                def _(act):
                    drain(act, used, copied, (moved_even, moved_odd))
            modulation_columns(kit, rows0, staged[:, 0, :], mod, 0)
        gn = lambda who: (lambda c: gain[:, c, who:who + 1])

        def norm_both(shift_at):
            rmsnorm(kit, x2, [(CTX, lambda c: hn[:, c, CTX], gn(0), lambda c: m(shift_at, c, 0), None),
                              (LAT, lambda c: hn[:, c, LAT], gn(1), lambda c: m(shift_at, c, 1), None)])

        shifts(kit, mod, 1, "norm_mix_g_2", 0, gain)
        norm_both(0)
        with ExitStack() as m2:
            cf = m2.enter_context(kit.sb("conformer_out", [P, DC, T2]))
            so = m2.enter_context(kit.sb("ssd_out", [P, DC, T2]))
            xbc = m2.enter_context(kit.sb("xbc", [P, 16, T2]))
            with ExitStack() as m3:
                staged = m3.enter_context(kit.sb("mod_staged", [P, 2, 512]))
                conformer(kit, hn, cf, (modulation_programs(kit, cond, staged, rows1),
                                        project_programs(kit, lambda k: hn[:, k, :], DC, T2, [WIDE] * 8,
                                                         lambda e, s, n, ps: e.copy(xbc[:, n, :], ps))))
            ssd(kit, inp, hn[:, :, :], xbc, so)

            def residual(e, s, c, ps):
                s.by(e.scalar_tensor_tensor(x2[:, c, CTX], ps[:, CTX], m(2, c, 0), x2[:, c, CTX], ALU.mult, ALU.add))
                return e.scalar_tensor_tensor(x2[:, c, LAT], ps[:, LAT], m(2, c, 1), x2[:, c, LAT], ALU.mult, ALU.add)

            project_down(kit, lambda k: so[:, k, :] if k < DC else cf[:, k - DC, :], T2, [2] * 8, residual)
        shifts(kit, mod, 4, "norm_ffn_g_2", 0, gain)
        norm_both(3)
        lists, table = new("item_lists", T2 // P, 2, ITEMS), mem.enter_context(nc.sbuf_tensor("item_table", [P, ITEMS + 1], I32))
        route(kit, inp, hn[:, :, :], T2, scratch[0], lists, table)

        def add_both(e, c, ps):
            e.scalar_tensor_tensor(x2[:, c, CTX], ps[:, CTX], m(5, c, 0), x2[:, c, CTX], ALU.mult, ALU.add)
            return e.scalar_tensor_tensor(x2[:, c, LAT], ps[:, LAT], m(5, c, 1), x2[:, c, LAT], ALU.mult, ALU.add)

        experts(kit, hn[:, :, :], T2, scratch[0], lists, table, add_both, inp, 0)
        modulation_columns(kit, rows1, rows0[:, :], mod, 1)
        shifts(kit, mod, 1, "norm_mix_g_2", 1, gain)
        turned_out = lambda ap: ap.rearrange("p (w r) -> p r w", r=ROWS)
        turned_in = lambda ap: ap.rearrange("p (r w) -> p r w", w=GRID_W)
        rmsnorm(kit, x2, [(CTX, lambda c: hn[:, c, CTX], gn(0), lambda c: m(0, c, 0), None),
                          (LAT, lambda c: turned_out(hn[:, c, LAT]), gn(1), lambda c: m(0, c, 1), None)])
        with ExitStack() as m2:
            o = m2.enter_context(kit.sb("hgrn2_out", [P, DC, SEQ]))
            hgrn2(kit, x2, hn[:, :, :], o)

            def residual(e, s, c, ps):
                x = turned_in(x2[:, c, LAT])
                return e.scalar_tensor_tensor(x, turned_out(ps), m(2, c, 1), x, ALU.mult, ALU.add)

            project(kit, lambda k: o[:, k, :], DC, SEQ, [WIDE] * 4, residual)
        shifts(kit, mod, 4, "norm_ffn_g_2", 1, gain)
        x = x2[:, :, LAT]
        rmsnorm(kit, x, [(slice(0, SEQ), lambda c: hn[:, c, 0:SEQ], gn(1), lambda c: m(3, c, 1), None)])
        route(kit, inp, hn[:, :, 0:SEQ], SEQ, scratch[1], lists[:, 0:SEQ // P], table)
        experts(kit, hn[:, :, 0:SEQ], SEQ, scratch[1], lists, table,
                lambda e, c, ps: e.scalar_tensor_tensor(x[:, c, :], ps, m(5, c, 1), x[:, c, :], ALU.mult, ALU.add), inp, 1)
        rmsnorm(kit, x, [(slice(0, SEQ), lambda c: hn[:, c, 0:SEQ], lambda c: kit.col("final_norm_g_2", c), None, None)])
        rows = new("out_tokens", 2, D)
        turn(kit, [([hn[:, c + j, t * P:(t + 1) * P] for j in range(4)], rows[:, t, c * P:(c + 4) * P])
                   for t in range(2) for c in (0, 4)])
        with stage(nc, "stored") as (block, stored):
            @block.sync
            def _(sp):
                sp.dma_start(out_dram[0].rearrange("(t p) d -> p t d", p=P), rows[:, :, :]).then_inc(stored, 16)
                sp.wait_ge(stored, 16)


def build(nc, inp, const, out):
    scratch = [nc.dram_tensor(f"combine{n}", (2, ITEMS, t), F32, kind="Internal").ap() for n, t in enumerate((T2, SEQ))]
    with ExitStack() as mem:
        kit = Kit(nc, mem.enter_context)
        plan_first(kit.feed, inp)
        plan_second(kit.feed, inp)
        kpn = lambda w: w.rearrange("(k p) n -> p k n", p=P)
        row = lambda ap: ap.rearrange("o d h -> o (d h)").broadcast_to([P, 32])
        small = {name: (mem.enter_context(kit.sb(name, [P, *shape])), src) for name, shape, src in (
            ("w_dt", (DC, 32), kpn(inp["ab_w_in_2"][0])[:, :, AB_DT:AB_DT + 32]),
            ("ssd_dt_bias", (32,), row(inp["ssd_dt_bias_2"])),
            ("ssd_a_log", (32,), row(inp["ssd_a_log_2"])),
            ("router_w", (DC, EXPERTS), kpn(inp["router_w_2"])),
            ("router_b", (EXPERTS,), inp["router_b_2"].rearrange("(o n) -> o n", o=1).broadcast_to([P, EXPERTS])),
            ("w_ba", (DC, 16), kpn(inp["w_in"][0])[:, :, 7168:7184]),
            ("dt_bias", (8,), inp["dt_bias"].broadcast_to([P, 8])),
            ("a_log", (8,), inp["a_log"].broadcast_to([P, 8])))}
        kit.small = {name: tensor for name, (tensor, _) in small.items()}
        x2 = mem.enter_context(kit.sb("x_both", [P, DC, 2 * SEQ]))
        h = x2[:, :, SEQ:2 * SEQ]
        with ExitStack() as early:
            kit.const_first = early.enter_context(kit.sb("first_block_constants", [P, CONST_WORDS - KEPT_WORDS]))
            start(kit, inp, const, lambda c: h[:, c:c + 2, :], lambda c: x2[:, c:c + 2, 0:SEQ], small)
            first_block(kit, inp, h, mem)
        second_block(kit, inp, x2, out, scratch)


INPUTS = ["x", "p", "ln_pre_mix", "w_in", "conv_w", "a_log", "dt_bias", "gdn_norm", "w_proj_a", "w_proj_b", "w_out",
          "ln_post_mix", "ln_pre_ffn", "w_ffn_gate", "w_ffn_up", "w_ffn_down", "ln_post_ffn", "w_ple", "ln_ple",
          "w_ple_gate", "c_2", "ctx_2", "c_ctx_2", "mod_w_2", "mod_b_2", "norm_mix_g_2", "norm_ffn_g_2", "router_w_2",
          "router_b_2", "moe_w_gate_2", "moe_w_up_2", "moe_w_down_2", "ab_w_in_2", "ssd_conv_w_2", "ssd_conv_b_2",
          "ssd_dt_bias_2", "ssd_a_log_2", "ssd_d_2", "ssd_norm_g_2", "cf_dw_w_2", "cf_dw_b_2", "cf_ln_g_2",
          "cf_ln_b_2", "ab_w_out_2", "hg_w_in_2", "hg_lb_2", "hg_norm_g_2", "hg_w_out_2", "final_norm_g_2"]


def kernel(**inputs):
    from concourse import bacc
    from concourse.bass_utils import run_bass_kernel_spmd

    nc = bacc.Bacc("TRN2", target_bir_lowering=False, num_devices=1)
    arrays, aps = {}, {}
    for name in INPUTS:
        a = np.ascontiguousarray(inputs[name])
        if name == "ssd_d_2":
            a = np.ascontiguousarray(np.repeat(a, S_HD, axis=1))
        arrays[f"in_{name}"] = a
        aps[name] = nc.dram_tensor(f"in_{name}", a.shape, mybir.dt.from_np(a.dtype), kind="ExternalInput").ap()
    table = np.concatenate(list(CONSTANTS.values()), axis=1)
    arrays["constants"] = table
    const = nc.dram_tensor("constants", table.shape, F32, kind="ExternalInput").ap()
    out = nc.dram_tensor("out", (1, SEQ, D), F32, kind="ExternalOutput").ap()
    build(nc, aps, const, out)
    r = run_bass_kernel_spmd(nc, [arrays], core_ids=[0])
    return r.results[0]["out"]
```
